# Optimizing a Trainium2 kernel written in Bass

```python
import math
import jax, jax.numpy as jnp
from jax import lax
import numpy as np

D_MODEL = 1024
BATCH = 1
SEQ = 256
DEPTH = 1

GLA_HEADS = 4
GLA_DK = 64
GLA_DV = 128
GLA_LOWRANK = 16
GLA_TAU = 16.0
GLA_CHUNK = 64
MOBA_HEADS = 8
MOBA_HD = 64
MOBA_BLOCK = 256
MOBA_TOPK = 3
Q_BLOCK = 128
REL_BUCKETS = 32
REL_MAX_DIST = 4096
D_FF = 2816
D_PLE = 256
EPS = 1e-6
NEG = -1e30

GLA_QK = GLA_HEADS * GLA_DK
GLA_V = GLA_HEADS * GLA_DV
MOBA_W = MOBA_HEADS * MOBA_HD
MIX_WIDTH = GLA_V + MOBA_W
IN_SIZES = (GLA_QK, GLA_QK, GLA_V, GLA_V, GLA_LOWRANK, MOBA_W, MOBA_W, MOBA_W)
IN_WIDTH = 2 * GLA_QK + 2 * GLA_V + GLA_LOWRANK + 3 * MOBA_W

kernel_name = "hymba_gla_moba_macaron_t5bias_ple"

def rmsnorm(x, g):
    xf = x.astype(jnp.float32)
    y = xf * lax.rsqrt(jnp.mean(xf * xf, axis=-1, keepdims=True) + EPS)
    return (y * g.astype(jnp.float32)).astype(x.dtype)

def swiglu(x, w_gu, w_down):
    gate, up = jnp.split(x @ w_gu, 2, axis=-1)
    return (jax.nn.silu(gate) * up) @ w_down

def rel_bucket(dist):
    n = jnp.maximum(dist, 0)
    max_exact = REL_BUCKETS // 2
    nf = jnp.maximum(n, 1).astype(jnp.float32)
    large = max_exact + (jnp.log(nf / max_exact) / math.log(REL_MAX_DIST / max_exact)
                         * (REL_BUCKETS - max_exact)).astype(jnp.int32)
    large = jnp.minimum(large, REL_BUCKETS - 1)
    return jnp.where(n < max_exact, n, large)

def gla_chunked(q, k, v, log_a):
    B, H, T, dk = q.shape
    dv = v.shape[-1]
    C = GLA_CHUNK
    n = T // C

    def to_chunks(t):
        return t.astype(jnp.float32).reshape(B, H, n, C, t.shape[-1]).transpose(2, 0, 1, 3, 4)

    qc, kc, vc, ac = to_chunks(q), to_chunks(k), to_chunks(v), to_chunks(log_a)
    causal = jnp.tril(jnp.ones((C, C), dtype=bool))[:, :, None]

    def step(S, inp):
        qi, ki, vi, ai = inp
        b = jnp.cumsum(ai, axis=-2)
        b_last = b[..., -1:, :]
        o_inter = jnp.einsum('bhcd,bhde->bhce', qi * jnp.exp(b), S)
        diff = b[..., :, None, :] - b[..., None, :, :]
        decay = jnp.exp(jnp.where(causal, diff, -jnp.inf))
        attn = jnp.einsum('bhid,bhjd,bhijd->bhij', qi, ki, decay)
        o_intra = jnp.einsum('bhij,bhje->bhie', attn, vi)
        S_new = (jnp.exp(b_last)[..., 0, :, None] * S
                 + jnp.einsum('bhcd,bhce->bhde', ki * jnp.exp(b_last - b), vi))
        return S_new, o_inter + o_intra

    S0 = jnp.zeros((B, H, dk, dv), jnp.float32)
    _, o = lax.scan(step, S0, (qc, kc, vc, ac))
    return o.transpose(1, 2, 0, 3, 4).reshape(B, H, T, dv).astype(v.dtype)

def moba_attention(q, k, v, rel_bias):
    B, H, T, hd = q.shape
    nb = -(-T // MOBA_BLOCK)
    pad = nb * MOBA_BLOCK - T
    kb = jnp.pad(k, ((0, 0), (0, 0), (0, pad), (0, 0))).reshape(B, H, nb, MOBA_BLOCK, hd)
    vb = jnp.pad(v, ((0, 0), (0, 0), (0, pad), (0, 0))).reshape(B, H, nb, MOBA_BLOCK, hd)
    k_mean = jnp.mean(kb.astype(jnp.float32), axis=3)
    topk = min(MOBA_TOPK, nb)
    scale = hd ** -0.5
    bias_tab = rel_bias.astype(jnp.float32).T
    bi = jnp.arange(B)[:, None, None, None]
    hi = jnp.arange(H)[None, :, None, None]
    blk_off = jnp.arange(MOBA_BLOCK)
    nq = T // Q_BLOCK
    qs = q.reshape(B, H, nq, Q_BLOCK, hd).transpose(2, 0, 1, 3, 4)

    def per_block(args):
        qi, iq = args
        qpos = iq * Q_BLOCK + jnp.arange(Q_BLOCK)
        own = (iq * Q_BLOCK) // MOBA_BLOCK
        gate = jnp.einsum('bhqd,bhnd->bhqn', qi.astype(jnp.float32), k_mean)
        gate = jnp.where(jnp.arange(nb) < own, gate, -jnp.inf)
        _, sel = lax.top_k(gate, topk)
        valid = sel < own
        k_sel = kb[bi, hi, sel]
        v_sel = vb[bi, hi, sel]
        s_past = jnp.einsum('bhqd,bhqnsd->bhqns', qi, k_sel,
                            preferred_element_type=jnp.float32) * scale
        kpos = sel[..., None] * MOBA_BLOCK + blk_off
        s_past = s_past + bias_tab[hi[..., None], rel_bucket(qpos[:, None, None] - kpos)]
        s_past = jnp.where(valid[..., None], s_past, NEG).reshape(B, H, Q_BLOCK, topk * MOBA_BLOCK)
        k_own = lax.dynamic_index_in_dim(kb, own, axis=2, keepdims=False)
        v_own = lax.dynamic_index_in_dim(vb, own, axis=2, keepdims=False)
        dist_own = qpos[:, None] - (own * MOBA_BLOCK + blk_off)[None, :]
        s_own = (jnp.einsum('bhqd,bhsd->bhqs', qi, k_own, preferred_element_type=jnp.float32) * scale
                 + bias_tab[:, rel_bucket(dist_own)])
        s_own = jnp.where(dist_own >= 0, s_own, NEG)
        probs = jax.nn.softmax(jnp.concatenate([s_past, s_own], axis=-1), axis=-1)
        p_past = probs[..., :topk * MOBA_BLOCK].reshape(B, H, Q_BLOCK, topk, MOBA_BLOCK).astype(v.dtype)
        p_own = probs[..., topk * MOBA_BLOCK:].astype(v.dtype)
        o = (jnp.einsum('bhqns,bhqnsd->bhqd', p_past, v_sel, preferred_element_type=jnp.float32)
             + jnp.einsum('bhqs,bhsd->bhqd', p_own, v_own, preferred_element_type=jnp.float32))
        return o.astype(q.dtype)

    o = lax.map(per_block, (qs, jnp.arange(nq)))
    return o.transpose(1, 2, 0, 3, 4).reshape(B, H, T, hd)

def hybrid_mixer(xn, w_in, w_gk_up, b_gk, gla_out_norm, w_out, rel_bias):
    B, T, _ = xn.shape
    split_points = np.cumsum(IN_SIZES)[:-1].tolist()
    q_g, k_g, v_g, g_g, gk_lr, q_m, k_m, v_m = jnp.split(xn @ w_in, split_points, axis=-1)

    def heads(t, nh):
        return t.reshape(B, T, nh, -1).transpose(0, 2, 1, 3)

    log_a = jax.nn.log_sigmoid((gk_lr @ w_gk_up + b_gk).astype(jnp.float32)) / GLA_TAU
    o_g = gla_chunked(heads(q_g, GLA_HEADS) * (GLA_DK ** -0.5), heads(k_g, GLA_HEADS),
                      heads(v_g, GLA_HEADS), heads(log_a, GLA_HEADS))
    o_g = rmsnorm(o_g, gla_out_norm)
    o_g = o_g.transpose(0, 2, 1, 3).reshape(B, T, GLA_V) * jax.nn.silu(g_g)
    o_m = moba_attention(heads(q_m, MOBA_HEADS), heads(k_m, MOBA_HEADS), heads(v_m, MOBA_HEADS), rel_bias)
    o_m = o_m.transpose(0, 2, 1, 3).reshape(B, T, MOBA_W)
    return jnp.concatenate([o_g, o_m], axis=-1) @ w_out

def setup_inputs(seed: int = 0) -> dict:
    key = jax.random.key(seed)
    ks = jax.random.split(key, 24)
    f32 = jnp.float32

    def w(k, shape, fan_in):
        return jax.random.normal(k, shape, f32) * (fan_in ** -0.5)

    def gain(k, shape):
        return 1.0 + 0.02 * jax.random.normal(k, shape, f32)

    L = DEPTH
    return {
        "x": jax.random.normal(ks[0], (BATCH, SEQ, D_MODEL), f32),
        "p": jax.random.normal(ks[1], (DEPTH, BATCH, SEQ, D_PLE), f32),
        "ffn1_norm": gain(ks[2], (L, D_MODEL)),
        "ffn1_w_gu": w(ks[3], (L, D_MODEL, 2 * D_FF), D_MODEL),
        "ffn1_w_down": w(ks[4], (L, D_FF, D_MODEL), D_FF),
        "mix_norm": gain(ks[5], (L, D_MODEL)),
        "w_in": w(ks[6], (L, D_MODEL, IN_WIDTH), D_MODEL),
        "w_gk_up": w(ks[7], (L, GLA_LOWRANK, GLA_QK), GLA_LOWRANK),
        "b_gk": 0.01 * jax.random.normal(ks[8], (L, GLA_QK), f32),
        "gla_out_norm": gain(ks[9], (L, GLA_DV)),
        "w_out": w(ks[10], (L, MIX_WIDTH, D_MODEL), MIX_WIDTH),
        "ffn2_norm": gain(ks[11], (L, D_MODEL)),
        "ffn2_w_gu": w(ks[12], (L, D_MODEL, 2 * D_FF), D_MODEL),
        "ffn2_w_down": w(ks[13], (L, D_FF, D_MODEL), D_FF),
        "ple_norm": gain(ks[14], (L, D_MODEL)),
        "w_ple_gate": w(ks[15], (L, D_MODEL, D_MODEL), D_MODEL),
        "w_ple_proj": w(ks[16], (L, D_PLE, D_MODEL), D_PLE),
        "rel_bias": 0.2 * jax.random.normal(ks[17], (REL_BUCKETS, MOBA_HEADS), f32),
        "final_norm": gain(ks[18], (D_MODEL,)),
    }

def reference(x, p, ffn1_norm, ffn1_w_gu, ffn1_w_down, mix_norm, w_in, w_gk_up, b_gk,
              gla_out_norm, w_out, ffn2_norm, ffn2_w_gu, ffn2_w_down, ple_norm,
              w_ple_gate, w_ple_proj, rel_bias, final_norm):
    h = x
    for i in range(DEPTH):
        h = h + 0.5 * swiglu(rmsnorm(h, ffn1_norm[i]), ffn1_w_gu[i], ffn1_w_down[i])
        h = h + hybrid_mixer(rmsnorm(h, mix_norm[i]), w_in[i], w_gk_up[i], b_gk[i],
                             gla_out_norm[i], w_out[i], rel_bias)
        h = h + 0.5 * swiglu(rmsnorm(h, ffn2_norm[i]), ffn2_w_gu[i], ffn2_w_down[i])
        ple_gate = jax.nn.sigmoid(rmsnorm(h, ple_norm[i]) @ w_ple_gate[i])
        h = h + ple_gate * (p[i] @ w_ple_proj[i])
    return rmsnorm(h, final_norm)


_drawn_inputs = setup_inputs


def setup_inputs(seed=0):
    import zlib

    import numpy as np

    out = dict(_drawn_inputs(seed))
    spreads = {}
    factors = {'ffn1_norm': 5.842,
     'mix_norm': 3.53,
     'b_gk': 27.625,
     'gla_out_norm': 19.947,
     'ffn2_norm': 29.89,
     'ple_norm': 200.0,
     'rel_bias': 16.653,
     'final_norm': 24.669,
     'w_ple_gate': 17.438,
     'p': 3.44,
     'w_ple_proj': 3.423}
    for name, (base, spread) in spreads.items():
        noise = np.random.default_rng([zlib.crc32(name.encode()), seed]).standard_normal(out[name].shape)
        drawn = base * np.exp(spread * noise) if base else spread * noise
        out[name] = __import__('jax').numpy.asarray(drawn.astype(out[name].dtype))
    for name, factor in factors.items():
        out[name] = (out[name] * factor).astype(out[name].dtype)
    return out
```

```python
from contextlib import ExitStack

import concourse.bass as bass
from concourse import mybir

F32 = mybir.dt.float32
F32R = mybir.dt.float32r
I32 = mybir.dt.int32
ALU = mybir.AluOpType
ACT = mybir.ActivationFunctionType
AX = mybir.AxisListType.X

P = 128
T = 256
M = T // P
D = 1024
KC = D // P
F = 2816
FC = F // P
FB = 256
NB = F // FB
N = 512
RING = 4
CH = 4
EPS = 1e-6
PLE = 256

GH, GDK, GDV = 4, 64, 128
LR = 16
MH, MD = 8, 64
BUCKETS = 32
BIAS_W = 384
TAU = 16.0

QK_G, V_G, G_G, LR_G, Q_M, K_M, V_M = 0, 512, 1024, 1536, 1552, 2064, 2576
WIN_BLOCKS = [("q_m", Q_M), ("k_m", K_M), ("qk_g", QK_G), ("v_m", V_M), ("v_g", V_G), ("g_g", G_G)]

DOWN_CH = [4, 4, 4, 4, 4, 2]
U_GU = [0, 50]
U_DOWN = [22, 72]
U_WIN = 34
U_WOUT = 46
U_PROJ = 84
U_GATE = 86
UNITS = 90
B_GU = [0, 21]
B_DOWN = [11, 32]
B_WIN = 13
B_WOUT = 19
B_PROJ = 34
B_GATE = 36

MIX = {
    34: ["lr"],
    35: ["lrT"],
    36: ["z", "T_q_m0", "T_q_m1"],
    37: ["D0", "D1", "D2", "D3"],
    38: ["T_k_m0", "T_k_m1", "D4", "D5", "D6", "D7"],
    39: ["sc0"],
    40: ["T_g0", "T_g1", "pt0", "sc1"],
    41: ["diag", "lv0", "pv0", "pt1"],
    42: ["pv1", "sc2", "lv1"],
    43: ["pt2", "sc3", "lv2", "lv3"],
    44: ["pv2", "pt3", "pvg"],
    45: ["pv3"],
    47: ["T_o0", "T_o1"],
}
Z_AT = {40: [0, 1], 41: [2, 3, 4, 5], 42: [6, 7]}


def chunks_of(u):
    for d in U_DOWN:
        if d <= u < d + 12:
            return DOWN_CH[(u - d) % 6]
    return 2 if U_PROJ <= u < U_GATE else CH


def plan_turns():
    at, n = {}, 0

    def add(name, k=1):
        nonlocal n
        at[name] = n
        n += k

    add("h0.0", 2)
    add("h0.1", 2)
    add("act0", NB)
    add("h1.0", 2)
    add("h1.1", 2)
    for u in sorted(MIX):
        for s in MIX[u]:
            if s[:2] == "T_":
                add(s)
            elif s[:2] == "pt":
                add(s, 2)
            elif s[:2] == "pv" and s != "pvg":
                add(s)
    add("h2.0", 2)
    add("h2.1", 2)
    add("act1", NB)
    add("p")
    add("h3.0", 2)
    add("h3.1", 2)
    return at


def plan_side():
    uses = [("gain", "dve"), ("bias_row", "dve")]
    for u in sorted(MIX):
        for s in MIX[u]:
            if s[0] == "D":
                uses.append((s, "act"))
            elif s[:2] == "sc":
                uses += [(f"{s}.{i}", "dve") for i in range(2)]
            elif s == "diag" or s[:2] == "lv":
                uses += [(f"{s}.{hh}", "dve") for hh in range(2)]
            elif s == "pvg":
                uses += [("pvg0", "dve"), ("pvg1", "dve")]
            elif s in ("lr", "lrT", "z"):
                uses.append((s, "dve"))
    count, out = {"dve": 0, "act": 0}, {}
    for i, (name, who) in enumerate(uses):
        count[who] += 1
        out[name] = (i, who, count[who])
    return out


TURN = plan_turns()
SIDE = plan_side()
SIDE_AT = {i: (who, c) for i, who, c in SIDE.values()}


def view(ap, dims, offset=0):
    return bass.AP(tensor=ap.tensor, offset=ap.offset + offset, ap=[list(ap.ap[0])] + [list(d) for d in dims])


def build(nc, x, p, ffn1_norm, ffn1_w_gu, ffn1_w_down, mix_norm, w_in, w_gk_up, b_gk, gla_out_norm,
          w_out, ffn2_norm, ffn2_w_gu, ffn2_w_down, ple_norm, w_ple_gate, w_ple_proj, rel_bias,
          final_norm, identity, seg_sums, pair_masks, bucket_rows, causal_row, out):
    x, out, w_gk_up, w_in, w_out = x[0], out[0], w_gk_up[0], w_in[0], w_out[0]
    p, w_ple_gate, w_ple_proj = p[0][0], w_ple_gate[0], w_ple_proj[0]
    ffn1_w_gu, ffn1_w_down, ffn2_w_gu, ffn2_w_down = ffn1_w_gu[0], ffn1_w_down[0], ffn2_w_gu[0], ffn2_w_down[0]
    ctx = ExitStack()
    with ctx:
        def sem(name):
            return ctx.enter_context(nc.semaphore(name))

        base = (nc.sbuf_base + 63) // 64 * 64
        top = [base]

        def sb(name, shape, dt=F32):
            size = 4
            for s in shape[1:]:
                size *= s
            t = nc.alloc_sbuf_tensor_at(name, shape, dt, offset=top[0])
            top[0] += (size + 31) // 32 * 32
            return t

        raw = sb("raw", [P, RING, CH * N])
        w_hi = sb("w_hi", [P, RING, CH * N], F32R)
        w_lo = sb("w_lo", [P, RING, CH * N], F32R)
        h = sb("h", [P, M, D])
        hT_hi = sb("hT_hi", [P, KC, T], F32R)
        hT_lo = sb("hT_lo", [P, KC, T], F32R)
        ident = sb("ident", [P, P])
        ident_r = sb("ident_r", [P, P], F32R)
        gains = sb("gains", [P, 4 * KC])
        lrw_hi = sb("lrw_hi", [P, KC, LR], F32R)
        lrw_lo = sb("lrw_lo", [P, KC, LR], F32R)
        lr_nat = sb("lr_nat", [P, M, LR])
        gk_up = sb("gk_up", [LR + 1, GH * GDK])
        gout = sb("gout", [P, GDV])
        ssq = sb("ssq", [P, 5, 2, M])
        rstd = sb("rstd", [P, 5, M])
        rtmp = sb("rtmp", [P, 5, M])
        mx = sb("mx", [P, MH, M])
        sums = sb("sums", [P, MH, M])
        gss = sb("gss", [P, M, GH])
        grs = sb("grs", [P, M, GH])
        junk = sb("junk", [P, N], mybir.dt.bfloat16)
        region = top[0]

        def at(name, kib, shape, dt=F32):
            size = 4
            for s in shape[1:]:
                size *= s
            assert region + int(kib * 1024) + size <= nc.sbuf_usable_end, name
            return nc.alloc_sbuf_tensor_at(name, shape, dt, offset=region + int(kib * 1024))

        a_hiT = at("a_hiT", 0, [P, FC, T], F32R)
        a_loT = at("a_loT", 22, [P, FC, T], F32R)
        silu_g = at("silu_g", 44, [P, M, FB])
        act = at("act", 46, [P, M, FB])
        act_hi = at("act_hi", 48, [P, M, FB], F32R)
        act_lo = at("act_lo", 50, [P, M, FB], F32R)
        hs_hi = at("hs_hi", 52, [P, M, N], F32R)
        hs_lo = at("hs_lo", 56, [P, M, N], F32R)
        gain_rows = at("gain_rows", 60, [4 * KC, P])
        rel = at("rel", 61, [BUCKETS, MH])
        rows = at("rows", 62, [BUCKETS, BIAS_W])
        causal = at("causal", 64, [MH, BIAS_W])
        bias_row = at("bias_row", 66, [MH, BIAS_W])
        lrw = at("lrw", 68, [P, KC, LR])
        seg_f = at("seg_f", 69, [P, 9 * P])
        E = at("E", 0, [P, 9, 2 * T])
        nat0 = at("nat0", 18, [P, M, N])
        nat1 = at("nat1", 22, [P, M, N])
        q_mT = at("q_mT", 26, [P, MH // 2, T])
        k_mT = at("k_mT", 30, [P, MH // 2, T])
        bias = at("bias", 34, [P, MH, T])
        q_gT = at("q_gT", 42, [P, 2 * T])
        k_gT = at("k_gT", 44, [P, 2 * T])
        gg = at("gg", 42, [P, M, N])
        lg = at("lg", 46, [P, M * T])
        log_a = at("log_a", 48, [P, M * T])
        vg = at("vg", 46, [P, M, N])
        lrT = at("lrT", 50, [LR + 1, T])
        sq = at("sq", 50, [P, N])
        la_hi = at("la_hi", 60, [P, M * T], F32R)
        la_lo = at("la_lo", 62, [P, M * T], F32R)
        AT = at("AT", 18, [P, 2 * GH, P])
        AT2 = at("AT2", 60, [P, GH, P])
        pr = at("pr", 62, [P, 2, 3 * P])
        prT = at("prT", 65, [P, 2, 3 * P])
        oT_hi = at("oT_hi", 68, [P, MH // 2, T], F32R)
        oT_lo = at("oT_lo", 72, [P, MH // 2, T], F32R)
        seg = at("seg", 76, [P, 9 * P], F32R)
        masks = at("masks", 54, [P, 7 * 64 + P], I32)
        p_nat = at("p_nat", 60, [P, M, PLE])
        p_hi = at("p_hi", 62, [P, M, PLE], F32R)
        p_lo = at("p_lo", 64, [P, M, PLE], F32R)
        pT_hi = at("pT_hi", 66, [P, 2, T], F32R)
        pT_lo = at("pT_lo", 68, [P, 2, T], F32R)
        pp = at("pp", 12, [P, M, D])
        fgain = at("fgain", 70, [P, D])
        gate = at("gate", 0, [P, M, N])
        res = at("res", 4, [P, M, D])

        acc = ctx.enter_context(nc.psum_tensor("acc", [P, 4, N], F32))
        turn = ctx.enter_context(nc.psum_tensor("turn", [P, 2, N], F32))
        side = ctx.enter_context(nc.psum_tensor("side", [P, 2, N], F32))

        row_dram = nc.dram_tensor("bias_row_dram", [MH, BIAS_W], F32).ap()
        skew_dram = nc.dram_tensor("bias_skew_dram", [P, MH, BIAS_W], F32).ap()

        x_in = [sem(f"x_in{n}") for n in range(2)]
        ident_in = sem("ident_in")
        gains_in = sem("gains_in")
        lrw_in = sem("lrw_in")
        seg_in = sem("seg_in")
        small_in = sem("small_in")
        masks_in = sem("masks_in")
        bias_in = sem("bias_in")
        row_out = sem("row_out")
        skew_out = sem("skew_out")
        biasT_in = sem("biasT_in")
        ple_in = sem("ple_in")
        raw_in = [sem(f"raw_in{s}") for s in range(RING)]
        hi_ready = sem("hi_ready")
        lo_ready = sem("lo_ready")
        unit_done = sem("unit_done")
        acc_read = sem("acc_read")
        turn_done = sem("turn_done")
        turn_hi = sem("turn_hi")
        turn_read = sem("turn_read")
        side_done = sem("side_done")
        side_dve = sem("side_dve")
        side_act = sem("side_act")
        hs_hi_ready = sem("hs_hi_ready")
        hs_lo_ready = sem("hs_lo_ready")
        ssq_ready = sem("ssq_ready")
        ms_ready = sem("ms_ready")
        root_ready = sem("root_ready")
        rstd_ready = sem("rstd_ready")
        silu_ready = sem("silu_ready")
        act_hi_ready = sem("act_hi_ready")
        act_lo_ready = sem("act_lo_ready")
        idr_ready = sem("idr_ready")
        consts_hi = sem("consts_hi")
        consts_lo = sem("consts_lo")
        z_abs = sem("z_abs")
        lg_ready = sem("lg_ready")
        la_ready = sem("la_ready")
        la_hi_ready = sem("la_hi_ready")
        la_lo_ready = sem("la_lo_ready")
        Z_ready = sem("Z_ready")
        neg_max = sem("neg_max")
        exp_ready = sem("exp_ready")
        probs_ready = sem("probs_ready")
        gss_sq = sem("gss_sq")
        gms_ready = sem("gms_ready")
        groot = sem("groot")
        gg_silu = sem("gg_silu")
        og_hi_ready = sem("og_hi_ready")
        og_lo_ready = sem("og_lo_ready")
        p_hi_ready = sem("p_hi_ready")
        p_lo_ready = sem("p_lo_ready")
        gate_ready = sem("gate_ready")
        h_final = sem("h_final")
        res_ready = sem("res_ready")
        res_out = sem("res_out")
        dve_step = sem("dve_step")
        act_step = sem("act_step")

        block = ctx.enter_context(nc.Block())

        GU_W = [ffn1_w_gu, ffn2_w_gu]
        DOWN_W = [ffn1_w_down, ffn2_w_down]

        @block.sync
        def _(sp):
            def free(u):
                if not isinstance(u, int) or u >= RING:
                    sp.wait_ge(lo_ready, u - (RING - 1))

            def gu_unit(f, b, kh, u, slot):
                free(u)
                w = GU_W[f].rearrange("(c p) f -> p c f", p=P)
                dst = raw[:, slot, :].rearrange("p (k g f) -> p k g f", k=CH, g=2)
                for g in range(2):
                    sp.dma_start(dst[:, :, g, :], w[:, CH * kh:CH * kh + CH, bass.ds(g * F + b * FB, FB)]
                                 ).then_inc(raw_in[slot], 16)

            def unit(w, c0, col, u):
                free(u)
                nk = chunks_of(u)
                slot = u % RING
                wv = w.rearrange("(c p) f -> p c f", p=P)
                dst = raw[:, slot, :nk * N].rearrange("p (k f) -> p k f", k=nk)
                for a in range(2):
                    r = slice(a * nk // 2, (a + 1) * nk // 2)
                    sp.dma_start(dst[:, r, :], wv[:, c0 + r.start:c0 + r.stop, col:col + N]
                                 ).then_inc(raw_in[slot], 16)

            def ffn(f):
                first = 3
                for b in range(first):
                    for kh in range(2):
                        u = U_GU[f] + 2 * b + kh
                        gu_unit(f, b, kh, u, u % RING)
                with sp.Fori(0, (NB - first) // 2) as i:
                    for j in range(2):
                        for kh in range(2):
                            u = U_GU[f] + 2 * (first + j) + kh
                            gu_unit(f, i * 2 + (first + j), kh, i * 4 + u, u % RING)
                for n in range(2):
                    for k in range(6):
                        unit(DOWN_W[f], CH * k, n * N, U_DOWN[f] + 6 * n + k)

            xv = x.rearrange("(m p) d -> p m d", p=P)
            for n in range(2):
                sp.dma_start(h[:, :, n * N:(n + 1) * N], xv[:, :, n * N:(n + 1) * N]).then_inc(x_in[n], 16)
            ffn(0)
            for b, (_, col) in enumerate(WIN_BLOCKS):
                for kh in range(2):
                    unit(w_in, CH * kh, col, U_WIN + 2 * b + kh)
            for v, (n, kh) in enumerate([(0, 1), (1, 1), (0, 0), (1, 0)]):
                unit(w_out, CH * kh, n * N, U_WOUT + v)
            ffn(1)
            for n in range(2):
                unit(w_ple_proj, 0, n * N, U_PROJ + n)
            for n in range(2):
                for kh in range(2):
                    unit(w_ple_gate, CH * kh, n * N, U_GATE + 2 * n + kh)
            ov = out.rearrange("(m p) d -> p m d", p=P)
            for m in range(M):
                sp.wait_ge(res_ready, m + 1)
                sp.dma_start(ov[:, m, :], res[:, m, :]).then_inc(res_out, 16)
            sp.wait_ge(res_out, 16 * M)

        @block.gpsimd
        def _(pool):
            pool.dma_start(rel[:], rel_bias).then_inc(bias_in, 16)
            pool.dma_start(rows[:], bucket_rows).then_inc(bias_in, 16)
            pool.dma_start(causal[:], causal_row).then_inc(bias_in, 16)
            pool.dma_start(gk_up[0:LR, :], w_gk_up).then_inc(small_in, 16)
            pool.dma_start(gk_up[LR:LR + 1, :], b_gk).then_inc(small_in, 16)
            pool.dma_start(gout[:], bass.AP(tensor=gla_out_norm.tensor, offset=0, ap=[[0, P], [1, GDV]])).then_inc(small_in, 16)
            pool.wait_ge(side_dve, SIDE["bias_row"][2])
            pool.dma_start(row_dram, bias_row[:]).then_inc(row_out, 16)
            pool.wait_ge(row_out, 16)
            pool.dma_start(skew_dram, bass.AP(tensor=row_dram.tensor, offset=0,
                                              ap=[[0, P], [BIAS_W, MH], [1, BIAS_W]])).then_inc(skew_out, 16)
            pool.wait_ge(skew_out, 16)
            pool.wait_ge(unit_done, U_WIN)
            pool.dma_start(bias[:], bass.AP(tensor=skew_dram.tensor, offset=P - 1,
                                            ap=[[MH * BIAS_W - 1, P], [BIAS_W, MH], [1, T]])).then_inc(biasT_in, 16)
            pool.wait_ge(unit_done, U_WIN + 1)
            pool.dma_start(masks[:], pair_masks).then_inc(masks_in, 16)
            pool.wait_ge(unit_done, U_GU[1])
            pool.dma_start(p_nat[:], p.rearrange("(m p) e -> p m e", p=P)).then_inc(ple_in, 16)
            pool.dma_start(fgain[:], bass.AP(tensor=final_norm.tensor, offset=0, ap=[[0, P], [1, D]])).then_inc(ple_in, 16)

        @block.tensor
        def _(pe):
            def mm(o, lhsT, rhs, start, stop):
                return nc.tensor.matmul(o, lhsT, rhs, start=start, stop=stop, skip_group_check=True)

            def exact3(o, l_hi, l_lo, r_hi, r_lo, start, stop):
                mm(o, l_hi, r_hi, start, False)
                mm(o, l_hi, r_lo, False, False)
                return mm(o, l_lo, r_hi, False, stop)

            def unit(u, slot, pair, lhs, k0, nk, first, last, part=None):
                if part in (None, 0):
                    pe.wait_ge(lo_ready, u + 1)
                ks = range(nk) if part is None else range(part * nk // 2, (part + 1) * nk // 2)
                for k in ks:
                    for m in range(M):
                        l_hi, l_lo = lhs(k0 + k, m)
                        ins = exact3(acc[:, 2 * pair + m, :], l_hi, l_lo,
                                     w_hi[:, slot, k * N:(k + 1) * N], w_lo[:, slot, k * N:(k + 1) * N],
                                     first and k == 0, last and k == nk - 1)
                if part in (None, 1):
                    ins.then_inc(unit_done, 1)

            def acc_free(B):
                if not isinstance(B, int) or B >= 2:
                    pe.wait_ge(acc_read, (B - 1) * 2)

            def from_hT(c, m):
                return hT_hi[:, c, m * P:(m + 1) * P], hT_lo[:, c, m * P:(m + 1) * P]

            def from_aT(c, m):
                return a_hiT[:, c, m * P:(m + 1) * P], a_loT[:, c, m * P:(m + 1) * P]

            def turn_open(t):
                if not isinstance(t, int) or t >= 2:
                    pe.wait_ge(turn_read, t - 1)

            def turn_split(bank, k, src_hi, src_lo):
                o = turn[:, bank, k * P:(k + 1) * P]
                mm(o, src_hi, ident_r[:], True, False)
                return mm(o, src_lo, ident_r[:], False, True)

            def h_turns(s, n):
                pe.wait_ge(hs_lo_ready, 2 * (2 * s + n) + 2)
                for a in range(2):
                    t = TURN[f"h{s}.{n}"] + a
                    turn_open(t)
                    for c in range(2):
                        for m in range(M):
                            r = slice((2 * a + c) * P, (2 * a + c + 1) * P)
                            ins = turn_split(t % 2, 2 * c + m, hs_hi[:, m, r], hs_lo[:, m, r])
                    ins.then_inc(turn_done, 1)

            def h_ready(s, n):
                pe.wait_ge(turn_read, TURN[f"h{s}.{n}"] + 2)

            def act_turn(f, b, par):
                pe.wait_ge(act_lo_ready, b * 2 + (2 * NB * f + 2))
                t = b + TURN[f"act{f}"]
                turn_open(t)
                for c in range(2):
                    for m in range(M):
                        ins = turn_split((TURN[f"act{f}"] + par) % 2, 2 * c + m,
                                         act_hi[:, m, c * P:(c + 1) * P], act_lo[:, m, c * P:(c + 1) * P])
                ins.then_inc(turn_done, 1)

            def gu_block(f, b, par, s0, first=False):
                pair = (B_GU[f] + par) % 2
                acc_free(b + B_GU[f])
                u = b * 2 + U_GU[f]
                if first:
                    s = 2 * f
                    h_ready(s, 0)
                    unit(u, s0, pair, from_hT, 0, CH, True, False, part=0)
                    h_turns(s, 1)
                    unit(u, s0, pair, from_hT, 0, CH, True, False, part=1)
                    h_ready(s, 1)
                else:
                    unit(u, s0, pair, from_hT, 0, CH, True, False)
                    act_turn(f, b - 1, 1 - par)
                unit(u + 1, (s0 + 1) % RING, pair, from_hT, CH, CH, False, True)

            def ffn(f):
                gu_block(f, 0, 0, U_GU[f] % RING, first=True)
                with pe.Fori(0, (NB - 1) // 2) as i:
                    for j in range(2):
                        gu_block(f, i * 2 + (1 + j), (1 + j) % 2, (U_GU[f] + 2 + 2 * j) % RING)
                for n in range(2):
                    B = B_DOWN[f] + n
                    acc_free(B)
                    for k in range(6):
                        u = U_DOWN[f] + 6 * n + k
                        if n == 0:
                            pe.wait_ge(turn_read, TURN[f"act{f}"] + min(2 * k + 2, NB))
                        unit(u, u % RING, B % 2, from_aT, CH * k, DOWN_CH[k], k == 0, k == 5)
                        if n == 0 and k == 0:
                            act_turn(f, NB - 1, (NB - 1) % 2)
                        if f == 1 and n == 0 and k == 2:
                            p_turn()
                        if n == 1 and k == 1:
                            h_turns(2 * f + 1, 0)

            def p_turn():
                pe.wait_ge(p_lo_ready, 1)
                t = TURN["p"]
                turn_open(t)
                for c in range(2):
                    for m in range(M):
                        ins = turn_split(t % 2, 2 * c + m, p_hi[:, m, c * P:(c + 1) * P], p_lo[:, m, c * P:(c + 1) * P])
                ins.then_inc(turn_done, 1)

            def side_open(name):
                i = SIDE[name][0]
                if i >= 2:
                    who, count = SIDE_AT[i - 2]
                    pe.wait_ge(side_dve if who == "dve" else side_act, count)
                return side[:, i % 2, :]

            def flip(o, src, k=P):
                return nc.tensor.transpose(o, src, ident[:k, :k])

            def nat_turn(name, src, cols):
                t = TURN[name]
                turn_open(t)
                for c in range(2):
                    for m in range(M):
                        ins = flip(turn[:, t % 2, (2 * c + m) * P:(2 * c + m + 1) * P],
                                   src[:, m, cols + c * P:cols + (c + 1) * P])
                ins.then_inc(turn_done, 1)

            def step(s):
                if s == "lr":
                    o = side_open(s)
                    pe.wait_ge(consts_lo, 1)
                    for m in range(M):
                        for c in range(KC):
                            l_hi, l_lo = from_hT(c, m)
                            ins = exact3(o[:, m * LR:(m + 1) * LR], l_hi, l_lo, lrw_hi[:, c, :], lrw_lo[:, c, :],
                                         c == 0, c == KC - 1)
                    ins.then_inc(side_done, 1)
                elif s == "lrT":
                    o = side_open(s)
                    pe.wait_ge(side_dve, SIDE["lr"][2])
                    for m in range(M):
                        ins = flip(o[0:LR, m * P:(m + 1) * P], lr_nat[:, m, :])
                    ins.then_inc(side_done, 1)
                elif s == "z":
                    o = side_open(s)
                    pe.wait_ge(side_dve, SIDE["lrT"][2])
                    pe.wait_ge(small_in, 48)
                    for m in range(M):
                        ins = mm(o[:, m * T:(m + 1) * T], lrT[:, m * P:(m + 1) * P], gk_up[:], True, True)
                    ins.then_inc(side_done, 1)
                elif s in ("T_q_m0", "T_q_m1"):
                    pe.wait_ge(acc_read, 2 * B_WIN + 2)
                    nat_turn(s, nat0, 2 * P * int(s[-1]))
                elif s in ("T_k_m0", "T_k_m1"):
                    pe.wait_ge(acc_read, 2 * B_WIN + 4)
                    nat_turn(s, nat1, 2 * P * int(s[-1]))
                elif s in ("T_g0", "T_g1"):
                    pe.wait_ge(acc_read, 2 * B_WIN + 6)
                    nat_turn(s, nat0, 2 * P * int(s[-1]))
                elif s[0] == "D":
                    d = int(s[1])
                    m, hp, half = d // 4, d // 2 % 2, d % 2
                    o = side_open(s)
                    pe.wait_ge(la_lo_ready, 1)
                    lhs = slice(m * T + hp * P, m * T + (hp + 1) * P)
                    r = seg[:, (m + 4 * half) * P:(m + 4 * half + 4) * P]
                    mm(o, la_hi[:, lhs], r, True, False)
                    mm(o, la_lo[:, lhs], r, False, True).then_inc(side_done, 1)
                elif s[:2] == "sc":
                    for i in range(2):
                        head = 2 * int(s[2]) + i
                        o = side_open(f"{s}.{i}")
                        pe.wait_ge(turn_read, TURN["T_k_m1"] + 1)
                        lo = 64 * (head % 2)
                        q, k = q_mT[lo:lo + 64, head // 2, :], k_mT[lo:lo + 64, head // 2, :]
                        mm(o[:, 0:P], q[:, 0:P], k[:, 0:P], True, True)
                        mm(o[:, P:3 * P], q[:, P:T], k[:, :], True, True).then_inc(side_done, 1)
                elif s[:2] == "pt":
                    pair = int(s[2])
                    for i in range(2):
                        t = TURN[s] + i
                        pe.wait_ge(probs_ready, 2 * pair + i + 1)
                        turn_open(t)
                        for k in range(3):
                            ins = flip(turn[:, t % 2, k * P:(k + 1) * P], pr[:, i, k * P:(k + 1) * P])
                        ins.then_inc(turn_done, 1)
                elif s == "pvg":
                    for m in range(M):
                        o = side_open(f"pvg{m}")
                        pe.wait_ge(acc_read, 2 * B_WIN + 10)
                        pe.wait_ge(side_dve, SIDE["lv3.1"][2])
                        for hd in range(GH):
                            c = slice(hd * GDV, (hd + 1) * GDV)
                            hh, hp = hd % 2, hd // 2
                            ins = mm(o[:, c], AT[:, 4 * hh + 2 * hp + m, :], vg[:, m, c], True, m == 0)
                            if m == 1:
                                ins = mm(o[:, c], AT2[:, 2 * hh + hp, :], vg[:, 0, c], False, True)
                        ins.then_inc(side_done, 1)
                elif s[:2] == "pv":
                    pair = int(s[2])
                    t = TURN[s]
                    pe.wait_ge(turn_read, TURN[f"pt{pair}"] + 2)
                    pe.wait_ge(acc_read, 2 * B_WIN + 8)
                    turn_open(t)
                    for i in range(2):
                        c = slice((2 * pair + i) * MD, (2 * pair + i + 1) * MD)
                        o = turn[64 * i:64 * i + 64, t % 2, 0:T]
                        mm(o, nat1[:, 0, c], prT[:, i, 0:T], True, False)
                        ins = mm(o[:, P:T], nat1[:, 1, c], prT[:, i, T:T + P], False, True)
                    ins.then_inc(turn_done, 1)
                elif s == "diag":
                    for hh in range(2):
                        o = side_open(f"diag.{hh}")
                        pe.wait_ge(turn_read, TURN["T_g1"] + 1)
                        r = slice(64 * hh, 64 * hh + 64)
                        for k in range(4):
                            c = slice(k * P, (k + 1) * P)
                            ins = mm(o[:, c], k_gT[r, c], q_gT[r, c], True, True)
                        ins.then_inc(side_done, 1)
                elif s[:2] == "lv":
                    for hh in range(2):
                        o = side_open(f"{s}.{hh}")
                        r = slice(64 * hh, 64 * hh + 64)
                        pe.wait_ge(Z_ready, 2 * int(s[2]) + 2)
                        for a in range(2):
                            lv = 2 * int(s[2]) + a
                            w = 1 << lv
                            if lv == 7:
                                for hp in range(2):
                                    c = hp * T
                                    ins = mm(o[:, T + hp * P:T + (hp + 1) * P], E[r, 0, c:c + P], E[r, 8, c + P:c + T],
                                             True, True)
                            else:
                                for k in range(4):
                                    z = E[r, lv + 1, k * P:(k + 1) * P]
                                    ins = mm(o[:, a * T + k * 64:a * T + (k + 1) * 64], z,
                                             view(z, [[2 * w, 64 // w], [1, w]], w), True, True)
                        ins.then_inc(side_done, 1)
                elif s[:3] == "T_o":
                    a = int(s[3])
                    t = TURN[s]
                    pe.wait_ge(og_lo_ready, 1)
                    turn_open(t)
                    for c in range(2):
                        for m in range(M):
                            k = m * 2 + (2 * a + c) // 2
                            r = slice((2 * a + c) % 2 * P, (2 * a + c) % 2 * P + P)
                            ins = turn_split(t % 2, 2 * c + m, hT_hi[:, k, r], hT_lo[:, k, r])
                    ins.then_inc(turn_done, 1)

            def from_oT(c, m):
                r = slice(m * P, (m + 1) * P)
                if c < 4:
                    return hT_hi[:, 4 + c, r], hT_lo[:, 4 + c, r]
                return oT_hi[:, c - 4, r], oT_lo[:, c - 4, r]

            pe.wait_ge(ident_in, 16)
            pe.wait_ge(gains_in, 64)
            o = side_open("gain")
            flip(o[:, 0:4 * KC], gain_rows[:], 4 * KC).then_inc(side_done, 1)
            o = side_open("bias_row")
            pe.wait_ge(bias_in, 48)
            mm(o[0:MH, 0:BIAS_W], rel[:], rows[:], True, True).then_inc(side_done, 1)
            pe.wait_ge(idr_ready, 1)
            h_turns(0, 0)
            ffn(0)
            for b in range(len(WIN_BLOCKS)):
                B = B_WIN + b
                for kh in range(2):
                    u = U_WIN + 2 * b + kh
                    if b == 0 and kh == 0:
                        acc_free(B)
                        h_ready(1, 0)
                        unit(u, u % RING, B % 2, from_hT, 0, CH, True, False, part=0)
                        h_turns(1, 1)
                        unit(u, u % RING, B % 2, from_hT, 0, CH, True, False, part=1)
                        h_ready(1, 1)
                    else:
                        if kh == 0:
                            acc_free(B)
                        unit(u, u % RING, B % 2, from_hT, CH * kh, CH, kh == 0, kh == 1)
                    for s in MIX.get(u, []):
                        step(s)
            for v, (n, kh) in enumerate([(0, 1), (1, 1), (0, 0), (1, 0)]):
                u, B = U_WOUT + v, B_WOUT + n
                if kh == 1:
                    acc_free(B)
                pe.wait_ge(turn_read, TURN["pv3"] + 1 if kh == 1 else TURN["T_o1"] + 1)
                unit(u, u % RING, B % 2, from_oT, CH * kh, CH, kh == 1, kh == 0)
                for s in MIX.get(u, []):
                    step(s)
            h_turns(2, 0)
            ffn(1)
            for n in range(2):
                u, B = U_PROJ + n, B_PROJ + n
                acc_free(B)
                pe.wait_ge(turn_read, TURN["p"] + 1)
                unit(u, u % RING, B % 2,
                     lambda c, m: (pT_hi[:, c, m * P:(m + 1) * P], pT_lo[:, c, m * P:(m + 1) * P]), 0, 2, True, True)
                if n == 0:
                    h_turns(3, 1)
            h_ready(3, 1)
            for n in range(2):
                B = B_GATE + n
                acc_free(B)
                for kh in range(2):
                    u = U_GATE + 2 * n + kh
                    unit(u, u % RING, B % 2, from_hT, CH * kh, CH, kh == 0, kh == 1)

        @block.scalar
        def _(act_e):
            A = nc.scalar.activation

            def split(v, slot=None, turn_of_slot=None):
                if isinstance(v, int):
                    if v >= UNITS:
                        return
                    slot, turn_of_slot, nk = v % RING, v // RING, chunks_of(v)
                else:
                    nk = CH
                act_e.wait_ge(raw_in[slot], turn_of_slot * 32 + 32)
                if not isinstance(v, int) or v >= RING:
                    act_e.wait_ge(unit_done, v - (RING - 1))
                A(w_hi[:, slot, :nk * N], raw[:, slot, :nk * N], ACT.Copy).then_inc(hi_ready, 1)

            def h_split(s, n):
                for m in range(M):
                    if s == 0:
                        act_e.wait_ge(x_in[n], 16)
                    else:
                        B = {1: B_DOWN[0], 2: B_WOUT, 3: B_DOWN[1]}[s] + n
                        act_e.wait_ge(acc_read, 2 * B + m + 1)
                    k = 2 * s + n
                    if k:
                        act_e.wait_ge(turn_done, TURN[f"h{(k - 1) // 2}.{(k - 1) % 2}"] + 2)
                    A(hs_hi[:, m, :], h[:, m, n * N:(n + 1) * N], ACT.Copy).then_inc(hs_hi_ready, 1)

            def squares(s, n):
                for m in range(M):
                    if 4 * s + 2 * n + m:
                        act_e.wait_ge(ssq_ready, 4 * s + 2 * n + m)
                    A(junk[:], h[:, m, n * N:(n + 1) * N], ACT.Square,
                      accum_out=ssq[:, s, n, m:m + 1]).then_inc(ssq_ready, 1)

            def h_turns(s, n):
                for a in range(2):
                    t = TURN[f"h{s}.{n}"] + a
                    act_e.wait_ge(turn_done, t + 1)
                    for c in range(2):
                        k = 4 * n + 2 * a + c
                        if s == 0 and n == 0 and a == 0 and c == 0:
                            act_e.wait_ge(side_dve, SIDE["gain"][2])
                        A(hT_hi[:, k, :], turn[:, t % 2, c * T:(c + 1) * T], ACT.Copy,
                          scale=gains[:, s * KC + k:s * KC + k + 1]).then_inc(turn_hi, 1)

            def root(s):
                act_e.wait_ge(ms_ready, s + 1)
                A(rtmp[:, s, :], rtmp[:, s, :], ACT.Sqrt).then_inc(root_ready, 1)

            def act_turn(f, b, par):
                t = b + TURN[f"act{f}"]
                act_e.wait_ge(turn_done, t + 1)
                dst = a_hiT[:, bass.ds(b * 2, 2), :]
                A(dst, turn[:, (TURN[f"act{f}"] + par) % 2, :].rearrange("p (c t) -> p c t", c=2), ACT.Copy).then_inc(turn_hi, 1)

            def gated(f, b, par):
                B = b + B_GU[f]
                for m in range(M):
                    if m == 0:
                        act_e.wait_ge(unit_done, b * 2 + (U_GU[f] + 2))
                        if isinstance(b, int) and b == 0:
                            act_e.wait_ge(rstd_ready, 2 * f + 1)
                        if not (isinstance(b, int) and B == 0):
                            act_e.wait_ge(acc_read, B * 2)
                    A(silu_g[:, m, :], acc[:, 2 * ((B_GU[f] + par) % 2) + m, 0:FB], ACT.Silu,
                      scale=rstd[:, 2 * f, m:m + 1]).then_inc(silu_ready, 1)
                for m in range(M):
                    act_e.wait_ge(acc_read, B * 2 + (m + 1))
                    A(act_hi[:, m, :], act[:, m, :], ACT.Copy).then_inc(act_hi_ready, 1)

            def ffn(f):
                U = U_GU[f]

                def blk(b, j, i=None):
                    def sp_(k):
                        v = U + 2 * j + k + RING
                        if i is None:
                            split(v)
                        else:
                            split(i * 4 + v, v % RING, i + v // RING)
                    if j == 0:
                        h_split(2 * f, 1)
                        h_turns(2 * f, 1)
                        squares(2 * f, 1)
                        root(2 * f)
                        sp_(0)
                    else:
                        act_turn(f, b - 1, (j - 1) % 2)
                        sp_(0)
                    gated(f, b, j % 2)
                    sp_(1)

                blk(0, 0)
                with act_e.Fori(0, (NB - 1) // 2) as i:
                    for j in range(2):
                        blk(i * 2 + (1 + j), 1 + j, i)
                for n in range(2):
                    for k in range(6):
                        u = U_DOWN[f] + 6 * n + k
                        if n == 0 and k == 0:
                            act_turn(f, NB - 1, (NB - 1) % 2)
                        if f == 1 and n == 0 and k == 1:
                            act_e.wait_ge(ple_in, 32)
                            A(p_hi[:], p_nat[:], ACT.Copy).then_inc(p_hi_ready, 1)
                        if f == 1 and n == 0 and k == 2:
                            t = TURN["p"]
                            act_e.wait_ge(turn_done, t + 1)
                            A(pT_hi[:], turn[:, t % 2, :].rearrange("p (c t) -> p c t", c=2), ACT.Copy).then_inc(turn_hi, 1)
                        if n == 1 and k == 0:
                            h_split(2 * f + 1, 0)
                            squares(2 * f + 1, 0)
                        if n == 1 and k == 1:
                            h_turns(2 * f + 1, 0)
                        split(u + RING)

            def step(s):
                if s == "z":
                    act_e.wait_ge(side_done, SIDE[s][0] + 1)
                    z = side[:, SIDE[s][0] % 2, :]
                    A(lg[:], z, ACT.Abs).then_inc(z_abs, 1)
                    act_e.wait_ge(z_abs, 1)
                    A(lg[:], lg[:], ACT.Exp, scale=-1.0).then_inc(act_step, 1)
                    act_e.wait_ge(act_step, 1)
                    A(lg[:], lg[:], ACT.Ln, bias=1.0).then_inc(lg_ready, 1)
                    act_e.wait_ge(la_ready, 1)
                    A(la_hi[:], log_a[:], ACT.Copy).then_inc(la_hi_ready, 1)
                elif s[0] == "D":
                    d = int(s[1])
                    m, hp, half = d // 4, d // 2 % 2, d % 2
                    act_e.wait_ge(side_done, SIDE[s][0] + 1)
                    k = m + 4 * half
                    A(E[:, k:k + 4, hp * T + m * P:hp * T + (m + 1) * P], side[:, SIDE[s][0] % 2, :].rearrange("p (l t) -> p l t", l=4), ACT.Exp
                      ).then_inc(side_act, 1)
                elif s[:2] == "sc":
                    for i in range(2):
                        head = 2 * int(s[2]) + i
                        act_e.wait_ge(neg_max, head + 1)
                        A(pr[:, i, 0:P], pr[:, i, 0:P], ACT.Exp, bias=mx[:, head, 0:1],
                          accum_out=sums[:, head, 0:1])
                        A(pr[:, i, P:3 * P], pr[:, i, P:3 * P], ACT.Exp, bias=mx[:, head, 1:2],
                          accum_out=sums[:, head, 1:2]).then_inc(exp_ready, 1)
                elif s == "pvg":
                    for m in range(M):
                        i = SIDE[f"pvg{m}"][0]
                        act_e.wait_ge(side_done, i + 1)
                        if m:
                            act_e.wait_ge(gms_ready, m)
                        A(sq[:], side[:, i % 2, :], ACT.Square).then_inc(gss_sq, 1)
                    act_e.wait_ge(gms_ready, M + 1)
                    A(grs[:], gss[:], ACT.Sqrt).then_inc(groot, 1)
                elif s[:2] == "pv":
                    t, pair = TURN[s], int(s[2])
                    act_e.wait_ge(turn_done, t + 1)
                    A(oT_hi[:, pair, :], turn[:, t % 2, 0:T], ACT.Copy).then_inc(turn_hi, 1)
                elif s[:3] == "T_o":
                    t, a = TURN[s], int(s[3])
                    act_e.wait_ge(turn_done, t + 1)
                    A(hT_hi[:, 4 + 2 * a:6 + 2 * a, :], turn[:, t % 2, :].rearrange("p (c t) -> p c t", c=2), ACT.Copy).then_inc(turn_hi, 1)

            act_e.dma_start(ident[:], identity).then_inc(ident_in, 16)
            for k, g in enumerate([ffn1_norm, mix_norm, ffn2_norm, ple_norm]):
                act_e.dma_start(gain_rows[k * KC:(k + 1) * KC, :], g.rearrange("a (c p) -> (a c) p", p=P)
                                ).then_inc(gains_in, 16)
            act_e.dma_start(lrw[:], w_in.rearrange("(c p) f -> p c f", p=P)[:, :, LR_G:LR_G + LR]).then_inc(lrw_in, 16)
            act_e.dma_start(seg_f[:], seg_sums).then_inc(seg_in, 16)
            act_e.wait_ge(ident_in, 16)
            A(ident_r[:], ident[:], ACT.Copy).then_inc(idr_ready, 1)
            h_split(0, 0)
            squares(0, 0)
            h_turns(0, 0)
            for v in range(RING):
                split(v)
            act_e.wait_ge(lrw_in, 16)
            A(lrw_hi[:], lrw[:], ACT.Copy).then_inc(consts_hi, 1)
            act_e.wait_ge(seg_in, 16)
            A(seg[:], seg_f[:], ACT.Copy).then_inc(consts_hi, 1)
            ffn(0)
            for u in range(U_WIN, U_WOUT):
                if u == U_WIN:
                    h_split(1, 1)
                    h_turns(1, 1)
                    squares(1, 1)
                    root(1)
                for s in MIX.get(u, []):
                    step(s)
                split(u + RING)
            act_e.wait_ge(acc_read, 2 * B_WOUT)
            A(gg[:], gg[:], ACT.Silu).then_inc(gg_silu, 1)
            act_e.wait_ge(side_dve, SIDE["pvg1"][2])
            A(hT_hi[:, 0:4, :].rearrange("p c t -> p (c t)"), gg[:].rearrange("p m f -> p (m f)"), ACT.Copy).then_inc(og_hi_ready, 1)
            for v in range(4):
                if v == 3:
                    h_split(2, 0)
                    squares(2, 0)
                for s in MIX.get(U_WOUT + v, []):
                    step(s)
                split(U_WOUT + v + RING)
            h_turns(2, 0)
            ffn(1)
            h_split(3, 1)
            h_turns(3, 1)
            squares(3, 1)
            root(3)
            for v in range(U_PROJ, U_PROJ + 2):
                split(v + RING)
            for n in range(2):
                act_e.wait_ge(unit_done, U_GATE + 2 * n + 2)
                if n == 0:
                    act_e.wait_ge(rstd_ready, 4)
                for m in range(M):
                    if n:
                        act_e.wait_ge(h_final, m + 1)
                    A(gate[:, m, :], acc[:, 2 * ((B_GATE + n) % 2) + m, :], ACT.Sigmoid,
                      scale=rstd[:, 3, m:m + 1]).then_inc(gate_ready, 1)
                for m in range(M):
                    act_e.wait_ge(h_final, 2 * n + m + 1)
                    act_e.wait_ge(ssq_ready, 16 + 2 * n + m)
                    A(junk[:], h[:, m, n * N:(n + 1) * N], ACT.Square,
                      accum_out=ssq[:, 4, n, m:m + 1]).then_inc(ssq_ready, 1)
            root(4)

        @block.vector
        def _(dve):
            V = nc.vector
            steps = [0]

            def link(ins):
                steps[0] += 1
                ins.then_inc(dve_step, 1)
                dve.wait_ge(dve_step, steps[0])

            def split(v, slot=None):
                if isinstance(v, int):
                    if v >= UNITS:
                        return
                    slot, nk = v % RING, chunks_of(v)
                else:
                    nk = CH
                dve.wait_ge(hi_ready, v + 1)
                V.tensor_tensor(w_lo[:, slot, :nk * N], raw[:, slot, :nk * N],
                                w_hi[:, slot, :nk * N].bitcast(F32), ALU.subtract).then_inc(lo_ready, 1)

            def resid(s, n, coef):
                B = {1: B_DOWN[0], 2: B_WOUT, 3: B_DOWN[1]}[s] + n
                last = {1: U_DOWN[0] + 6 * n + 6, 2: U_WOUT + 3 + n, 3: U_DOWN[1] + 6 * n + 6}[s]
                dve.wait_ge(unit_done, last)
                for m in range(M):
                    c = slice(n * N, (n + 1) * N)
                    V.scalar_tensor_tensor(out=h[:, m, c], in0=acc[:, 2 * (B % 2) + m, :], scalar=coef,
                                           in1=h[:, m, c], op0=ALU.mult, op1=ALU.add).then_inc(acc_read, 1)

            def h_split(s, n):
                for m in range(M):
                    dve.wait_ge(hs_hi_ready, 2 * (2 * s + n) + m + 1)
                    V.tensor_tensor(hs_lo[:, m, :], h[:, m, n * N:(n + 1) * N], hs_hi[:, m, :].bitcast(F32),
                                    ALU.subtract).then_inc(hs_lo_ready, 1)

            def h_turns(s, n):
                for a in range(2):
                    t = TURN[f"h{s}.{n}"] + a
                    for c in range(2):
                        k = 4 * n + 2 * a + c
                        dve.wait_ge(turn_hi, hi_count[f"h{s}.{n}"] + 2 * a + 2)
                        ins = V.scalar_tensor_tensor(
                            out=hT_lo[:, k, :], in0=turn[:, t % 2, c * T:(c + 1) * T],
                            scalar=gains[:, s * KC + k:s * KC + k + 1], in1=hT_hi[:, k, :].bitcast(F32),
                            op0=ALU.mult, op1=ALU.subtract)
                    ins.then_inc(turn_read, 1)

            def rms(s):
                dve.wait_ge(ssq_ready, 4 * s + 4)
                link(V.tensor_tensor(rtmp[:, s, :], ssq[:, s, 0, :], ssq[:, s, 1, :], ALU.add))
                V.tensor_scalar(rtmp[:, s, :], rtmp[:, s, :], 1.0 / D, EPS, ALU.mult, ALU.add).then_inc(ms_ready, 1)
                dve.wait_ge(root_ready, s + 1)
                V.reciprocal(rstd[:, s, :], rtmp[:, s, :]).then_inc(rstd_ready, 1)
                dve.wait_ge(rstd_ready, s + 1)

            def act_turn(f, b, par):
                dve.wait_ge(turn_hi, b + (hi_count[f"act{f}"] + 1))
                r = bass.ds(b * 2, 2)
                V.tensor_tensor(a_loT[:, r, :], turn[:, (TURN[f"act{f}"] + par) % 2, :].rearrange("p (c t) -> p c t", c=2),
                                a_hiT[:, r, :].bitcast(F32), ALU.subtract).then_inc(turn_read, 1)

            def gated(f, b, par):
                for m in range(M):
                    dve.wait_ge(silu_ready, b * 2 + (2 * NB * f + m + 1))
                    V.scalar_tensor_tensor(out=act[:, m, :], in0=acc[:, 2 * ((B_GU[f] + par) % 2) + m, FB:N],
                                           scalar=rstd[:, 2 * f, m:m + 1], in1=silu_g[:, m, :],
                                           op0=ALU.mult, op1=ALU.mult).then_inc(acc_read, 1)
                for m in range(M):
                    dve.wait_ge(act_hi_ready, b * 2 + (2 * NB * f + m + 1))
                    V.tensor_tensor(act_lo[:, m, :], act[:, m, :], act_hi[:, m, :].bitcast(F32),
                                    ALU.subtract).then_inc(act_lo_ready, 1)

            def ffn(f):
                U = U_GU[f]

                def blk(b, j, i=None):
                    def sp_(k):
                        v = U + 2 * j + k + RING
                        split(v if i is None else i * 4 + v, v % RING)
                    if j == 0:
                        h_split(2 * f, 1)
                        h_turns(2 * f, 1)
                        rms(2 * f)
                    else:
                        act_turn(f, b - 1, (j - 1) % 2)
                    sp_(0)
                    gated(f, b, j % 2)
                    sp_(1)

                if f == 1:
                    resid(2, 1, 1.0)
                blk(0, 0)
                with dve.Fori(0, (NB - 1) // 2) as i:
                    for j in range(2):
                        blk(i * 2 + (1 + j), 1 + j, i)
                for n in range(2):
                    for k in range(6):
                        u = U_DOWN[f] + 6 * n + k
                        if n == 0 and k == 0:
                            act_turn(f, NB - 1, (NB - 1) % 2)
                        if f == 1 and n == 0 and k == 1:
                            dve.wait_ge(p_hi_ready, 1)
                            V.tensor_tensor(p_lo[:], p_nat[:], p_hi[:].bitcast(F32), ALU.subtract).then_inc(p_lo_ready, 1)
                        if f == 1 and n == 0 and k == 2:
                            dve.wait_ge(turn_hi, hi_count["p"] + 1)
                            V.tensor_tensor(pT_lo[:].rearrange("p c t -> p (c t)"), turn[:, TURN["p"] % 2, :],
                                            pT_hi[:].rearrange("p c t -> p (c t)").bitcast(F32),
                                            ALU.subtract).then_inc(turn_read, 1)
                        if n == 1 and k == 0:
                            resid(2 * f + 1, 0, 0.5)
                            h_split(2 * f + 1, 0)
                        if n == 1 and k == 1:
                            h_turns(2 * f + 1, 0)
                        split(u + RING)

            def nat(b, dst):
                B = B_WIN + b
                dve.wait_ge(unit_done, U_WIN + 2 * b + 2)
                for m in range(M):
                    ins = V.tensor_scalar(dst[:, m, :], acc[:, 2 * (B % 2) + m, :], rstd[:, 1, m:m + 1], None, ALU.mult)
                    ins.then_inc(acc_read, 1)

            def side_of(name):
                dve.wait_ge(side_done, SIDE[name][0] + 1)
                return side[:, SIDE[name][0] % 2, :]

            def make_z(lv):
                w = 1 << lv
                dve.wait_ge(side_act, SIDE["D7"][2])
                if lv == 7:
                    lower, upper = E[:, 0, :], E[:, 8, :]
                else:
                    lower = upper = E[:, lv + 1, :]
                dims = [[2 * w, T // w], [1, w]]
                V.tensor_tensor(view(lower, dims), view(lower, dims), view(k_gT[:], dims), ALU.mult)
                V.tensor_tensor(view(upper, dims, w), view(upper, dims, w), view(q_gT[:], dims, w), ALU.mult
                                ).then_inc(Z_ready, 1)

            def step(s):
                if s == "lr":
                    o = side_of(s)
                    link(V.memset(lrT[:], 1.0))
                    for m in range(M):
                        ins = V.tensor_scalar(lr_nat[:, m, :], o[:, m * LR:(m + 1) * LR], rstd[:, 1, m:m + 1],
                                              None, ALU.mult)
                    ins.then_inc(side_dve, 1)
                elif s == "lrT":
                    o = side_of(s)
                    V.tensor_copy(lrT[0:LR, :], o[0:LR, 0:T]).then_inc(side_dve, 1)
                elif s == "z":
                    o = side_of(s)
                    dve.wait_ge(z_abs, 1)
                    V.tensor_scalar(log_a[:], o, 0.0, 1.0 / TAU, ALU.min, ALU.mult).then_inc(side_dve, 1)
                    dve.wait_ge(side_dve, SIDE[s][2])
                    dve.wait_ge(lg_ready, 1)
                    V.scalar_tensor_tensor(out=log_a[:], in0=lg[:], scalar=-1.0 / TAU, in1=log_a[:],
                                           op0=ALU.mult, op1=ALU.add).then_inc(la_ready, 1)
                    dve.wait_ge(la_ready, 1)
                    dve.wait_ge(la_hi_ready, 1)
                    V.tensor_tensor(la_lo[:], log_a[:], la_hi[:].bitcast(F32), ALU.subtract).then_inc(la_lo_ready, 1)
                elif s[:3] == "T_q" or s[:3] == "T_k" or s[:3] == "T_g":
                    t, a = TURN[s], int(s[-1])
                    dve.wait_ge(turn_done, t + 1)
                    src = turn[:, t % 2, :]
                    if s[:3] == "T_q":
                        V.tensor_scalar(q_mT[:, 2 * a:2 * a + 2, :].rearrange("p c t -> p (c t)"), src,
                                        MD ** -0.5, None, ALU.mult).then_inc(turn_read, 1)
                    elif s[:3] == "T_k":
                        V.tensor_copy(k_mT[:, 2 * a:2 * a + 2, :].rearrange("p c t -> p (c t)"), src).then_inc(turn_read, 1)
                    elif a == 0:
                        V.tensor_scalar(q_gT[:], src, GDK ** -0.5, None, ALU.mult).then_inc(turn_read, 1)
                    else:
                        V.tensor_copy(k_gT[:], src).then_inc(turn_read, 1)
                        dve.wait_ge(turn_read, t + 1)
                        link(V.memset(AT[:], 0.0))
                elif s[:2] == "sc":
                    pair = int(s[2])
                    for i in range(2):
                        head = 2 * pair + i
                        o = side_of(f"{s}.{i}")
                        if head == 0:
                            dve.wait_ge(biasT_in, 16)
                        if pair:
                            dve.wait_ge(turn_done, TURN[f"pt{pair - 1}"] + i + 1)
                        V.tensor_tensor_reduce(pr[:, i, 0:P], o[:, 0:P], bias[:, head, P:T], 1.0, -3.0e38,
                                               ALU.add, ALU.max, mx[:, head, 0:1])
                        V.tensor_tensor_reduce(pr[:, i, P:3 * P], o[:, P:3 * P], bias[:, head, :], 1.0, -3.0e38,
                                               ALU.add, ALU.max, mx[:, head, 1:2]).then_inc(side_dve, 1)
                        dve.wait_ge(side_dve, SIDE[f"{s}.{i}"][2])
                        V.tensor_scalar(mx[:, head, :], mx[:, head, :], -1.0, None, ALU.mult).then_inc(neg_max, 1)
                    for i in range(2):
                        head = 2 * pair + i
                        dve.wait_ge(exp_ready, head + 1)
                        link(V.reciprocal(sums[:, head, :], sums[:, head, :]))
                        V.tensor_scalar(pr[:, i, 0:P], pr[:, i, 0:P], sums[:, head, 0:1], None, ALU.mult)
                        V.tensor_scalar(pr[:, i, P:3 * P], pr[:, i, P:3 * P], sums[:, head, 1:2], None,
                                        ALU.mult).then_inc(probs_ready, 1)
                elif s[:2] == "pt":
                    for i in range(2):
                        t = TURN[s] + i
                        dve.wait_ge(turn_done, t + 1)
                        if int(s[2]):
                            dve.wait_ge(turn_done, TURN[f"pv{int(s[2]) - 1}"] + 1)
                        V.tensor_copy(prT[:, i, :], turn[:, t % 2, 0:3 * P]).then_inc(turn_read, 1)
                elif s == "pvg":
                    for m in range(M):
                        dve.wait_ge(gss_sq, m + 1)
                        V.tensor_reduce(gss[:, m, :], sq[:].rearrange("p (g e) -> p g e", g=GH), AX, ALU.add
                                        ).then_inc(gms_ready, 1)
                    dve.wait_ge(gms_ready, M)
                    V.tensor_scalar(gss[:], gss[:], 1.0 / GDV, EPS, ALU.mult, ALU.add).then_inc(gms_ready, 1)
                    dve.wait_ge(groot, 1)
                    link(V.reciprocal(grs[:], grs[:]))
                elif s[:2] == "pv":
                    pair = int(s[2])
                    dve.wait_ge(turn_hi, hi_count[s] + 1)
                    V.tensor_tensor(oT_lo[:, pair, :], turn[:, TURN[s] % 2, 0:T], oT_hi[:, pair, :].bitcast(F32),
                                    ALU.subtract).then_inc(turn_read, 1)
                elif s == "diag":
                    dve.wait_ge(masks_in, 16)
                    for hh in range(2):
                        o = side_of(f"diag.{hh}")
                        V.copy_predicated(AT[:, 4 * hh:4 * hh + 4, :], view(masks[:, 7 * 64:], [[0, 4], [1, P]]),
                                          o.rearrange("p (b i) -> p b i", b=4)).then_inc(side_dve, 1)
                    dve.wait_ge(side_dve, SIDE["diag.1"][2])
                elif s[:2] == "lv":
                    for hh in range(2):
                        o = side_of(f"{s}.{hh}")
                        for a in range(2):
                            lv = 2 * int(s[2]) + a
                            w = 1 << lv
                            n = 64 // w if lv < 7 else 0
                            if lv == 7:
                                ins = V.tensor_copy(AT2[:, 2 * hh:2 * hh + 2, :].rearrange("p g i -> p (g i)"), o[:, T:])
                            else:
                                ins = V.copy_predicated(view(AT[:, 4 * hh, :], [[P, 4], [2 * w, n], [1, w]], w),
                                                        view(masks[:, lv * 64:], [[0, 4], [w, n], [1, w]]),
                                                        view(o[:, a * T:], [[64, 4], [w, n], [1, w]]))
                            if a == 0:
                                link(ins)
                        ins.then_inc(side_dve, 1)
                    dve.wait_ge(side_dve, SIDE[f"{s}.1"][2])
                elif s[:3] == "T_o":
                    t, a = TURN[s], int(s[3])
                    dve.wait_ge(turn_hi, hi_count[s] + 1)
                    V.tensor_tensor(hT_lo[:, 4 + 2 * a:6 + 2 * a, :], turn[:, t % 2, :].rearrange("p (c t) -> p c t", c=2),
                                    hT_hi[:, 4 + 2 * a:6 + 2 * a, :].bitcast(F32), ALU.subtract).then_inc(turn_read, 1)

            hi_count, n = {}, 0
            for name in sorted(TURN, key=lambda k: TURN[k]):
                hi_count[name] = n
                if name[0] == "h":
                    n += 4
                elif name[:3] == "act":
                    n += NB
                elif name == "p" or name[:2] == "pv" or name[:3] == "T_o":
                    n += 1

            o = side_of("gain")
            V.tensor_copy(gains[:], o[:, 0:4 * KC]).then_inc(side_dve, 1)
            dve.wait_ge(side_dve, SIDE["gain"][2])
            h_split(0, 0)
            h_turns(0, 0)
            for v in range(RING):
                split(v)
            o = side_of("bias_row")
            V.tensor_tensor(bias_row[:], o[0:MH, 0:BIAS_W], causal[:], ALU.add).then_inc(side_dve, 1)
            dve.wait_ge(consts_hi, 1)
            V.tensor_tensor(lrw_lo[:], lrw[:], lrw_hi[:].bitcast(F32), ALU.subtract).then_inc(consts_lo, 1)
            ffn(0)
            resid(1, 1, 0.5)
            dsts = [nat0, nat1, nat0, nat1, vg, gg]
            for u in range(U_WIN, U_WOUT):
                if u == U_WIN:
                    h_split(1, 1)
                    h_turns(1, 1)
                    rms(1)
                elif (u - U_WIN) % 2 == 1:
                    nat((u - U_WIN) // 2, dsts[(u - U_WIN) // 2])
                for s in MIX.get(u, []):
                    step(s)
                for lv in Z_AT.get(u, []):
                    make_z(lv)
                split(u + RING)
            dve.wait_ge(gg_silu, 1)
            link(V.tensor_tensor(gg[:].rearrange("p m (g e) -> p (m g) e", g=GH),
                                 gg[:].rearrange("p m (g e) -> p (m g) e", g=GH),
                                 view(gout[:], [[0, M * GH], [1, GDV]]), ALU.mult))
            for m in range(M):
                i = SIDE[f"pvg{m}"][0]
                for hd in range(GH):
                    c = slice(hd * GDV, (hd + 1) * GDV)
                    ins = V.scalar_tensor_tensor(out=gg[:, m, c], in0=side[:, i % 2, c], scalar=grs[:, m, hd:hd + 1],
                                                 in1=gg[:, m, c], op0=ALU.mult, op1=ALU.mult)
                ins.then_inc(side_dve, 1)
            dve.wait_ge(og_hi_ready, 1)
            V.tensor_tensor(hT_lo[:, 0:4, :].rearrange("p c t -> p (c t)"), gg[:].rearrange("p m f -> p (m f)"),
                            hT_hi[:, 0:4, :].rearrange("p c t -> p (c t)").bitcast(F32), ALU.subtract
                            ).then_inc(og_lo_ready, 1)
            for v in range(4):
                if v == 3:
                    resid(2, 0, 1.0)
                    h_split(2, 0)
                for s in MIX.get(U_WOUT + v, []):
                    step(s)
                split(U_WOUT + v + RING)
            h_turns(2, 0)
            ffn(1)
            resid(3, 1, 0.5)
            h_split(3, 1)
            h_turns(3, 1)
            rms(3)
            for n in range(2):
                B = B_PROJ + n
                dve.wait_ge(unit_done, U_PROJ + n + 1)
                for m in range(M):
                    V.tensor_copy(pp[:, m, n * N:(n + 1) * N], acc[:, 2 * (B % 2) + m, :]).then_inc(acc_read, 1)
                split(U_PROJ + n + RING)
            dve.wait_ge(acc_read, 2 * B_GATE)
            for n in range(2):
                c = slice(n * N, (n + 1) * N)
                for m in range(M):
                    dve.wait_ge(gate_ready, 2 * n + m + 1)
                    V.tensor_tensor(gate[:, m, :], gate[:, m, :], pp[:, m, c], ALU.mult).then_inc(acc_read, 1)
                    dve.wait_ge(acc_read, 2 * (B_GATE + n) + m + 1)
                    V.tensor_tensor(h[:, m, c], h[:, m, c], gate[:, m, :], ALU.add).then_inc(h_final, 1)
            rms(4)
            dve.wait_ge(h_final, 4)
            for m in range(M):
                V.scalar_tensor_tensor(out=res[:, m, :], in0=h[:, m, :], scalar=rstd[:, 4, m:m + 1], in1=fgain[:],
                                       op0=ALU.mult, op1=ALU.mult).then_inc(res_ready, 1)


_INS = ["x", "p", "ffn1_norm", "ffn1_w_gu", "ffn1_w_down", "mix_norm", "w_in", "w_gk_up", "b_gk", "gla_out_norm",
        "w_out", "ffn2_norm", "ffn2_w_gu", "ffn2_w_down", "ple_norm", "w_ple_gate", "w_ple_proj", "rel_bias",
        "final_norm"]


def constants():
    import math
    import numpy as np

    t = np.arange(P)
    seg = np.zeros((P, 9, P), np.float32)
    for lv in range(7):
        w = 1 << lv
        mid = t // (2 * w) * 2 * w + w
        upper = (t[:, None] >= mid) & (t[:, None] <= t)
        lower = (t[:, None] > t) & (t[:, None] < mid)
        seg[:, lv + 1] = np.where(t >= mid, upper, lower)
    seg[:, 0] = t[:, None] > t
    seg[:, 8] = t[:, None] <= t
    masks = np.zeros((P, 7 * 64 + P), np.int32)
    q = np.arange(64)
    for lv in range(7):
        w = 1 << lv
        i = q // w * 2 * w + w + q % w
        masks[:, lv * 64:(lv + 1) * 64] = (t[:, None] // (2 * w) == i // (2 * w)) & (t[:, None] % (2 * w) < w)
    masks[:, 7 * 64:] = np.eye(P, dtype=np.int32)
    dist = np.arange(T)
    nf = np.maximum(dist, 1).astype(np.float32)
    exact = BUCKETS // 2
    large = exact + (np.log(nf / np.float32(exact)) / np.float32(math.log(4096 / exact))
                     * np.float32(BUCKETS - exact)).astype(np.int32)
    bucket = np.where(dist < exact, dist, np.minimum(large, BUCKETS - 1))
    rows = np.zeros((BUCKETS, BIAS_W), np.float32)
    rows[bucket, T - 1 - dist] = 1.0
    causal = np.zeros((MH, BIAS_W), np.float32)
    causal[:, T:] = -1e30
    return {"identity": np.eye(P, dtype=np.float32), "seg_sums": seg.reshape(P, 9 * P), "pair_masks": masks,
            "bucket_rows": rows, "causal_row": causal}


def kernel(**inputs):
    import numpy as _np
    import concourse.bacc as _bacc
    from concourse import mybir as _mybir
    from concourse.bass_utils import run_bass_kernel_spmd as _run

    nc = _bacc.Bacc("TRN2", target_bir_lowering=False, num_devices=1)
    arrays, args = {}, []
    given = {name: _np.ascontiguousarray(inputs[name]) for name in _INS} | constants()
    for name, a in given.items():
        arrays[f"in_{name}"] = a
        args.append(nc.dram_tensor(f"in_{name}", a.shape, _mybir.dt.from_np(a.dtype), kind="ExternalInput").ap())
    args.append(nc.dram_tensor("out_0", (1, T, D), _mybir.dt.float32, kind="ExternalOutput").ap())
    build(nc, *args)
    r = _run(nc, [arrays], core_ids=[0])
    return r.results[0]["out_0"]
```

```python
from contextlib import ExitStack

import concourse.bass as bass
from concourse import mybir

F32 = mybir.dt.float32
F32R = mybir.dt.float32r
I32 = mybir.dt.int32
ALU = mybir.AluOpType
ACT = mybir.ActivationFunctionType
AX = mybir.AxisListType.X

P = 128
T = 256
M = T // P
D = 1024
KC = D // P
F = 2816
FC = F // P
FB = 256
NB = F // FB
N = 512
RING = 4
CH = 4
EPS = 1e-6
PLE = 256

GH, GDK, GDV = 4, 64, 128
LR = 16
MH, MD = 8, 64
BUCKETS = 32
BIAS_W = 384
TAU = 16.0

QK_G, V_G, G_G, LR_G, Q_M, K_M, V_M = 0, 512, 1024, 1536, 1552, 2064, 2576
WIN_BLOCKS = [("q_m", Q_M), ("k_m", K_M), ("qk_g", QK_G), ("v_m", V_M), ("v_g", V_G), ("g_g", G_G)]

DOWN_CH = [4, 4, 4, 4, 4, 2]
U_GU = [0, 50]
U_DOWN = [22, 72]
U_WIN = 34
U_WOUT = 46
U_PROJ = 84
U_GATE = 86
UNITS = 90
B_GU = [0, 21]
B_DOWN = [11, 32]
B_WIN = 13
B_WOUT = 19
B_PROJ = 34
B_GATE = 36
B_H = {1: 11, 2: 19, 3: 32}

MIX = {
    35: ["lr"],
    36: ["z", "T_q_m0", "T_q_m1"],
    38: ["T_k_m0", "T_k_m1", "D0", "D1", "D2", "D3"],
    39: ["D4", "D5", "D6", "D7", "sc0"],
    40: ["T_g0", "T_g1", "pt0", "sc1"],
    41: ["diag", "lv0"],
    42: ["pv0", "pt1", "sc2", "lv1"],
    43: ["pv1", "pt2", "sc3", "lv2"],
    44: ["pv2", "pt3", "lv3"],
    45: ["pv3", "pvg"],
    47: ["T_o0", "T_o1"],
}
Z_AT = {40: [0, 1], 41: [2, 3], 42: [4, 5], 43: [6, 7]}


def chunks_of(u):
    for d in U_DOWN:
        if d <= u < d + 12:
            return DOWN_CH[(u - d) % 6]
    return 2 if U_PROJ <= u < U_GATE else CH


def plan_turns():
    at, n = {}, 0

    def add(name, k=1):
        nonlocal n
        at[name] = n
        n += k

    add("h0.0", 2)
    add("h0.1", 2)
    add("act0", NB)
    add("h1.0", 2)
    add("h1.1", 2)
    for u in sorted(MIX):
        for s in MIX[u]:
            if s[:2] == "T_":
                add(s)
            elif s[:2] == "pt":
                add(s, 2)
            elif s[:2] == "pv" and s != "pvg":
                add(s)
    add("h2.0", 2)
    add("h2.1", 2)
    add("act1", NB)
    add("p")
    add("h3.0", 2)
    add("h3.1", 2)
    return at


def plan_side():
    uses = [("gain0", "dve"), ("gain", "dve"), ("bias_row", "dve")]
    for u in sorted(MIX):
        for s in MIX[u]:
            if s[0] == "D":
                uses.append((s, "act"))
            elif s[:2] == "sc":
                uses += [(f"{s}.{i}", "dve") for i in range(2)]
            elif s == "diag" or s[:2] == "lv":
                uses += [(f"{s}.{hh}", "dve") for hh in range(2)]
            elif s == "pvg":
                uses += [("pvg0", "dve"), ("pvg1", "dve")]
            elif s in ("lr", "z"):
                uses.append((s, "dve"))
    count, out = {"dve": 0, "act": 0}, {}
    for i, (name, who) in enumerate(uses):
        count[who] += 1
        out[name] = (i, who, count[who])
    return out


TURN = plan_turns()
SIDE = plan_side()
SIDE_AT = {i: (who, c) for i, who, c in SIDE.values()}


def view(ap, dims, offset=0):
    return bass.AP(tensor=ap.tensor, offset=ap.offset + offset, ap=[list(ap.ap[0])] + [list(d) for d in dims])


def build(nc, x, p, ffn1_norm, ffn1_w_gu, ffn1_w_down, mix_norm, w_in, w_gk_up, b_gk, gla_out_norm,
          w_out, ffn2_norm, ffn2_w_gu, ffn2_w_down, ple_norm, w_ple_gate, w_ple_proj, rel_bias,
          final_norm, identity, seg_sums, pair_masks, bucket_rows, causal_row, out):
    x, out, w_gk_up, w_in, w_out = x[0], out[0], w_gk_up[0], w_in[0], w_out[0]
    p, w_ple_gate, w_ple_proj = p[0][0], w_ple_gate[0], w_ple_proj[0]
    ffn1_w_gu, ffn1_w_down, ffn2_w_gu, ffn2_w_down = ffn1_w_gu[0], ffn1_w_down[0], ffn2_w_gu[0], ffn2_w_down[0]
    ctx = ExitStack()
    with ctx:
        def sem(name):
            return ctx.enter_context(nc.semaphore(name))

        base = (nc.sbuf_base + 63) // 64 * 64
        top = [base]

        def sb(name, shape, dt=F32):
            size = 4
            for s in shape[1:]:
                size *= s
            t = nc.alloc_sbuf_tensor_at(name, shape, dt, offset=top[0])
            top[0] += (size + 31) // 32 * 32
            return t

        raw = sb("raw", [P, RING, CH * N])
        w_hi = sb("w_hi", [P, RING, CH * N], F32R)
        w_lo = sb("w_lo", [P, RING, CH * N], F32R)
        h = sb("h", [P, M, D])
        hT_hi = sb("hT_hi", [P, KC, T], F32R)
        hT_lo = sb("hT_lo", [P, KC, T], F32R)
        ident = sb("ident", [P, P])
        gains = sb("gains", [P, 4 * KC])
        lrw_pad = sb("lrw_pad", [P, KC, P], F32R)
        gk_up = sb("gk_up", [3 * LR, GH * GDK])
        b_row = sb("b_row", [P, GH * GDK])
        gout = sb("gout", [P, GDV])
        ssq = sb("ssq", [P, 5, 2, M])
        rstd = sb("rstd", [P, 5, M])
        rtmp = sb("rtmp", [P, 5, M])
        mx = sb("mx", [P, MH, M])
        sums = sb("sums", [P, MH, M])
        gss = sb("gss", [P, M, GH])
        grs = sb("grs", [P, M, GH])
        spare = sb("spare", [P, 4])
        junk = sb("junk", [P, N], mybir.dt.bfloat16)
        region = top[0]

        def at(name, kib, shape, dt=F32):
            size = 4
            for s in shape[1:]:
                size *= s
            assert region + int(kib * 1024) + size <= nc.sbuf_usable_end, name
            return nc.alloc_sbuf_tensor_at(name, shape, dt, offset=region + int(kib * 1024))

        a_hiT = at("a_hiT", 0, [P, FC, T], F32R)
        a_loT = at("a_loT", 22, [P, FC, T], F32R)
        silu_g = at("silu_g", 44, [P, M, FB])
        act = at("act", 46, [P, M, FB])
        gain_rows0 = at("gain_rows0", 55, [KC, P])
        gain_rows = at("gain_rows", 56, [3 * KC, P])
        rel = at("rel", 57, [BUCKETS, MH])
        rows = at("rows", 58, [BUCKETS, BIAS_W])
        causal = at("causal", 60, [MH, BIAS_W])
        bias_row = at("bias_row", 62, [MH, BIAS_W])
        lrw = at("lrw", 64, [P, KC, LR])
        seg_f = at("seg_f", 65, [P, 9 * P])
        E = at("E", 0, [P, 9, 2 * T])
        nat0 = at("nat0", 18, [P, M, N])
        nat1 = at("nat1", 22, [P, M, N])
        q_mT = at("q_mT", 26, [P, MH // 2, T])
        k_mT = at("k_mT", 30, [P, MH // 2, T])
        bias = at("bias", 34, [P, MH, T])
        q_gT = at("q_gT", 42, [P, 2 * T])
        k_gT = at("k_gT", 44, [P, 2 * T])
        gg = at("gg", 42, [P, M, N])
        lg = at("lg", 46, [P, M * T])
        log_a = at("log_a", 48, [P, M * T])
        vg = at("vg", 46, [P, M, N])
        lrT = at("lrT", 50, [3 * LR, T])
        sq = at("sq", 50, [P, N])
        la_hi = at("la_hi", 56, [P, M * T], F32R)
        la_lo = at("la_lo", 58, [P, M * T], F32R)
        AT = at("AT", 18, [P, 2 * GH, P])
        AT2 = at("AT2", 56, [P, GH, P])
        pr = at("pr", 58, [P, 2, 3 * P])
        prT = at("prT", 61, [P, 2, 3 * P])
        oT_hi = at("oT_hi", 64, [P, MH // 2, T], F32R)
        oT_lo = at("oT_lo", 68, [P, MH // 2, T], F32R)
        seg = at("seg", 72, [P, 9 * P], F32R)
        masks = at("masks", 52, [P, 7 * 64 + P], I32)
        p_nat = at("p_nat", 56, [P, M, PLE])
        pT_hi = at("pT_hi", 62, [P, 2, T], F32R)
        pT_lo = at("pT_lo", 64, [P, 2, T], F32R)
        pp = at("pp", 12, [P, M, D])
        fgain = at("fgain", 66, [P, D])
        gate = at("gate", 0, [P, M, N])
        res = at("res", 4, [P, M, D])

        acc = ctx.enter_context(nc.psum_tensor("acc", [P, 4, N], F32))
        turn = ctx.enter_context(nc.psum_tensor("turn", [P, 2, N], F32))
        side = ctx.enter_context(nc.psum_tensor("side", [P, 2, N], F32))

        row_dram = nc.dram_tensor("bias_row_dram", [MH, BIAS_W], F32).ap()
        skew_dram = nc.dram_tensor("bias_skew_dram", [P, MH, BIAS_W], F32).ap()

        x_in = [sem(f"x_in{n}") for n in range(2)]
        ident_in = sem("ident_in")
        gain0_in = sem("gain0_in")
        gains_in = sem("gains_in")
        lrw_in = sem("lrw_in")
        seg_in = sem("seg_in")
        small_in = sem("small_in")
        masks_in = sem("masks_in")
        bias_in = sem("bias_in")
        row_out = sem("row_out")
        skew_out = sem("skew_out")
        biasT_in = sem("biasT_in")
        ple_in = sem("ple_in")
        raw_in = [sem(f"raw_in{s}") for s in range(RING)]
        hi_ready = sem("hi_ready")
        lo_ready = sem("lo_ready")
        unit_done = sem("unit_done")
        acc_read = sem("acc_read")
        turn_done = sem("turn_done")
        turn_hi = sem("turn_hi")
        turn_read = sem("turn_read")
        side_done = sem("side_done")
        side_dve = sem("side_dve")
        side_act = sem("side_act")
        ssq_ready = sem("ssq_ready")
        ms_ready = sem("ms_ready")
        root_ready = sem("root_ready")
        rstd_ready = sem("rstd_ready")
        silu_ready = sem("silu_ready")
        zeroed = sem("zeroed")
        consts_hi = sem("consts_hi")
        consts_lo = sem("consts_lo")
        z_abs = sem("z_abs")
        lg_ready = sem("lg_ready")
        la_ready = sem("la_ready")
        la_hi_ready = sem("la_hi_ready")
        la_lo_ready = sem("la_lo_ready")
        Z_ready = sem("Z_ready")
        neg_max = sem("neg_max")
        exp_ready = sem("exp_ready")
        probs_ready = sem("probs_ready")
        gss_sq = sem("gss_sq")
        gms_ready = sem("gms_ready")
        groot = sem("groot")
        gg_silu = sem("gg_silu")
        gate_ready = sem("gate_ready")
        spare_set = sem("spare_set")
        last_tile = sem("last_tile")
        h_final = sem("h_final")
        half_in = sem("half_in")
        half_hi = sem("half_hi")
        half_lo = sem("half_lo")
        res_ready = sem("res_ready")
        res_out = sem("res_out")
        dve_step = sem("dve_step")
        act_step = sem("act_step")

        block = ctx.enter_context(nc.Block())

        GU_W = [ffn1_w_gu, ffn2_w_gu]
        DOWN_W = [ffn1_w_down, ffn2_w_down]

        @block.sync
        def _(sp):
            def free(u):
                if not isinstance(u, int) or u >= RING:
                    sp.wait_ge(lo_ready, u - (RING - 1))

            def gu_unit(f, b, kh, u, slot):
                free(u)
                w = GU_W[f].rearrange("(c p) f -> p c f", p=P)
                dst = raw[:, slot, :].rearrange("p (k g f) -> p k g f", k=CH, g=2)
                for g in range(2):
                    sp.dma_start(dst[:, :, g, :], w[:, CH * kh:CH * kh + CH, bass.ds(g * F + b * FB, FB)]
                                 ).then_inc(raw_in[slot], 16)

            def unit(w, c0, col, u):
                free(u)
                nk = chunks_of(u)
                slot = u % RING
                wv = w.rearrange("(c p) f -> p c f", p=P)
                dst = raw[:, slot, :nk * N].rearrange("p (k f) -> p k f", k=nk)
                for a in range(2):
                    r = slice(a * nk // 2, (a + 1) * nk // 2)
                    sp.dma_start(dst[:, r, :], wv[:, c0 + r.start:c0 + r.stop, col:col + N]
                                 ).then_inc(raw_in[slot], 16)

            def ffn(f):
                first = 3
                for b in range(first):
                    for kh in range(2):
                        u = U_GU[f] + 2 * b + kh
                        if u >= 2:
                            gu_unit(f, b, kh, u, u % RING)
                with sp.Fori(0, (NB - first) // 2) as i:
                    for j in range(2):
                        for kh in range(2):
                            u = U_GU[f] + 2 * (first + j) + kh
                            gu_unit(f, i * 2 + (first + j), kh, i * 4 + u, u % RING)
                for n in range(2):
                    for k in range(6):
                        unit(DOWN_W[f], CH * k, n * N, U_DOWN[f] + 6 * n + k)

            xv = x.rearrange("(m p) d -> p m d", p=P)
            w = ffn1_w_gu.rearrange("(c p) f -> p c f", p=P)
            dst = raw[:, 0, :].rearrange("p (k g f) -> p k g f", k=CH, g=2)
            for n, arrived in ((0, half_in), (1, raw_in[0])):
                sp.dma_start(h[:, :, n * N:(n + 1) * N], xv[:, :, n * N:(n + 1) * N]).then_inc(x_in[n], 16)
                for g in range(2):
                    sp.dma_start(dst[:, 2 * n:2 * n + 2, g, :], w[:, 2 * n:2 * n + 2, g * F:g * F + FB]
                                 ).then_inc(arrived, 16)
            gu_unit(0, 0, 1, 1, 1)
            ffn(0)
            for b, (_, col) in enumerate(WIN_BLOCKS):
                for kh in range(2):
                    unit(w_in, CH * kh, col, U_WIN + 2 * b + kh)
            for v, (n, kh) in enumerate([(0, 1), (1, 1), (0, 0), (1, 0)]):
                unit(w_out, CH * kh, n * N, U_WOUT + v)
            ffn(1)
            for n in range(2):
                unit(w_ple_proj, 0, n * N, U_PROJ + n)
            for n in range(2):
                for kh in range(2):
                    unit(w_ple_gate, CH * kh, n * N, U_GATE + 2 * n + kh)
            ov = out.rearrange("(m p) d -> p m d", p=P)
            for m in range(M):
                sp.wait_ge(res_ready, m + 1)
                sp.dma_start(ov[:, m, :], res[:, m, :]).then_inc(res_out, 16)
            sp.wait_ge(res_out, 16 * M)

        @block.gpsimd
        def _(pool):
            nc.gpsimd.memset(lrw_pad[:].bitcast(F32), 0.0).then_inc(zeroed, 1)
            nc.gpsimd.memset(gk_up[:], 0.0).then_inc(zeroed, 1)
            pool.dma_start(lrw[:], w_in.rearrange("(c p) f -> p c f", p=P)[:, :, LR_G:LR_G + LR]).then_inc(lrw_in, 16)
            pool.dma_start(seg_f[:], seg_sums).then_inc(seg_in, 16)
            for k, g in enumerate([mix_norm, ffn2_norm, ple_norm]):
                pool.dma_start(gain_rows[k * KC:(k + 1) * KC, :], g.rearrange("a (c p) -> (a c) p", p=P)
                               ).then_inc(gains_in, 16)
            pool.dma_start(rel[:], rel_bias).then_inc(bias_in, 16)
            pool.dma_start(rows[:], bucket_rows).then_inc(bias_in, 16)
            pool.dma_start(causal[:], causal_row).then_inc(bias_in, 16)
            pool.wait_ge(zeroed, 2)
            pool.dma_start(gk_up[0:LR, :], w_gk_up).then_inc(small_in, 16)
            pool.dma_start(gk_up[2 * LR:3 * LR, :], w_gk_up).then_inc(small_in, 16)
            pool.dma_start(b_row[:], bass.AP(tensor=b_gk.tensor, offset=0, ap=[[0, P], [1, GH * GDK]])
                           ).then_inc(small_in, 16)
            pool.dma_start(gout[:], bass.AP(tensor=gla_out_norm.tensor, offset=0, ap=[[0, P], [1, GDV]])).then_inc(small_in, 16)
            pool.wait_ge(side_dve, SIDE["bias_row"][2])
            pool.dma_start(row_dram, bias_row[:]).then_inc(row_out, 16)
            pool.wait_ge(row_out, 16)
            pool.dma_start(skew_dram, bass.AP(tensor=row_dram.tensor, offset=0,
                                              ap=[[0, P], [BIAS_W, MH], [1, BIAS_W]])).then_inc(skew_out, 16)
            pool.wait_ge(skew_out, 16)
            pool.wait_ge(unit_done, U_WIN)
            pool.dma_start(bias[:], bass.AP(tensor=skew_dram.tensor, offset=P - 1,
                                            ap=[[MH * BIAS_W - 1, P], [BIAS_W, MH], [1, T]])).then_inc(biasT_in, 16)
            pool.dma_start(masks[:], pair_masks).then_inc(masks_in, 16)
            pool.wait_ge(unit_done, U_GU[1])
            pool.dma_start(p_nat[:], p.rearrange("(m p) e -> p m e", p=P)).then_inc(ple_in, 16)
            pool.dma_start(fgain[:], bass.AP(tensor=final_norm.tensor, offset=0, ap=[[0, P], [1, D]])).then_inc(ple_in, 16)

        @block.tensor
        def _(pe):
            def mm(o, lhsT, rhs, start, stop):
                return nc.tensor.matmul(o, lhsT, rhs, start=start, stop=stop, skip_group_check=True)

            def exact3(o, l_hi, l_lo, r_hi, r_lo, start, stop):
                mm(o, l_hi, r_hi, start, False)
                mm(o, l_hi, r_lo, False, False)
                return mm(o, l_lo, r_hi, False, stop)

            def unit(u, slot, pair, lhs, k0, nk, first, last, part=None):
                if isinstance(u, int) and u == 0:
                    pe.wait_ge(lo_ready if part else half_lo, 1)
                elif part in (None, 0):
                    pe.wait_ge(lo_ready, u + 1)
                ks = range(nk) if part is None else range(part * nk // 2, (part + 1) * nk // 2)
                for k in ks:
                    for m in range(M):
                        l_hi, l_lo = lhs(k0 + k, m)
                        ins = exact3(acc[:, 2 * pair + m, :], l_hi, l_lo,
                                     w_hi[:, slot, k * N:(k + 1) * N], w_lo[:, slot, k * N:(k + 1) * N],
                                     first and k == 0, last and k == nk - 1)
                if part in (None, 1):
                    ins.then_inc(unit_done, 1)

            def acc_free(B):
                if not isinstance(B, int) or B >= 2:
                    pe.wait_ge(acc_read, (B - 1) * 2)

            def from_hT(c, m):
                return hT_hi[:, c, m * P:(m + 1) * P], hT_lo[:, c, m * P:(m + 1) * P]

            def from_aT(c, m):
                return a_hiT[:, c, m * P:(m + 1) * P], a_loT[:, c, m * P:(m + 1) * P]

            def turn_open(t):
                if not isinstance(t, int) or t >= 2:
                    pe.wait_ge(turn_read, t - 1)

            def flip(o, src, k=P):
                return nc.tensor.transpose(o, src, ident[:k, :k])

            def h_turns(s, n):
                if s == 0:
                    pe.wait_ge(x_in[n], 16)
                else:
                    pe.wait_ge(acc_read, 2 * (B_H[s] + n) + 2)
                for a in range(2):
                    t = TURN[f"h{s}.{n}"] + a
                    turn_open(t)
                    for c in range(2):
                        for m in range(M):
                            k = 4 * n + 2 * a + c
                            ins = flip(turn[:, t % 2, (2 * c + m) * P:(2 * c + m + 1) * P], h[:, m, k * P:(k + 1) * P])
                    ins.then_inc(turn_done, 1)

            def h_ready(s, n):
                pe.wait_ge(turn_read, TURN[f"h{s}.{n}"] + 2)

            def act_turn(f, b, par):
                pe.wait_ge(acc_read, (b + B_GU[f]) * 2 + 2)
                t = b + TURN[f"act{f}"]
                turn_open(t)
                for c in range(2):
                    for m in range(M):
                        ins = flip(turn[:, (TURN[f"act{f}"] + par) % 2, (2 * c + m) * P:(2 * c + m + 1) * P],
                                   act[:, m, c * P:(c + 1) * P])
                ins.then_inc(turn_done, 1)

            def gu_block(f, b, par, s0, first=False):
                pair = (B_GU[f] + par) % 2
                acc_free(b + B_GU[f])
                u = b * 2 + U_GU[f]
                if first:
                    s = 2 * f
                    if f == 0:
                        h_turns(s, 1)
                        pe.wait_ge(turn_read, 1)
                        unit(u, s0, pair, from_hT, 0, CH, True, False, part=0)
                        h_ready(s, 0)
                    else:
                        h_ready(s, 0)
                        unit(u, s0, pair, from_hT, 0, CH, True, False, part=0)
                        h_turns(s, 1)
                    unit(u, s0, pair, from_hT, 0, CH, True, False, part=1)
                    h_ready(s, 1)
                else:
                    unit(u, s0, pair, from_hT, 0, CH, True, False)
                    act_turn(f, b - 1, 1 - par)
                unit(u + 1, (s0 + 1) % RING, pair, from_hT, CH, CH, False, True)

            def ffn(f):
                gu_block(f, 0, 0, U_GU[f] % RING, first=True)
                with pe.Fori(0, (NB - 1) // 2) as i:
                    for j in range(2):
                        gu_block(f, i * 2 + (1 + j), (1 + j) % 2, (U_GU[f] + 2 + 2 * j) % RING)
                for n in range(2):
                    B = B_DOWN[f] + n
                    acc_free(B)
                    for k in range(6):
                        u = U_DOWN[f] + 6 * n + k
                        if n == 0:
                            pe.wait_ge(turn_read, TURN[f"act{f}"] + min(2 * k + 2, NB))
                        unit(u, u % RING, B % 2, from_aT, CH * k, DOWN_CH[k], k == 0, k == 5)
                        if n == 0 and k == 0:
                            act_turn(f, NB - 1, (NB - 1) % 2)
                        if f == 1 and n == 0 and k == 2:
                            p_turn()
                        if n == 1 and k == 1:
                            h_turns(2 * f + 1, 0)
                        if f == 0 and n == 0 and k == 1:
                            o = side_open("gain")
                            pe.wait_ge(gains_in, 48)
                            flip(o[:, 0:3 * KC], gain_rows[:], 3 * KC).then_inc(side_done, 1)
                            o = side_open("bias_row")
                            pe.wait_ge(bias_in, 48)
                            mm(o[0:MH, 0:BIAS_W], rel[:], rows[:], True, True).then_inc(side_done, 1)

            def p_turn():
                pe.wait_ge(ple_in, 32)
                nat_turn("p", p_nat, 0)

            def side_open(name):
                i = SIDE[name][0]
                if i >= 2:
                    who, count = SIDE_AT[i - 2]
                    pe.wait_ge(side_dve if who == "dve" else side_act, count)
                return side[:, i % 2, :]

            def nat_turn(name, src, cols):
                t = TURN[name]
                turn_open(t)
                for c in range(2):
                    for m in range(M):
                        ins = flip(turn[:, t % 2, (2 * c + m) * P:(2 * c + m + 1) * P],
                                   src[:, m, cols + c * P:cols + (c + 1) * P])
                ins.then_inc(turn_done, 1)

            def step(s):
                if s == "lr":
                    o = side_open(s)
                    pe.wait_ge(consts_lo, 1)
                    for c in range(KC):
                        mm(o[:, 0:T], lrw_pad[:, c, :], hT_hi[:, c, :], c == 0, False)
                        ins = mm(o[:, 0:T], lrw_pad[:, c, :], hT_lo[:, c, :], False, c == KC - 1)
                    ins.then_inc(side_done, 1)
                elif s == "z":
                    o = side_open(s)
                    pe.wait_ge(side_dve, SIDE["lr"][2])
                    pe.wait_ge(small_in, 64)
                    for m in range(M):
                        ins = mm(o[:, m * T:(m + 1) * T], lrT[:, m * P:(m + 1) * P], gk_up[:], True, True)
                    ins.then_inc(side_done, 1)
                elif s in ("T_q_m0", "T_q_m1"):
                    pe.wait_ge(acc_read, 2 * B_WIN + 2)
                    nat_turn(s, nat0, 2 * P * int(s[-1]))
                elif s in ("T_k_m0", "T_k_m1"):
                    pe.wait_ge(acc_read, 2 * B_WIN + 4)
                    nat_turn(s, nat1, 2 * P * int(s[-1]))
                elif s in ("T_g0", "T_g1"):
                    pe.wait_ge(acc_read, 2 * B_WIN + 6)
                    nat_turn(s, nat0, 2 * P * int(s[-1]))
                elif s[0] == "D":
                    d = int(s[1])
                    m, hp, half = d // 4, d // 2 % 2, d % 2
                    o = side_open(s)
                    pe.wait_ge(la_lo_ready, 1)
                    lhs = slice(m * T + hp * P, m * T + (hp + 1) * P)
                    r = seg[:, (m + 4 * half) * P:(m + 4 * half + 4) * P]
                    mm(o, la_hi[:, lhs], r, True, False)
                    mm(o, la_lo[:, lhs], r, False, True).then_inc(side_done, 1)
                elif s[:2] == "sc":
                    for i in range(2):
                        head = 2 * int(s[2]) + i
                        o = side_open(f"{s}.{i}")
                        pe.wait_ge(turn_read, TURN["T_k_m1"] + 1)
                        lo = 64 * (head % 2)
                        q, k = q_mT[lo:lo + 64, head // 2, :], k_mT[lo:lo + 64, head // 2, :]
                        mm(o[:, 0:P], q[:, 0:P], k[:, 0:P], True, True)
                        mm(o[:, P:3 * P], q[:, P:T], k[:, :], True, True).then_inc(side_done, 1)
                elif s[:2] == "pt":
                    pair = int(s[2])
                    for i in range(2):
                        t = TURN[s] + i
                        pe.wait_ge(probs_ready, 2 * pair + i + 1)
                        turn_open(t)
                        for k in range(3):
                            ins = flip(turn[:, t % 2, k * P:(k + 1) * P], pr[:, i, k * P:(k + 1) * P])
                        ins.then_inc(turn_done, 1)
                elif s == "pvg":
                    for m in range(M):
                        o = side_open(f"pvg{m}")
                        pe.wait_ge(acc_read, 2 * B_WIN + 10)
                        pe.wait_ge(side_dve, SIDE["lv3.1"][2])
                        for hd in range(GH):
                            c = slice(hd * GDV, (hd + 1) * GDV)
                            hh, hp = hd % 2, hd // 2
                            ins = mm(o[:, c], AT[:, 4 * hh + 2 * hp + m, :], vg[:, m, c], True, m == 0)
                            if m == 1:
                                ins = mm(o[:, c], AT2[:, 2 * hh + hp, :], vg[:, 0, c], False, True)
                        ins.then_inc(side_done, 1)
                elif s[:2] == "pv":
                    pair = int(s[2])
                    t = TURN[s]
                    pe.wait_ge(turn_read, TURN[f"pt{pair}"] + 2)
                    pe.wait_ge(acc_read, 2 * B_WIN + 8)
                    turn_open(t)
                    for i in range(2):
                        c = slice((2 * pair + i) * MD, (2 * pair + i + 1) * MD)
                        o = turn[64 * i:64 * i + 64, t % 2, 0:T]
                        mm(o, nat1[:, 0, c], prT[:, i, 0:T], True, False)
                        ins = mm(o[:, P:T], nat1[:, 1, c], prT[:, i, T:T + P], False, True)
                    ins.then_inc(turn_done, 1)
                elif s == "diag":
                    for hh in range(2):
                        o = side_open(f"diag.{hh}")
                        pe.wait_ge(turn_read, TURN["T_g1"] + 1)
                        r = slice(64 * hh, 64 * hh + 64)
                        for k in range(4):
                            c = slice(k * P, (k + 1) * P)
                            ins = mm(o[:, c], k_gT[r, c], q_gT[r, c], True, True)
                        ins.then_inc(side_done, 1)
                elif s[:2] == "lv":
                    for hh in range(2):
                        o = side_open(f"{s}.{hh}")
                        r = slice(64 * hh, 64 * hh + 64)
                        pe.wait_ge(Z_ready, 2 * int(s[2]) + 2)
                        for a in range(2):
                            lv = 2 * int(s[2]) + a
                            w = 1 << lv
                            if lv == 7:
                                for hp in range(2):
                                    c = hp * T
                                    ins = mm(o[:, T + hp * P:T + (hp + 1) * P], E[r, 0, c:c + P], E[r, 8, c + P:c + T],
                                             True, True)
                            else:
                                for k in range(4):
                                    z = E[r, lv + 1, k * P:(k + 1) * P]
                                    ins = mm(o[:, a * T + k * 64:a * T + (k + 1) * 64], z,
                                             view(z, [[2 * w, 64 // w], [1, w]], w), True, True)
                        ins.then_inc(side_done, 1)
                elif s[:3] == "T_o":
                    a = int(s[3])
                    t = TURN[s]
                    pe.wait_ge(side_dve, SIDE["pvg1"][2])
                    turn_open(t)
                    for c in range(2):
                        for m in range(M):
                            ins = flip(turn[:, t % 2, (2 * c + m) * P:(2 * c + m + 1) * P],
                                       gg[:, m, (2 * a + c) * P:(2 * a + c + 1) * P])
                    ins.then_inc(turn_done, 1)

            def from_oT(c, m):
                r = slice(m * P, (m + 1) * P)
                if c < 4:
                    return hT_hi[:, 4 + c, r], hT_lo[:, 4 + c, r]
                return oT_hi[:, c - 4, r], oT_lo[:, c - 4, r]

            pe.wait_ge(ident_in, 16)
            h_turns(0, 0)
            pe.wait_ge(gain0_in, 16)
            o = side_open("gain0")
            flip(o[:, 0:KC], gain_rows0[:], KC).then_inc(side_done, 1)
            ffn(0)
            for b in range(len(WIN_BLOCKS)):
                B = B_WIN + b
                for kh in range(2):
                    u = U_WIN + 2 * b + kh
                    if kh == 0:
                        acc_free(B)
                    if u == U_WIN:
                        h_ready(1, 0)
                    unit(u, u % RING, B % 2, from_hT, CH * kh, CH, kh == 0, kh == 1, part=0)
                    if u == U_WIN:
                        h_turns(1, 1)
                    for s in MIX.get(u, []):
                        step(s)
                    unit(u, u % RING, B % 2, from_hT, CH * kh, CH, kh == 0, kh == 1, part=1)
                    if u == U_WIN:
                        h_ready(1, 1)
            for v, (n, kh) in enumerate([(0, 1), (1, 1), (0, 0), (1, 0)]):
                u, B = U_WOUT + v, B_WOUT + n
                if kh == 1:
                    acc_free(B)
                pe.wait_ge(turn_read, TURN["pv3"] + 1 if kh == 1 else TURN["T_o1"] + 1)
                unit(u, u % RING, B % 2, from_oT, CH * kh, CH, kh == 1, kh == 0, part=0)
                if v == 3:
                    h_turns(2, 0)
                for s in MIX.get(u, []):
                    step(s)
                unit(u, u % RING, B % 2, from_oT, CH * kh, CH, kh == 1, kh == 0, part=1)
            ffn(1)
            for n in range(2):
                u, B = U_PROJ + n, B_PROJ + n
                acc_free(B)
                pe.wait_ge(turn_read, TURN["p"] + 1)
                unit(u, u % RING, B % 2,
                     lambda c, m: (pT_hi[:, c, m * P:(m + 1) * P], pT_lo[:, c, m * P:(m + 1) * P]), 0, 2, True, True)
                if n == 0:
                    h_turns(3, 1)
            h_ready(3, 1)
            acc_free(B_GATE)
            for kh in range(2):
                u = U_GATE + kh
                unit(u, u % RING, B_GATE % 2, from_hT, CH * kh, CH, kh == 0, kh == 1)
            acc_free(B_GATE + 1)
            for m in range(M):
                for c in range(KC):
                    u, k = U_GATE + 2 + c // CH, c % CH
                    if m == 0 and k == 0:
                        pe.wait_ge(lo_ready, u + 1)
                    l_hi, l_lo = from_hT(c, m)
                    ins = exact3(acc[:, 2 * ((B_GATE + 1) % 2) + m, :], l_hi, l_lo,
                                 w_hi[:, u % RING, k * N:(k + 1) * N], w_lo[:, u % RING, k * N:(k + 1) * N],
                                 c == 0, c == KC - 1)
                ins.then_inc(last_tile, 1)

        @block.scalar
        def _(act_e):
            A = nc.scalar.activation

            def split(v, slot=None, turn_of_slot=None):
                if isinstance(v, int):
                    if v >= UNITS:
                        return
                    slot, turn_of_slot, nk = v % RING, v // RING, chunks_of(v)
                else:
                    nk = CH
                act_e.wait_ge(raw_in[slot], turn_of_slot * 32 + 32)
                if not isinstance(v, int) or v >= RING:
                    act_e.wait_ge(unit_done, v - (RING - 1))
                A(w_hi[:, slot, :nk * N], raw[:, slot, :nk * N], ACT.Copy).then_inc(hi_ready, 1)

            def squares(s, n):
                if s == 0:
                    act_e.wait_ge(x_in[n], 16)
                else:
                    act_e.wait_ge(acc_read, 2 * (B_H[s] + n) + 2)
                for m in range(M):
                    if 4 * s + 2 * n + m:
                        act_e.wait_ge(ssq_ready, 4 * s + 2 * n + m)
                    A(junk[:], h[:, m, n * N:(n + 1) * N], ACT.Square,
                      accum_out=ssq[:, s, n, m:m + 1]).then_inc(ssq_ready, 1)

            def h_turns(s, n):
                for a in range(2):
                    t = TURN[f"h{s}.{n}"] + a
                    act_e.wait_ge(turn_done, t + 1)
                    for c in range(2):
                        k = 4 * n + 2 * a + c
                        if n == 0 and a == 0 and c == 0:
                            act_e.wait_ge(side_dve, SIDE["gain" if s else "gain0"][2])
                        A(hT_hi[:, k, :], turn[:, t % 2, c * T:(c + 1) * T], ACT.Copy,
                          scale=gains[:, s * KC + k:s * KC + k + 1]).then_inc(turn_hi, 1)

            def root(s):
                act_e.wait_ge(ms_ready, s + 1)
                A(rtmp[:, s, :], rtmp[:, s, :], ACT.Sqrt).then_inc(root_ready, 1)

            def act_turn(f, b, par):
                t = b + TURN[f"act{f}"]
                act_e.wait_ge(turn_done, t + 1)
                dst = a_hiT[:, bass.ds(b * 2, 2), :]
                A(dst, turn[:, (TURN[f"act{f}"] + par) % 2, :].rearrange("p (c t) -> p c t", c=2), ACT.Copy).then_inc(turn_hi, 1)

            def gated(f, b, par):
                B = b + B_GU[f]
                for m in range(M):
                    if m == 0:
                        act_e.wait_ge(unit_done, b * 2 + (U_GU[f] + 2))
                        if isinstance(b, int) and b == 0:
                            act_e.wait_ge(rstd_ready, 2 * f + 1)
                        if not (isinstance(b, int) and B == 0):
                            act_e.wait_ge(acc_read, B * 2)
                    A(silu_g[:, m, :], acc[:, 2 * ((B_GU[f] + par) % 2) + m, 0:FB], ACT.Silu,
                      scale=rstd[:, 2 * f, m:m + 1]).then_inc(silu_ready, 1)

            def ffn(f):
                U = U_GU[f]

                def blk(b, j, i=None):
                    def sp_(k):
                        v = U + 2 * j + k + RING
                        if i is None:
                            split(v)
                        else:
                            split(i * 4 + v, v % RING, i + v // RING)
                    if j == 0:
                        if f == 1:
                            squares(2, 1)
                            h_turns(2, 1)
                            root(2)
                            sp_(0)
                    else:
                        act_turn(f, b - 1, (j - 1) % 2)
                        sp_(0)
                    gated(f, b, j % 2)
                    if f == 0 and j == 0:
                        sp_(0)
                    sp_(1)

                blk(0, 0)
                with act_e.Fori(0, (NB - 1) // 2) as i:
                    for j in range(2):
                        blk(i * 2 + (1 + j), 1 + j, i)
                for n in range(2):
                    for k in range(6):
                        u = U_DOWN[f] + 6 * n + k
                        if n == 0 and k == 0:
                            act_turn(f, NB - 1, (NB - 1) % 2)
                        if f == 1 and n == 0 and k == 2:
                            t = TURN["p"]
                            act_e.wait_ge(turn_done, t + 1)
                            A(pT_hi[:], turn[:, t % 2, :].rearrange("p (c t) -> p c t", c=2), ACT.Copy).then_inc(turn_hi, 1)
                        if f == 0 and n == 0 and k == 2:
                            act_e.wait_ge(lrw_in, 16)
                            act_e.wait_ge(zeroed, 2)
                            A(lrw_pad[:, :, 0:LR], lrw[:], ACT.Copy).then_inc(consts_hi, 1)
                            act_e.wait_ge(seg_in, 16)
                            A(seg[:], seg_f[:], ACT.Copy).then_inc(consts_hi, 1)
                        if n == 1 and k == 0:
                            squares(2 * f + 1, 0)
                        if n == 1 and k == 1:
                            h_turns(2 * f + 1, 0)
                        split(u + RING)

            def step(s):
                if s == "z":
                    act_e.wait_ge(side_dve, SIDE[s][2])
                    A(lg[:], log_a[:], ACT.Abs).then_inc(z_abs, 1)
                    act_e.wait_ge(z_abs, 1)
                    A(lg[:], lg[:], ACT.Exp, scale=-1.0).then_inc(act_step, 1)
                    act_e.wait_ge(act_step, 1)
                    A(lg[:], lg[:], ACT.Ln, bias=1.0).then_inc(lg_ready, 1)
                    act_e.wait_ge(la_ready, 1)
                    A(la_hi[:], log_a[:], ACT.Copy).then_inc(la_hi_ready, 1)
                elif s[0] == "D":
                    d = int(s[1])
                    m, hp, half = d // 4, d // 2 % 2, d % 2
                    act_e.wait_ge(side_done, SIDE[s][0] + 1)
                    k = m + 4 * half
                    A(E[:, k:k + 4, hp * T + m * P:hp * T + (m + 1) * P], side[:, SIDE[s][0] % 2, :].rearrange("p (l t) -> p l t", l=4), ACT.Exp
                      ).then_inc(side_act, 1)
                elif s[:2] == "sc":
                    for i in range(2):
                        head = 2 * int(s[2]) + i
                        act_e.wait_ge(neg_max, head + 1)
                        A(pr[:, i, 0:P], pr[:, i, 0:P], ACT.Exp, bias=mx[:, head, 0:1],
                          accum_out=sums[:, head, 0:1])
                        A(pr[:, i, P:3 * P], pr[:, i, P:3 * P], ACT.Exp, bias=mx[:, head, 1:2],
                          accum_out=sums[:, head, 1:2]).then_inc(exp_ready, 1)
                elif s == "pvg":
                    for m in range(M):
                        i = SIDE[f"pvg{m}"][0]
                        act_e.wait_ge(side_done, i + 1)
                        if m:
                            act_e.wait_ge(gms_ready, m)
                        A(sq[:], side[:, i % 2, :], ACT.Square).then_inc(gss_sq, 1)
                    act_e.wait_ge(gms_ready, M + 1)
                    A(grs[:], gss[:], ACT.Sqrt).then_inc(groot, 1)
                elif s[:2] == "pv":
                    t, pair = TURN[s], int(s[2])
                    act_e.wait_ge(turn_done, t + 1)
                    A(oT_hi[:, pair, :], turn[:, t % 2, 0:T], ACT.Copy).then_inc(turn_hi, 1)
                elif s[:3] == "T_o":
                    t, a = TURN[s], int(s[3])
                    act_e.wait_ge(turn_done, t + 1)
                    A(hT_hi[:, 4 + 2 * a:6 + 2 * a, :], turn[:, t % 2, :].rearrange("p (c t) -> p c t", c=2), ACT.Copy).then_inc(turn_hi, 1)

            act_e.dma_start(ident[:], identity).then_inc(ident_in, 16)
            act_e.dma_start(gain_rows0[:], ffn1_norm.rearrange("a (c p) -> (a c) p", p=P)).then_inc(gain0_in, 16)
            act_e.wait_ge(spare_set, 1)
            A(spare[:, 0:1], spare[:, 1:2], ACT.Silu)
            half = CH * N // 2
            act_e.wait_ge(half_in, 32)
            A(w_hi[:, 0, :half], raw[:, 0, :half], ACT.Copy).then_inc(half_hi, 1)
            h_turns(0, 0)
            act_e.wait_ge(raw_in[0], 32)
            A(w_hi[:, 0, half:], raw[:, 0, half:], ACT.Copy).then_inc(hi_ready, 1)
            h_turns(0, 1)
            split(1)
            split(2)
            squares(0, 0)
            squares(0, 1)
            root(0)
            split(3)
            ffn(0)
            for u in range(U_WIN, U_WOUT):
                if u == U_WIN:
                    squares(1, 1)
                    h_turns(1, 1)
                    root(1)
                for s in MIX.get(u, []):
                    step(s)
                split(u + RING)
            act_e.wait_ge(acc_read, 2 * B_WOUT)
            A(gg[:], gg[:], ACT.Silu).then_inc(gg_silu, 1)
            for v in range(4):
                if v == 3:
                    squares(2, 0)
                    h_turns(2, 0)
                for s in MIX.get(U_WOUT + v, []):
                    step(s)
                split(U_WOUT + v + RING)
            ffn(1)
            squares(3, 1)
            h_turns(3, 1)
            for v in range(U_PROJ, U_PROJ + 2):
                split(v + RING)
            root(3)

            def sigmoid(n, m):
                k = 2 * n + m
                if n:
                    act_e.wait_ge(h_final, m + 1)
                A(gate[:, m, :], acc[:, 2 * ((B_GATE + n) % 2) + m, :], ACT.Sigmoid,
                  scale=rstd[:, 3, m:m + 1]).then_inc(gate_ready, 1)

            def last_squares(n, m):
                k = 2 * n + m
                act_e.wait_ge(h_final, k + 1)
                act_e.wait_ge(ssq_ready, 16 + k)
                A(junk[:], h[:, m, n * N:(n + 1) * N], ACT.Square, accum_out=ssq[:, 4, n, m:m + 1]).then_inc(ssq_ready, 1)

            act_e.wait_ge(spare_set, 1)
            act_e.wait_ge(rstd_ready, 4)
            act_e.wait_ge(unit_done, U_GATE + 2)
            for m in range(M):
                sigmoid(0, m)
            for m in range(M):
                last_squares(0, m)
            for m in range(M):
                act_e.wait_ge(last_tile, m + 1)
                sigmoid(1, m)
                A(spare[:, 0:1], spare[:, 1:2], ACT.Sqrt)
                last_squares(1, m)
                act_e.wait_ge(ms_ready, 5 + m)
                A(rtmp[:, 4, m:m + 1], rtmp[:, 4, m:m + 1], ACT.Sqrt).then_inc(root_ready, 1)
                if m == 0:
                    A(spare[:, 2:3], spare[:, 1:2], ACT.Sigmoid)

        @block.vector
        def _(dve):
            V = nc.vector
            steps = [0]

            def link(ins):
                steps[0] += 1
                ins.then_inc(dve_step, 1)
                dve.wait_ge(dve_step, steps[0])

            def split(v, slot=None):
                if isinstance(v, int):
                    if v >= UNITS:
                        return
                    slot, nk = v % RING, chunks_of(v)
                else:
                    nk = CH
                dve.wait_ge(hi_ready, v + 1)
                V.tensor_tensor(w_lo[:, slot, :nk * N], raw[:, slot, :nk * N],
                                w_hi[:, slot, :nk * N].bitcast(F32), ALU.subtract).then_inc(lo_ready, 1)

            def resid(s, n, coef):
                B = B_H[s] + n
                last = {1: U_DOWN[0] + 6 * n + 6, 2: U_WOUT + 3 + n, 3: U_DOWN[1] + 6 * n + 6}[s]
                dve.wait_ge(unit_done, last)
                for m in range(M):
                    c = slice(n * N, (n + 1) * N)
                    V.scalar_tensor_tensor(out=h[:, m, c], in0=acc[:, 2 * (B % 2) + m, :], scalar=coef,
                                           in1=h[:, m, c], op0=ALU.mult, op1=ALU.add).then_inc(acc_read, 1)

            def h_turns(s, n):
                for a in range(2):
                    t = TURN[f"h{s}.{n}"] + a
                    for c in range(2):
                        k = 4 * n + 2 * a + c
                        dve.wait_ge(turn_hi, hi_count[f"h{s}.{n}"] + 2 * a + 2)
                        ins = V.scalar_tensor_tensor(
                            out=hT_lo[:, k, :], in0=turn[:, t % 2, c * T:(c + 1) * T],
                            scalar=gains[:, s * KC + k:s * KC + k + 1], in1=hT_hi[:, k, :].bitcast(F32),
                            op0=ALU.mult, op1=ALU.subtract)
                    ins.then_inc(turn_read, 1)

            def rms(s):
                dve.wait_ge(ssq_ready, 4 * s + 4)
                link(V.tensor_tensor(rtmp[:, s, :], ssq[:, s, 0, :], ssq[:, s, 1, :], ALU.add))
                V.tensor_scalar(rtmp[:, s, :], rtmp[:, s, :], 1.0 / D, EPS, ALU.mult, ALU.add).then_inc(ms_ready, 1)
                dve.wait_ge(root_ready, s + 1)
                V.reciprocal(rstd[:, s, :], rtmp[:, s, :]).then_inc(rstd_ready, 1)
                dve.wait_ge(rstd_ready, s + 1)

            def act_turn(f, b, par):
                dve.wait_ge(turn_hi, b + (hi_count[f"act{f}"] + 1))
                r = bass.ds(b * 2, 2)
                V.tensor_tensor(a_loT[:, r, :], turn[:, (TURN[f"act{f}"] + par) % 2, :].rearrange("p (c t) -> p c t", c=2),
                                a_hiT[:, r, :].bitcast(F32), ALU.subtract).then_inc(turn_read, 1)

            def gated(f, b, par):
                for m in range(M):
                    dve.wait_ge(silu_ready, b * 2 + (2 * NB * f + m + 1))
                    V.scalar_tensor_tensor(out=act[:, m, :], in0=acc[:, 2 * ((B_GU[f] + par) % 2) + m, FB:N],
                                           scalar=rstd[:, 2 * f, m:m + 1], in1=silu_g[:, m, :],
                                           op0=ALU.mult, op1=ALU.mult).then_inc(acc_read, 1)

            def ffn(f):
                U = U_GU[f]

                def blk(b, j, i=None):
                    def sp_(k):
                        v = U + 2 * j + k + RING
                        split(v if i is None else i * 4 + v, v % RING)
                    if j == 0:
                        if f == 1:
                            resid(2, 1, 1.0)
                            split(U + 3)
                            h_turns(2, 1)
                            rms(2)
                            sp_(0)
                    else:
                        act_turn(f, b - 1, (j - 1) % 2)
                        sp_(0)
                    gated(f, b, j % 2)
                    if f == 0 and j == 0:
                        sp_(0)
                    sp_(1)

                blk(0, 0)
                with dve.Fori(0, (NB - 1) // 2) as i:
                    for j in range(2):
                        blk(i * 2 + (1 + j), 1 + j, i)
                for n in range(2):
                    for k in range(6):
                        u = U_DOWN[f] + 6 * n + k
                        if n == 0 and k == 0:
                            act_turn(f, NB - 1, (NB - 1) % 2)
                        if f == 0 and n == 0 and k == 2:
                            o = side_of("gain")
                            V.tensor_copy(gains[:, KC:], o[:, 0:3 * KC]).then_inc(side_dve, 1)
                            dve.wait_ge(side_dve, SIDE["gain"][2])
                            o = side_of("bias_row")
                            V.tensor_tensor(bias_row[:], o[0:MH, 0:BIAS_W], causal[:], ALU.add).then_inc(side_dve, 1)
                            dve.wait_ge(consts_hi, 1)
                            V.tensor_tensor(lrw_pad[:, :, 2 * LR:3 * LR], lrw[:], lrw_pad[:, :, 0:LR].bitcast(F32),
                                            ALU.subtract).then_inc(consts_lo, 1)
                        if f == 1 and n == 0 and k == 2:
                            dve.wait_ge(turn_hi, hi_count["p"] + 1)
                            V.tensor_tensor(pT_lo[:].rearrange("p c t -> p (c t)"), turn[:, TURN["p"] % 2, :],
                                            pT_hi[:].rearrange("p c t -> p (c t)").bitcast(F32),
                                            ALU.subtract).then_inc(turn_read, 1)
                        if n == 1 and k == 0:
                            resid(2 * f + 1, 0, 0.5)
                        if n == 1 and k == 1:
                            h_turns(2 * f + 1, 0)
                        if n == 0 or k < 4:
                            split(u + RING)
                resid(2 * f + 1, 1, 0.5)
                split(U_DOWN[f] + 10 + RING)
                h_turns(2 * f + 1, 1)
                if f == 0:
                    split(U_DOWN[f] + 11 + RING)

            def nat(b, dst):
                B = B_WIN + b
                dve.wait_ge(unit_done, U_WIN + 2 * b + 2)
                for m in range(M):
                    ins = V.tensor_scalar(dst[:, m, :], acc[:, 2 * (B % 2) + m, :], rstd[:, 1, m:m + 1], None, ALU.mult)
                    ins.then_inc(acc_read, 1)

            def side_of(name):
                dve.wait_ge(side_done, SIDE[name][0] + 1)
                return side[:, SIDE[name][0] % 2, :]

            def make_z(lv):
                w = 1 << lv
                dve.wait_ge(side_act, SIDE["D7"][2])
                if lv == 7:
                    lower, upper = E[:, 0, :], E[:, 8, :]
                else:
                    lower = upper = E[:, lv + 1, :]
                dims = [[2 * w, T // w], [1, w]]
                V.tensor_tensor(view(lower, dims), view(lower, dims), view(k_gT[:], dims), ALU.mult)
                V.tensor_tensor(view(upper, dims, w), view(upper, dims, w), view(q_gT[:], dims, w), ALU.mult
                                ).then_inc(Z_ready, 1)

            def step(s):
                if s == "lr":
                    o = side_of(s)
                    V.tensor_copy(lrT[:], o[0:3 * LR, 0:T]).then_inc(side_dve, 1)
                elif s == "z":
                    o = side_of(s)
                    for m in range(M):
                        c = slice(m * T, (m + 1) * T)
                        ins = V.scalar_tensor_tensor(out=log_a[:, c], in0=o[:, c], scalar=rstd[:, 1, m:m + 1],
                                                     in1=b_row[:], op0=ALU.mult, op1=ALU.add)
                        if m == 0:
                            link(ins)
                    ins.then_inc(side_dve, 1)
                    dve.wait_ge(side_dve, SIDE[s][2])
                    dve.wait_ge(z_abs, 1)
                    link(V.tensor_scalar(log_a[:], log_a[:], 0.0, 1.0 / TAU, ALU.min, ALU.mult))
                    dve.wait_ge(lg_ready, 1)
                    V.scalar_tensor_tensor(out=log_a[:], in0=lg[:], scalar=-1.0 / TAU, in1=log_a[:],
                                           op0=ALU.mult, op1=ALU.add).then_inc(la_ready, 1)
                    dve.wait_ge(la_ready, 1)
                    dve.wait_ge(la_hi_ready, 1)
                    V.tensor_tensor(la_lo[:], log_a[:], la_hi[:].bitcast(F32), ALU.subtract).then_inc(la_lo_ready, 1)
                elif s[:3] == "T_q" or s[:3] == "T_k" or s[:3] == "T_g":
                    t, a = TURN[s], int(s[-1])
                    dve.wait_ge(turn_done, t + 1)
                    src = turn[:, t % 2, :]
                    if s[:3] == "T_q":
                        V.tensor_scalar(q_mT[:, 2 * a:2 * a + 2, :].rearrange("p c t -> p (c t)"), src,
                                        MD ** -0.5, None, ALU.mult).then_inc(turn_read, 1)
                    elif s[:3] == "T_k":
                        V.tensor_copy(k_mT[:, 2 * a:2 * a + 2, :].rearrange("p c t -> p (c t)"), src).then_inc(turn_read, 1)
                    elif a == 0:
                        V.tensor_scalar(q_gT[:], src, GDK ** -0.5, None, ALU.mult).then_inc(turn_read, 1)
                    else:
                        V.tensor_copy(k_gT[:], src).then_inc(turn_read, 1)
                        dve.wait_ge(turn_read, t + 1)
                        link(V.memset(AT[:], 0.0))
                elif s[:2] == "sc":
                    pair = int(s[2])
                    for i in range(2):
                        head = 2 * pair + i
                        o = side_of(f"{s}.{i}")
                        if head == 0:
                            dve.wait_ge(biasT_in, 16)
                        if pair:
                            dve.wait_ge(turn_done, TURN[f"pt{pair - 1}"] + i + 1)
                        V.tensor_tensor_reduce(pr[:, i, 0:P], o[:, 0:P], bias[:, head, P:T], 1.0, -3.0e38,
                                               ALU.add, ALU.max, mx[:, head, 0:1])
                        V.tensor_tensor_reduce(pr[:, i, P:3 * P], o[:, P:3 * P], bias[:, head, :], 1.0, -3.0e38,
                                               ALU.add, ALU.max, mx[:, head, 1:2]).then_inc(side_dve, 1)
                        dve.wait_ge(side_dve, SIDE[f"{s}.{i}"][2])
                        V.tensor_scalar(mx[:, head, :], mx[:, head, :], -1.0, None, ALU.mult).then_inc(neg_max, 1)
                    for i in range(2):
                        head = 2 * pair + i
                        dve.wait_ge(exp_ready, head + 1)
                        link(V.reciprocal(sums[:, head, :], sums[:, head, :]))
                        V.tensor_scalar(pr[:, i, 0:P], pr[:, i, 0:P], sums[:, head, 0:1], None, ALU.mult)
                        V.tensor_scalar(pr[:, i, P:3 * P], pr[:, i, P:3 * P], sums[:, head, 1:2], None,
                                        ALU.mult).then_inc(probs_ready, 1)
                elif s[:2] == "pt":
                    for i in range(2):
                        t = TURN[s] + i
                        dve.wait_ge(turn_done, t + 1)
                        if int(s[2]):
                            dve.wait_ge(turn_done, TURN[f"pv{int(s[2]) - 1}"] + 1)
                        V.tensor_copy(prT[:, i, :], turn[:, t % 2, 0:3 * P]).then_inc(turn_read, 1)
                elif s == "pvg":
                    for m in range(M):
                        dve.wait_ge(gss_sq, m + 1)
                        V.tensor_reduce(gss[:, m, :], sq[:].rearrange("p (g e) -> p g e", g=GH), AX, ALU.add
                                        ).then_inc(gms_ready, 1)
                    dve.wait_ge(gms_ready, M)
                    V.tensor_scalar(gss[:], gss[:], 1.0 / GDV, EPS, ALU.mult, ALU.add).then_inc(gms_ready, 1)
                    dve.wait_ge(groot, 1)
                    link(V.reciprocal(grs[:], grs[:]))
                elif s[:2] == "pv":
                    pair = int(s[2])
                    dve.wait_ge(turn_hi, hi_count[s] + 1)
                    V.tensor_tensor(oT_lo[:, pair, :], turn[:, TURN[s] % 2, 0:T], oT_hi[:, pair, :].bitcast(F32),
                                    ALU.subtract).then_inc(turn_read, 1)
                elif s == "diag":
                    dve.wait_ge(masks_in, 16)
                    for hh in range(2):
                        o = side_of(f"diag.{hh}")
                        V.copy_predicated(AT[:, 4 * hh:4 * hh + 4, :], view(masks[:, 7 * 64:], [[0, 4], [1, P]]),
                                          o.rearrange("p (b i) -> p b i", b=4)).then_inc(side_dve, 1)
                    dve.wait_ge(side_dve, SIDE["diag.1"][2])
                elif s[:2] == "lv":
                    for hh in range(2):
                        o = side_of(f"{s}.{hh}")
                        for a in range(2):
                            lv = 2 * int(s[2]) + a
                            w = 1 << lv
                            n = 64 // w if lv < 7 else 0
                            if lv == 7:
                                ins = V.tensor_copy(AT2[:, 2 * hh:2 * hh + 2, :].rearrange("p g i -> p (g i)"), o[:, T:])
                            else:
                                ins = V.copy_predicated(view(AT[:, 4 * hh, :], [[P, 4], [2 * w, n], [1, w]], w),
                                                        view(masks[:, lv * 64:], [[0, 4], [w, n], [1, w]]),
                                                        view(o[:, a * T:], [[64, 4], [w, n], [1, w]]))
                            if a == 0:
                                link(ins)
                        ins.then_inc(side_dve, 1)
                    dve.wait_ge(side_dve, SIDE[f"{s}.1"][2])
                elif s[:3] == "T_o":
                    t, a = TURN[s], int(s[3])
                    dve.wait_ge(turn_hi, hi_count[s] + 1)
                    V.tensor_tensor(hT_lo[:, 4 + 2 * a:6 + 2 * a, :], turn[:, t % 2, :].rearrange("p (c t) -> p c t", c=2),
                                    hT_hi[:, 4 + 2 * a:6 + 2 * a, :].bitcast(F32), ALU.subtract).then_inc(turn_read, 1)

            hi_count, n = {}, 0
            for name in sorted(TURN, key=lambda k: TURN[k]):
                hi_count[name] = n
                if name[0] == "h":
                    n += 4
                elif name[:3] == "act":
                    n += NB
                elif name == "p" or name[:2] == "pv" or name[:3] == "T_o":
                    n += 1

            V.memset(spare[:], 1.0).then_inc(spare_set, 1)
            o = side_of("gain0")
            V.tensor_copy(gains[:, 0:KC], o[:, 0:KC]).then_inc(side_dve, 1)
            dve.wait_ge(side_dve, SIDE["gain0"][2])
            half = CH * N // 2
            for ready, done, c in ((half_hi, half_lo, slice(0, half)), (hi_ready, lo_ready, slice(half, None))):
                dve.wait_ge(ready, 1)
                V.tensor_tensor(w_lo[:, 0, c], raw[:, 0, c], w_hi[:, 0, c].bitcast(F32), ALU.subtract).then_inc(done, 1)
                if done is half_lo:
                    h_turns(0, 0)
            h_turns(0, 1)
            split(1)
            split(2)
            rms(0)
            split(3)
            ffn(0)
            dsts = [nat0, nat1, nat0, nat1, vg, gg]
            for u in range(U_WIN, U_WOUT):
                if u == U_WIN:
                    rms(1)
                for s in MIX.get(u, []):
                    step(s)
                if (u - U_WIN) % 2 == 1:
                    nat((u - U_WIN) // 2, dsts[(u - U_WIN) // 2])
                for lv in Z_AT.get(u, []):
                    make_z(lv)
                split(u + RING)
            dve.wait_ge(gg_silu, 1)
            link(V.tensor_tensor(gg[:].rearrange("p m (g e) -> p (m g) e", g=GH),
                                 gg[:].rearrange("p m (g e) -> p (m g) e", g=GH),
                                 view(gout[:], [[0, M * GH], [1, GDV]]), ALU.mult))
            for m in range(M):
                i = SIDE[f"pvg{m}"][0]
                for hd in range(GH):
                    c = slice(hd * GDV, (hd + 1) * GDV)
                    ins = V.scalar_tensor_tensor(out=gg[:, m, c], in0=side[:, i % 2, c], scalar=grs[:, m, hd:hd + 1],
                                                 in1=gg[:, m, c], op0=ALU.mult, op1=ALU.mult)
                ins.then_inc(side_dve, 1)
            for v in range(4):
                if v == 3:
                    resid(2, 0, 1.0)
                    split(U_WOUT + 2 + RING)
                    h_turns(2, 0)
                for s in MIX.get(U_WOUT + v, []):
                    step(s)
                if v < 2:
                    split(U_WOUT + v + RING)
            ffn(1)
            for n in range(2):
                B = B_PROJ + n
                dve.wait_ge(unit_done, U_PROJ + n + 1)
                for m in range(M):
                    V.tensor_copy(pp[:, m, n * N:(n + 1) * N], acc[:, 2 * (B % 2) + m, :]).then_inc(acc_read, 1)
                split(U_GATE + n + 1)
            rms(3)
            split(U_GATE + 3)
            dve.wait_ge(acc_read, 2 * B_GATE)
            for n in range(2):
                c = slice(n * N, (n + 1) * N)
                for m in range(M):
                    dve.wait_ge(gate_ready, 2 * n + m + 1)
                    V.tensor_tensor(gate[:, m, :], gate[:, m, :], pp[:, m, c], ALU.mult).then_inc(acc_read, 1)
                    dve.wait_ge(acc_read, 2 * (B_GATE + n) + m + 1)
                    V.tensor_tensor(h[:, m, c], h[:, m, c], gate[:, m, :], ALU.add).then_inc(h_final, 1)
                    dve.wait_ge(h_final, 2 * n + m + 1)
                    link(V.tensor_tensor(res[:, m, c], h[:, m, c], fgain[:, c], ALU.mult))
                    if n == 1:
                        dve.wait_ge(ssq_ready, 19 + m)
                        link(V.tensor_tensor(rtmp[:, 4, m:m + 1], ssq[:, 4, 0, m:m + 1], ssq[:, 4, 1, m:m + 1], ALU.add))
                        V.tensor_scalar(rtmp[:, 4, m:m + 1], rtmp[:, 4, m:m + 1], 1.0 / D, EPS, ALU.mult, ALU.add
                                        ).then_inc(ms_ready, 1)
                        dve.wait_ge(root_ready, 5 + m)
                        link(V.reciprocal(rstd[:, 4, m:m + 1], rtmp[:, 4, m:m + 1]))
                        V.tensor_scalar(res[:, m, :], res[:, m, :], rstd[:, 4, m:m + 1], None, ALU.mult
                                        ).then_inc(res_ready, 1)


_INS = ["x", "p", "ffn1_norm", "ffn1_w_gu", "ffn1_w_down", "mix_norm", "w_in", "w_gk_up", "b_gk", "gla_out_norm",
        "w_out", "ffn2_norm", "ffn2_w_gu", "ffn2_w_down", "ple_norm", "w_ple_gate", "w_ple_proj", "rel_bias",
        "final_norm"]


def constants():
    import math
    import numpy as np

    t = np.arange(P)
    seg = np.zeros((P, 9, P), np.float32)
    for lv in range(7):
        w = 1 << lv
        mid = t // (2 * w) * 2 * w + w
        upper = (t[:, None] >= mid) & (t[:, None] <= t)
        lower = (t[:, None] > t) & (t[:, None] < mid)
        seg[:, lv + 1] = np.where(t >= mid, upper, lower)
    seg[:, 0] = t[:, None] > t
    seg[:, 8] = t[:, None] <= t
    masks = np.zeros((P, 7 * 64 + P), np.int32)
    q = np.arange(64)
    for lv in range(7):
        w = 1 << lv
        i = q // w * 2 * w + w + q % w
        masks[:, lv * 64:(lv + 1) * 64] = (t[:, None] // (2 * w) == i // (2 * w)) & (t[:, None] % (2 * w) < w)
    masks[:, 7 * 64:] = np.eye(P, dtype=np.int32)
    dist = np.arange(T)
    nf = np.maximum(dist, 1).astype(np.float32)
    exact = BUCKETS // 2
    large = exact + (np.log(nf / np.float32(exact)) / np.float32(math.log(4096 / exact))
                     * np.float32(BUCKETS - exact)).astype(np.int32)
    bucket = np.where(dist < exact, dist, np.minimum(large, BUCKETS - 1))
    rows = np.zeros((BUCKETS, BIAS_W), np.float32)
    rows[bucket, T - 1 - dist] = 1.0
    causal = np.zeros((MH, BIAS_W), np.float32)
    causal[:, T:] = -1e30
    return {"identity": np.eye(P, dtype=np.float32), "seg_sums": seg.reshape(P, 9 * P), "pair_masks": masks,
            "bucket_rows": rows, "causal_row": causal}


def kernel(**inputs):
    import numpy as _np
    import concourse.bacc as _bacc
    from concourse import mybir as _mybir
    from concourse.bass_utils import run_bass_kernel_spmd as _run

    nc = _bacc.Bacc("TRN2", target_bir_lowering=False, num_devices=1)
    arrays, args = {}, []
    given = {name: _np.ascontiguousarray(inputs[name]) for name in _INS} | constants()
    for name, a in given.items():
        arrays[f"in_{name}"] = a
        args.append(nc.dram_tensor(f"in_{name}", a.shape, _mybir.dt.from_np(a.dtype), kind="ExternalInput").ap())
    args.append(nc.dram_tensor("out_0", (1, T, D), _mybir.dt.float32, kind="ExternalOutput").ap())
    build(nc, *args)
    r = _run(nc, [arrays], core_ids=[0])
    return r.results[0]["out_0"]
```

```python
from contextlib import ExitStack

import concourse.bass as bass
from concourse import mybir

F32 = mybir.dt.float32
F32R = mybir.dt.float32r
I32 = mybir.dt.int32
ALU = mybir.AluOpType
ACT = mybir.ActivationFunctionType
AX = mybir.AxisListType.X

P = 128
T = 256
M = T // P
D = 1024
KC = D // P
F = 2816
FC = F // P
FB = 256
NB = F // FB
N = 512
RING = 4
CH = 4
EPS = 1e-6
PLE = 256

GH, GDK, GDV = 4, 64, 128
LR = 16
MH, MD = 8, 64
BUCKETS = 32
BIAS_W = 384
TAU = 16.0

QK_G, V_G, G_G, LR_G, Q_M, K_M, V_M = 0, 512, 1024, 1536, 1552, 2064, 2576
WIN_BLOCKS = [("q_m", Q_M), ("k_m", K_M), ("qk_g", QK_G), ("v_m", V_M), ("v_g", V_G), ("g_g", G_G)]

DOWN_CH = [4, 4, 4, 4, 4, 2]
U_GU = [0, 50]
U_DOWN = [22, 72]
U_WIN = 34
U_WOUT = 46
U_PROJ = 84
U_GATE = 86
UNITS = 90
B_GU = [0, 21]
B_DOWN = [11, 32]
B_WIN = 13
B_WOUT = 19
B_PROJ = 34
B_GATE = 36
B_H = {1: 11, 2: 19, 3: 32}

MIX = {
    (35, 1): ["lr"],
    (36, 1): ["z", "T_q0", "T_q1"],
    (38, 1): ["T_k0", "D0"],
    (38, 2): ["T_k1", "D1"],
    (38, 3): ["D2"],
    (39, 0): ["D3"],
    (39, 1): ["D4"],
    (39, 2): ["sc0.0", "sc0.1"],
    (39, 3): ["D5"],
    (40, 0): ["D6"],
    (40, 1): ["D7", "T_g0"],
    (40, 2): ["T_g1", "pt0.0"],
    (40, 3): ["pt0.1"],
    (41, 0): ["sc1.0", "sc1.1"],
    (41, 1): ["diag.0"],
    (41, 2): ["diag.1"],
    (41, 3): ["lv0.0"],
    (42, 0): ["lv0.1"],
    (42, 1): ["pv0", "lv1.0"],
    (42, 2): ["pt1.0", "pt1.1"],
    (42, 3): ["lv1.1"],
    (43, 0): ["sc2.0", "sc2.1"],
    (43, 1): ["pv1", "lv2.0"],
    (43, 2): ["lv2.1"],
    (44, 0): ["pt2.0", "pt2.1"],
    (44, 1): ["sc3.0", "sc3.1"],
    (44, 2): ["pv2", "lv3.0"],
    (44, 3): ["lv3.1"],
    (45, 1): ["pt3.0", "pt3.1"],
    (45, 2): ["pvg0"],
    (45, 3): ["pvg1"],
    (46, 0): ["pv3"],
    (47, 2): ["T_o0"],
    (47, 3): ["T_o1"],
}
ACT_STEPS = ["hi38", "nat0", "hi39", "z", "hi40", "nat1", "T_k0", "D0", "hi41",
             "T_k1", "D1", "D2", "hi42", "D3", "D4", "sc0", "D5", "nat2", "D6", "D7", "T_g0", "T_g1", "hi43",
             "sc1", "hi44", "nat3", "pv0", "hi45", "sc2", "pv1", "hi46", "nat4", "hi47", "sc3", "pv2",
             "hi48", "pvg", "pv3", "nat5", "groot", "hi49"]
DVE_STEPS = ["lo38", "lr", "z", "lo39", "la", "lo40", "lo41", "sc0", "lo42", "pr0", "pt0.0", "clear", "pt0.1",
             "Z0", "sc1", "diag", "Z1", "pr1", "lo43", "lv0", "pv0", "lv1.0", "pt1.0", "pt1.1", "lo44", "lv1.1",
             "Z2", "sc2", "lo45", "pr2", "pv1", "lv2", "Z3", "lo46", "pt2.0", "pt2.1", "sc3", "lo47", "pr3",
             "pv2", "lv3", "lo48", "pt3.0", "pt3.1", "pvg", "pv3", "gg", "o_g", "lo49"]


def chunks_of(u):
    for d in U_DOWN:
        if d <= u < d + 12:
            return DOWN_CH[(u - d) % 6]
    return 2 if U_PROJ <= u < U_GATE else CH


def plan_turns():
    first, uses = {}, []

    def add(name, k=1, who="dve"):
        first[name] = len(uses)
        uses.extend([who] * k)

    add("h0.0", 2)
    add("h0.1", 2)
    add("act0", NB)
    add("h1.0", 2)
    add("h1.1", 2)
    for at in sorted(MIX):
        for s in MIX[at]:
            if s[:3] in ("T_q", "T_k", "T_g"):
                add(s, who="act")
            elif s[:2] in ("T_", "pt") or s[:2] == "pv" and s[:3] != "pvg":
                add(s)
    add("h2.0", 2)
    add("h2.1", 2)
    add("act1", NB)
    add("p")
    add("h3.0", 2)
    add("h3.1", 2)
    count, out = {"dve": 0, "act": 0}, []
    for who in uses:
        count[who] += 1
        out.append((who, count[who]))
    return first, out


def plan_side():
    uses = [("gain0", "dve"), ("gain", "dve"), ("bias_row", "dve")]
    for at in sorted(MIX):
        for s in MIX[at]:
            if s[0] == "D":
                uses.append((s, "act"))
            elif s[:2] not in ("T_", "pt") and (s[:2] != "pv" or s[:3] == "pvg"):
                uses.append((s, "dve"))
    count, out = {"dve": 0, "act": 0}, {}
    for i, (name, who) in enumerate(uses):
        count[who] += 1
        out[name] = (i, who, count[who])
    return out


TURN, TURN_AT = plan_turns()
SIDE = plan_side()
SIDE_AT = {i: (who, c) for i, who, c in SIDE.values()}


def turned(name, k=0):
    return TURN_AT[TURN[name] + k][1]


def view(ap, dims, offset=0):
    return bass.AP(tensor=ap.tensor, offset=ap.offset + offset, ap=[list(ap.ap[0])] + [list(d) for d in dims])


def build(nc, x, p, ffn1_norm, ffn1_w_gu, ffn1_w_down, mix_norm, w_in, w_gk_up, b_gk, gla_out_norm,
          w_out, ffn2_norm, ffn2_w_gu, ffn2_w_down, ple_norm, w_ple_gate, w_ple_proj, rel_bias,
          final_norm, identity, seg_sums, pair_masks, bucket_rows, causal_row, out):
    x, out, w_gk_up, w_in, w_out = x[0], out[0], w_gk_up[0], w_in[0], w_out[0]
    p, w_ple_gate, w_ple_proj = p[0][0], w_ple_gate[0], w_ple_proj[0]
    ffn1_w_gu, ffn1_w_down, ffn2_w_gu, ffn2_w_down = ffn1_w_gu[0], ffn1_w_down[0], ffn2_w_gu[0], ffn2_w_down[0]
    ctx = ExitStack()
    with ctx:
        def sem(name):
            return ctx.enter_context(nc.semaphore(name))

        base = (nc.sbuf_base + 63) // 64 * 64
        top = [base]

        def sb(name, shape, dt=F32):
            size = 4
            for s in shape[1:]:
                size *= s
            t = nc.alloc_sbuf_tensor_at(name, shape, dt, offset=top[0])
            top[0] += (size + 31) // 32 * 32
            return t

        raw = sb("raw", [P, RING, CH * N])
        w_hi = sb("w_hi", [P, RING, CH * N], F32R)
        w_lo = sb("w_lo", [P, RING, CH * N], F32R)
        h = sb("h", [P, M, D])
        hT_hi = sb("hT_hi", [P, KC, T], F32R)
        hT_lo = sb("hT_lo", [P, KC, T], F32R)
        ident = sb("ident", [P, P])
        gains = sb("gains", [P, 4 * KC])
        lrw_pad = sb("lrw_pad", [P, KC, P], F32R)
        gk_up = sb("gk_up", [3 * LR, GH * GDK])
        b_row = sb("b_row", [P, GH * GDK])
        gout = sb("gout", [P, GDV])
        ssq = sb("ssq", [P, 5, 2, M])
        rstd = sb("rstd", [P, 5, M])
        rtmp = sb("rtmp", [P, 5, M])
        mx = sb("mx", [P, MH, M])
        sums = sb("sums", [P, MH, M])
        gss = sb("gss", [P, M, GH])
        grs = sb("grs", [P, M, GH])
        spare = sb("spare", [P, 4])
        junk = sb("junk", [P, N], mybir.dt.bfloat16)
        region = top[0]

        def at(name, kib, shape, dt=F32):
            size = 4
            for s in shape[1:]:
                size *= s
            assert region + int(kib * 1024) + size <= nc.sbuf_usable_end, name
            return nc.alloc_sbuf_tensor_at(name, shape, dt, offset=region + int(kib * 1024))

        a_hiT = at("a_hiT", 0, [P, FC, T], F32R)
        a_loT = at("a_loT", 22, [P, FC, T], F32R)
        silu_g = at("silu_g", 44, [P, M, FB])
        act = at("act", 46, [P, M, FB])
        gain_rows0 = at("gain_rows0", 55, [KC, P])
        gain_rows = at("gain_rows", 56, [3 * KC, P])
        rel = at("rel", 57, [BUCKETS, MH])
        rows = at("rows", 58, [BUCKETS, BIAS_W])
        causal = at("causal", 60, [MH, BIAS_W])
        bias_row = at("bias_row", 62, [MH, BIAS_W])
        lrw = at("lrw", 64, [P, KC, LR])
        seg_f = at("seg_f", 65, [P, 9 * P])
        E = at("E", 0, [P, 9, 2 * T])
        nat0 = at("nat0", 18, [P, M, N])
        nat1 = at("nat1", 22, [P, M, N])
        q_mT = at("q_mT", 26, [P, MH // 2, T])
        k_mT = at("k_mT", 30, [P, MH // 2, T])
        bias = at("bias", 34, [P, MH, T])
        q_gT = at("q_gT", 42, [P, 2 * T])
        k_gT = at("k_gT", 44, [P, 2 * T])
        gg = at("gg", 42, [P, M, N])
        lg = at("lg", 46, [P, M * T])
        log_a = at("log_a", 48, [P, M * T])
        vg = at("vg", 46, [P, M, N])
        lrT = at("lrT", 50, [3 * LR, T])
        sq = at("sq", 50, [P, N])
        la_hi = at("la_hi", 56, [P, M * T], F32R)
        la_lo = at("la_lo", 64, [P, M * T], F32R)
        AT = at("AT", 18, [P, 2 * GH, P])
        AT2 = at("AT2", 56, [P, GH, P])
        pr = at("pr", 58, [P, 2, 3 * P])
        prT = at("prT", 61, [P, 2, 3 * P])
        oT_hi = at("oT_hi", 64, [P, MH // 2, T], F32R)
        oT_lo = at("oT_lo", 68, [P, MH // 2, T], F32R)
        seg = at("seg", 72, [P, 9 * P], F32R)
        masks = at("masks", 52, [P, 7 * 64 + P], I32)
        p_nat = at("p_nat", 56, [P, M, PLE])
        pT_hi = at("pT_hi", 62, [P, 2, T], F32R)
        pT_lo = at("pT_lo", 64, [P, 2, T], F32R)
        pp = at("pp", 12, [P, M, D])
        fgain = at("fgain", 66, [P, D])
        gate = at("gate", 0, [P, M, N])
        res = at("res", 4, [P, M, D])

        acc = ctx.enter_context(nc.psum_tensor("acc", [P, 4, N], F32))
        turn = ctx.enter_context(nc.psum_tensor("turn", [P, 2, N], F32))
        side = ctx.enter_context(nc.psum_tensor("side", [P, 2, N], F32))

        row_dram = nc.dram_tensor("bias_row_dram", [MH, BIAS_W], F32).ap()
        skew_dram = nc.dram_tensor("bias_skew_dram", [P, MH, BIAS_W], F32).ap()

        x_in = [sem(f"x_in{n}") for n in range(2)]
        ident_in = sem("ident_in")
        gain0_in = sem("gain0_in")
        gains_in = sem("gains_in")
        lrw_in = sem("lrw_in")
        seg_in = sem("seg_in")
        small_in = sem("small_in")
        masks_in = sem("masks_in")
        bias_in = sem("bias_in")
        row_out = sem("row_out")
        skew_out = sem("skew_out")
        biasT_in = sem("biasT_in")
        ple_in = sem("ple_in")
        raw_in = [sem(f"raw_in{s}") for s in range(RING)]
        hi_ready = sem("hi_ready")
        lo_ready = sem("lo_ready")
        unit_done = sem("unit_done")
        acc_read = sem("acc_read")
        turn_done = sem("turn_done")
        turn_hi = sem("turn_hi")
        turn_read = sem("turn_read")
        turn_act = sem("turn_act")
        side_done = sem("side_done")
        side_dve = sem("side_dve")
        side_act = sem("side_act")
        ssq_ready = sem("ssq_ready")
        ms_ready = sem("ms_ready")
        root_ready = sem("root_ready")
        rstd_ready = sem("rstd_ready")
        silu_ready = sem("silu_ready")
        zeroed = sem("zeroed")
        consts_hi = sem("consts_hi")
        consts_lo = sem("consts_lo")
        z_abs = sem("z_abs")
        lg_ready = sem("lg_ready")
        la_ready = sem("la_ready")
        la_hi_ready = sem("la_hi_ready")
        la_lo_ready = sem("la_lo_ready")
        Z_ready = sem("Z_ready")
        neg_max = sem("neg_max")
        exp_ready = sem("exp_ready")
        probs_ready = sem("probs_ready")
        gss_sq = sem("gss_sq")
        gms_ready = sem("gms_ready")
        groot = sem("groot")
        gate_ready = sem("gate_ready")
        spare_set = sem("spare_set")
        junk_set = sem("junk_set")
        last_tile = sem("last_tile")
        h_final = sem("h_final")
        half_in = sem("half_in")
        half_hi = sem("half_hi")
        half_lo = sem("half_lo")
        res_ready = sem("res_ready")
        res_out = sem("res_out")
        dve_step = sem("dve_step")
        act_step = sem("act_step")

        block = ctx.enter_context(nc.Block())

        GU_W = [ffn1_w_gu, ffn2_w_gu]
        DOWN_W = [ffn1_w_down, ffn2_w_down]

        @block.sync
        def _(sp):
            def free(u):
                if not isinstance(u, int) or u >= RING:
                    sp.wait_ge(lo_ready, u - (RING - 1))

            def gu_unit(f, b, kh, u, slot):
                free(u)
                w = GU_W[f].rearrange("(c p) f -> p c f", p=P)
                dst = raw[:, slot, :].rearrange("p (k g f) -> p k g f", k=CH, g=2)
                for g in range(2):
                    sp.dma_start(dst[:, :, g, :], w[:, CH * kh:CH * kh + CH, bass.ds(g * F + b * FB, FB)]
                                 ).then_inc(raw_in[slot], 16)

            def unit(w, c0, col, u):
                free(u)
                nk = chunks_of(u)
                slot = u % RING
                wv = w.rearrange("(c p) f -> p c f", p=P)
                dst = raw[:, slot, :nk * N].rearrange("p (k f) -> p k f", k=nk)
                for a in range(2):
                    r = slice(a * nk // 2, (a + 1) * nk // 2)
                    sp.dma_start(dst[:, r, :], wv[:, c0 + r.start:c0 + r.stop, col:col + N]
                                 ).then_inc(raw_in[slot], 16)

            def ffn(f):
                first = 3
                for b in range(first):
                    for kh in range(2):
                        u = U_GU[f] + 2 * b + kh
                        if u >= 2:
                            gu_unit(f, b, kh, u, u % RING)
                with sp.Fori(0, (NB - first) // 2) as i:
                    for j in range(2):
                        for kh in range(2):
                            u = U_GU[f] + 2 * (first + j) + kh
                            gu_unit(f, i * 2 + (first + j), kh, i * 4 + u, u % RING)
                for n in range(2):
                    for k in range(6):
                        unit(DOWN_W[f], CH * k, n * N, U_DOWN[f] + 6 * n + k)

            xv = x.rearrange("(m p) d -> p m d", p=P)
            w = ffn1_w_gu.rearrange("(c p) f -> p c f", p=P)
            dst = raw[:, 0, :].rearrange("p (k g f) -> p k g f", k=CH, g=2)
            for n, arrived in ((0, half_in), (1, raw_in[0])):
                sp.dma_start(h[:, :, n * N:(n + 1) * N], xv[:, :, n * N:(n + 1) * N]).then_inc(x_in[n], 16)
                for g in range(2):
                    sp.dma_start(dst[:, 2 * n:2 * n + 2, g, :], w[:, 2 * n:2 * n + 2, g * F:g * F + FB]
                                 ).then_inc(arrived, 16)
            gu_unit(0, 0, 1, 1, 1)
            ffn(0)
            for b, (_, col) in enumerate(WIN_BLOCKS):
                for kh in range(2):
                    unit(w_in, CH * kh, col, U_WIN + 2 * b + kh)
            for v, (n, kh) in enumerate([(0, 1), (1, 1), (0, 0), (1, 0)]):
                unit(w_out, CH * kh, n * N, U_WOUT + v)
            ffn(1)
            for n in range(2):
                unit(w_ple_proj, 0, n * N, U_PROJ + n)
            for n in range(2):
                for kh in range(2):
                    unit(w_ple_gate, CH * kh, n * N, U_GATE + 2 * n + kh)
            ov = out.rearrange("(m p) d -> p m d", p=P)
            for m in range(M):
                for n in range(2):
                    c = slice(n * N, (n + 1) * N)
                    sp.wait_ge(res_ready, 2 * m + n + 1)
                    sp.dma_start(ov[:, m, c], res[:, m, c]).then_inc(res_out, 16)
            sp.wait_ge(res_out, 32 * M)

        @block.gpsimd
        def _(pool):
            nc.gpsimd.memset(lrw_pad[:].bitcast(F32), 0.0).then_inc(zeroed, 1)
            nc.gpsimd.memset(gk_up[:], 0.0).then_inc(zeroed, 1)
            pool.wait_ge(unit_done, 1)
            pool.dma_start(lrw[:], w_in.rearrange("(c p) f -> p c f", p=P)[:, :, LR_G:LR_G + LR]).then_inc(lrw_in, 16)
            pool.dma_start(seg_f[:], seg_sums).then_inc(seg_in, 16)
            for k, g in enumerate([mix_norm, ffn2_norm, ple_norm]):
                pool.dma_start(gain_rows[k * KC:(k + 1) * KC, :], g.rearrange("a (c p) -> (a c) p", p=P)
                               ).then_inc(gains_in, 16)
            pool.dma_start(rel[:], rel_bias).then_inc(bias_in, 16)
            pool.dma_start(rows[:], bucket_rows).then_inc(bias_in, 16)
            pool.dma_start(causal[:], causal_row).then_inc(bias_in, 16)
            pool.wait_ge(zeroed, 2)
            pool.dma_start(gk_up[0:LR, :], w_gk_up).then_inc(small_in, 16)
            pool.dma_start(gk_up[2 * LR:3 * LR, :], w_gk_up).then_inc(small_in, 16)
            pool.dma_start(b_row[:], bass.AP(tensor=b_gk.tensor, offset=0, ap=[[0, P], [1, GH * GDK]])
                           ).then_inc(small_in, 16)
            pool.dma_start(gout[:], bass.AP(tensor=gla_out_norm.tensor, offset=0, ap=[[0, P], [1, GDV]])
                           ).then_inc(small_in, 16)
            pool.wait_ge(side_dve, SIDE["bias_row"][2])
            pool.dma_start(row_dram, bias_row[:]).then_inc(row_out, 16)
            pool.wait_ge(row_out, 16)
            pool.dma_start(skew_dram, bass.AP(tensor=row_dram.tensor, offset=0,
                                              ap=[[0, P], [BIAS_W, MH], [1, BIAS_W]])).then_inc(skew_out, 16)
            pool.wait_ge(skew_out, 16)
            pool.wait_ge(unit_done, U_WIN)
            pool.dma_start(bias[:], bass.AP(tensor=skew_dram.tensor, offset=P - 1,
                                            ap=[[MH * BIAS_W - 1, P], [BIAS_W, MH], [1, T]])).then_inc(biasT_in, 16)
            pool.dma_start(masks[:], pair_masks).then_inc(masks_in, 16)
            pool.wait_ge(unit_done, U_GU[1])
            pool.dma_start(p_nat[:], p.rearrange("(m p) e -> p m e", p=P)).then_inc(ple_in, 16)
            pool.dma_start(fgain[:], bass.AP(tensor=final_norm.tensor, offset=0, ap=[[0, P], [1, D]])
                           ).then_inc(ple_in, 16)

        @block.tensor
        def _(pe):
            def mm(o, lhsT, rhs, start, stop):
                return nc.tensor.matmul(o, lhsT, rhs, start=start, stop=stop, skip_group_check=True)

            def exact3(o, l_hi, l_lo, r_hi, r_lo, start, stop):
                mm(o, l_hi, r_hi, start, False)
                mm(o, l_hi, r_lo, False, False)
                return mm(o, l_lo, r_hi, False, stop)

            def unit(u, slot, pair, lhs, k0, nk, first, last, ks=None):
                ks = ks or range(nk)
                if isinstance(u, int) and u == 0:
                    pe.wait_ge(lo_ready if ks[0] else half_lo, 1)
                elif ks[0] == 0:
                    pe.wait_ge(lo_ready, u + 1)
                for k in ks:
                    for m in range(M):
                        l_hi, l_lo = lhs(k0 + k, m)
                        ins = exact3(acc[:, 2 * pair + m, :], l_hi, l_lo,
                                     w_hi[:, slot, k * N:(k + 1) * N], w_lo[:, slot, k * N:(k + 1) * N],
                                     first and k == 0, last and k == nk - 1)
                if ks[-1] == nk - 1:
                    ins.then_inc(unit_done, 1)

            def acc_free(B):
                if not isinstance(B, int) or B >= 2:
                    pe.wait_ge(acc_read, (B - 1) * 2)

            def from_hT(c, m):
                return hT_hi[:, c, m * P:(m + 1) * P], hT_lo[:, c, m * P:(m + 1) * P]

            def from_aT(c, m):
                return a_hiT[:, c, m * P:(m + 1) * P], a_loT[:, c, m * P:(m + 1) * P]

            def turn_open(t):
                if t >= 2:
                    who, count = TURN_AT[t - 2]
                    pe.wait_ge(turn_read if who == "dve" else turn_act, count)

            def flip(o, src, k=P):
                return nc.tensor.transpose(o, src, ident[:k, :k])

            def h_turns(s, n):
                if s == 0:
                    pe.wait_ge(x_in[n], 16)
                else:
                    pe.wait_ge(acc_read, 2 * (B_H[s] + n) + 2)
                for a in range(2):
                    t = TURN[f"h{s}.{n}"] + a
                    turn_open(t)
                    for c in range(2):
                        for m in range(M):
                            k = 4 * n + 2 * a + c
                            ins = flip(turn[:, t % 2, (2 * c + m) * P:(2 * c + m + 1) * P], h[:, m, k * P:(k + 1) * P])
                    ins.then_inc(turn_done, 1)

            def h_ready(s, n, a=1):
                pe.wait_ge(turn_read, turned(f"h{s}.{n}", a))

            def act_turn(f, b, par):
                pe.wait_ge(acc_read, (b + B_GU[f]) * 2 + 2)
                pe.wait_ge(turn_read, b + (turned(f"act{f}") - 2))
                for c in range(2):
                    for m in range(M):
                        ins = flip(turn[:, (TURN[f"act{f}"] + par) % 2, (2 * c + m) * P:(2 * c + m + 1) * P],
                                   act[:, m, c * P:(c + 1) * P])
                ins.then_inc(turn_done, 1)

            def gu_block(f, b, par, s0, first=False):
                pair = (B_GU[f] + par) % 2
                acc_free(b + B_GU[f])
                u = b * 2 + U_GU[f]
                if first:
                    s = 2 * f
                    if f == 0:
                        h_turns(s, 1)
                        h_ready(s, 0, 0)
                        unit(u, s0, pair, from_hT, 0, CH, True, False, range(2))
                        h_ready(s, 0)
                    else:
                        h_ready(s, 0)
                        unit(u, s0, pair, from_hT, 0, CH, True, False, range(2))
                        h_turns(s, 1)
                    unit(u, s0, pair, from_hT, 0, CH, True, False, range(2, CH))
                    h_ready(s, 1)
                else:
                    unit(u, s0, pair, from_hT, 0, CH, True, False)
                    act_turn(f, b - 1, 1 - par)
                unit(u + 1, (s0 + 1) % RING, pair, from_hT, CH, CH, False, True)

            def ffn(f):
                gu_block(f, 0, 0, U_GU[f] % RING, first=True)
                with pe.Fori(0, (NB - 1) // 2) as i:
                    for j in range(2):
                        gu_block(f, i * 2 + (1 + j), (1 + j) % 2, (U_GU[f] + 2 + 2 * j) % RING)
                for n in range(2):
                    B = B_DOWN[f] + n
                    acc_free(B)
                    for k in range(6):
                        u = U_DOWN[f] + 6 * n + k
                        if n == 0:
                            pe.wait_ge(turn_read, turned(f"act{f}", min(2 * k + 2, NB) - 1))
                        unit(u, u % RING, B % 2, from_aT, CH * k, DOWN_CH[k], k == 0, k == 5)
                        if n == 0 and k == 0:
                            act_turn(f, NB - 1, (NB - 1) % 2)
                        if f == 1 and n == 0 and k == 2:
                            p_turn()
                        if n == 1 and k == 1:
                            h_turns(2 * f + 1, 0)
                        if f == 0 and n == 0 and k == 1:
                            o = side_open("gain")
                            pe.wait_ge(gains_in, 48)
                            flip(o[:, 0:3 * KC], gain_rows[:], 3 * KC).then_inc(side_done, 1)
                            o = side_open("bias_row")
                            pe.wait_ge(bias_in, 48)
                            mm(o[0:MH, 0:BIAS_W], rel[:], rows[:], True, True).then_inc(side_done, 1)

            def p_turn():
                pe.wait_ge(ple_in, 32)
                nat_turn("p", p_nat, 0)

            def side_open(name):
                i = SIDE[name][0]
                if i >= 2:
                    who, count = SIDE_AT[i - 2]
                    pe.wait_ge(side_dve if who == "dve" else side_act, count)
                return side[:, i % 2, :]

            def nat_turn(name, src, cols):
                t = TURN[name]
                turn_open(t)
                for c in range(2):
                    for m in range(M):
                        ins = flip(turn[:, t % 2, (2 * c + m) * P:(2 * c + m + 1) * P],
                                   src[:, m, cols + c * P:cols + (c + 1) * P])
                ins.then_inc(turn_done, 1)

            def step(s):
                if s == "lr":
                    o = side_open(s)
                    pe.wait_ge(consts_lo, 1)
                    h_ready(1, 1)
                    for c in range(KC):
                        mm(o[:, 0:T], lrw_pad[:, c, :], hT_hi[:, c, :], c == 0, False)
                        ins = mm(o[:, 0:T], lrw_pad[:, c, :], hT_lo[:, c, :], False, c == KC - 1)
                    ins.then_inc(side_done, 1)
                elif s == "z":
                    o = side_open(s)
                    pe.wait_ge(side_dve, SIDE["lr"][2])
                    pe.wait_ge(small_in, 64)
                    for m in range(M):
                        ins = mm(o[:, m * T:(m + 1) * T], lrT[:, m * P:(m + 1) * P], gk_up[:], True, True)
                    ins.then_inc(side_done, 1)
                elif s[:3] == "T_q":
                    pe.wait_ge(acc_read, 2 * B_WIN + 2)
                    nat_turn(s, nat0, 2 * P * int(s[-1]))
                elif s[:3] == "T_k":
                    pe.wait_ge(acc_read, 2 * B_WIN + 4)
                    nat_turn(s, nat1, 2 * P * int(s[-1]))
                elif s[:3] == "T_g":
                    pe.wait_ge(acc_read, 2 * B_WIN + 6)
                    nat_turn(s, nat0, 2 * P * int(s[-1]))
                elif s[0] == "D":
                    d = int(s[1])
                    m, hp, half = d // 4, d // 2 % 2, d % 2
                    o = side_open(s)
                    pe.wait_ge(la_lo_ready, 1)
                    lhs = slice(m * T + hp * P, m * T + (hp + 1) * P)
                    r = seg[:, (m + 4 * half) * P:(m + 4 * half + 4) * P]
                    mm(o, la_hi[:, lhs], r, True, False)
                    mm(o, la_lo[:, lhs], r, False, True).then_inc(side_done, 1)
                elif s[:2] == "sc":
                    head = 2 * int(s[2]) + int(s[4])
                    o = side_open(s)
                    pe.wait_ge(turn_act, turned("T_k1"))
                    lo = 64 * (head % 2)
                    q, k = q_mT[lo:lo + 64, head // 2, :], k_mT[lo:lo + 64, head // 2, :]
                    mm(o[:, 0:P], q[:, 0:P], k[:, 0:P], True, True)
                    mm(o[:, P:3 * P], q[:, P:T], k[:, :], True, True).then_inc(side_done, 1)
                elif s[:2] == "pt":
                    pair, i = int(s[2]), int(s[4])
                    t = TURN[s]
                    pe.wait_ge(probs_ready, 2 * pair + i + 1)
                    turn_open(t)
                    for k in range(3):
                        ins = flip(turn[:, t % 2, k * P:(k + 1) * P], pr[:, i, k * P:(k + 1) * P])
                    ins.then_inc(turn_done, 1)
                elif s[:3] == "pvg":
                    m = int(s[3])
                    o = side_open(s)
                    pe.wait_ge(acc_read, 2 * B_WIN + 10)
                    pe.wait_ge(side_dve, SIDE["lv3.1"][2])
                    for hd in range(GH):
                        c = slice(hd * GDV, (hd + 1) * GDV)
                        hh, hp = hd % 2, hd // 2
                        ins = mm(o[:, c], AT[:, 4 * hh + 2 * hp + m, :], vg[:, m, c], True, m == 0)
                        if m == 1:
                            ins = mm(o[:, c], AT2[:, 2 * hh + hp, :], vg[:, 0, c], False, True)
                    ins.then_inc(side_done, 1)
                elif s[:2] == "pv":
                    pair = int(s[2])
                    t = TURN[s]
                    pe.wait_ge(turn_read, turned(f"pt{pair}.1"))
                    pe.wait_ge(acc_read, 2 * B_WIN + 8)
                    turn_open(t)
                    for i in range(2):
                        c = slice((2 * pair + i) * MD, (2 * pair + i + 1) * MD)
                        o = turn[64 * i:64 * i + 64, t % 2, 0:T]
                        mm(o, nat1[:, 0, c], prT[:, i, 0:T], True, False)
                        ins = mm(o[:, P:T], nat1[:, 1, c], prT[:, i, T:T + P], False, True)
                    ins.then_inc(turn_done, 1)
                elif s[:4] == "diag":
                    hh = int(s[5])
                    o = side_open(s)
                    pe.wait_ge(turn_act, turned("T_g1"))
                    r = slice(64 * hh, 64 * hh + 64)
                    for k in range(4):
                        c = slice(k * P, (k + 1) * P)
                        ins = mm(o[:, c], k_gT[r, c], q_gT[r, c], True, True)
                    ins.then_inc(side_done, 1)
                elif s[:2] == "lv":
                    hh = int(s[4])
                    o = side_open(s)
                    r = slice(64 * hh, 64 * hh + 64)
                    pe.wait_ge(Z_ready, 2 * int(s[2]) + 2)
                    for a in range(2):
                        lv = 2 * int(s[2]) + a
                        w = 1 << lv
                        if lv == 7:
                            for hp in range(2):
                                c = hp * T
                                ins = mm(o[:, T + hp * P:T + (hp + 1) * P], E[r, 0, c:c + P], E[r, 8, c + P:c + T],
                                         True, True)
                        else:
                            for k in range(4):
                                z = E[r, lv + 1, k * P:(k + 1) * P]
                                ins = mm(o[:, a * T + k * 64:a * T + (k + 1) * 64], z,
                                         view(z, [[2 * w, 64 // w], [1, w]], w), True, True)
                    ins.then_inc(side_done, 1)
                elif s[:3] == "T_o":
                    a = int(s[3])
                    t = TURN[s]
                    pe.wait_ge(side_dve, SIDE["pvg1"][2])
                    turn_open(t)
                    for c in range(2):
                        for m in range(M):
                            ins = flip(turn[:, t % 2, (2 * c + m) * P:(2 * c + m + 1) * P],
                                       gg[:, m, (2 * a + c) * P:(2 * a + c + 1) * P])
                    ins.then_inc(turn_done, 1)

            def from_oT(c, m):
                r = slice(m * P, (m + 1) * P)
                if c < 4:
                    return hT_hi[:, 4 + c, r], hT_lo[:, 4 + c, r]
                return oT_hi[:, c - 4, r], oT_lo[:, c - 4, r]

            def keep_warm(count):
                for _ in range(count):
                    mm(acc[:, 3, :], junk[:, 0:P], junk[:], True, True)

            pe.wait_ge(junk_set, 1)
            keep_warm(7)
            pe.wait_ge(ident_in, 16)
            h_turns(0, 0)
            pe.wait_ge(gain0_in, 16)
            o = side_open("gain0")
            flip(o[:, 0:KC], gain_rows0[:], KC).then_inc(side_done, 1)
            keep_warm(12)
            ffn(0)
            for b in range(len(WIN_BLOCKS)):
                B = B_WIN + b
                acc_free(B)
                for kh in range(2):
                    u = U_WIN + 2 * b + kh
                    for k in range(CH):
                        if u <= U_WIN + 1:
                            h_ready(1, kh, k // 2)
                        unit(u, u % RING, B % 2, from_hT, CH * kh, CH, kh == 0, kh == 1, range(k, k + 1))
                        if u == U_WIN and k == 1:
                            h_turns(1, 1)
                        for s in MIX.get((u, k), []):
                            step(s)
            for v, (n, kh) in enumerate([(0, 1), (1, 1), (0, 0), (1, 0)]):
                u, B = U_WOUT + v, B_WOUT + n
                if kh == 1:
                    acc_free(B)
                for k in range(CH):
                    if v == 2:
                        pe.wait_ge(turn_read, turned(f"T_o{k // 2}"))
                    if v == 0:
                        pe.wait_ge(turn_read, turned(f"pv{k}"))
                    unit(u, u % RING, B % 2, from_oT, CH * kh, CH, kh == 1, kh == 0, range(k, k + 1))
                    if v == 3 and k == 1:
                        h_turns(2, 0)
                    for s in MIX.get((u, k), []):
                        step(s)
            ffn(1)
            for n in range(2):
                u, B = U_PROJ + n, B_PROJ + n
                acc_free(B)
                pe.wait_ge(turn_read, turned("p"))
                unit(u, u % RING, B % 2,
                     lambda c, m: (pT_hi[:, c, m * P:(m + 1) * P], pT_lo[:, c, m * P:(m + 1) * P]), 0, 2, True, True)
                if n == 0:
                    h_turns(3, 1)
            acc_free(B_GATE)
            for kh in range(2):
                u = U_GATE + kh
                h_ready(3, kh)
                unit(u, u % RING, B_GATE % 2, from_hT, CH * kh, CH, kh == 0, kh == 1)
            acc_free(B_GATE + 1)
            for m in range(M):
                for c in range(KC):
                    u, k = U_GATE + 2 + c // CH, c % CH
                    if m == 0 and k == 0:
                        pe.wait_ge(lo_ready, u + 1)
                    l_hi, l_lo = from_hT(c, m)
                    ins = exact3(acc[:, 2 * ((B_GATE + 1) % 2) + m, :], l_hi, l_lo,
                                 w_hi[:, u % RING, k * N:(k + 1) * N], w_lo[:, u % RING, k * N:(k + 1) * N],
                                 c == 0, c == KC - 1)
                ins.then_inc(last_tile, 1)

        @block.scalar
        def _(act_e):
            A = nc.scalar.activation

            def split(v, slot=None, turn_of_slot=None):
                if isinstance(v, int):
                    if v >= UNITS:
                        return
                    slot, turn_of_slot, nk = v % RING, v // RING, chunks_of(v)
                else:
                    nk = CH
                act_e.wait_ge(raw_in[slot], turn_of_slot * 32 + 32)
                if not isinstance(v, int) or v >= RING:
                    act_e.wait_ge(unit_done, v - (RING - 1))
                A(w_hi[:, slot, :nk * N], raw[:, slot, :nk * N], ACT.Copy).then_inc(hi_ready, 1)

            def squares(s, n):
                if s == 0:
                    act_e.wait_ge(x_in[n], 16)
                else:
                    act_e.wait_ge(acc_read, 2 * (B_H[s] + n) + 2)
                for m in range(M):
                    if 4 * s + 2 * n + m:
                        act_e.wait_ge(ssq_ready, 4 * s + 2 * n + m)
                    A(junk[:], h[:, m, n * N:(n + 1) * N], ACT.Square,
                      accum_out=ssq[:, s, n, m:m + 1]).then_inc(ssq_ready, 1)

            def h_turns(s, n):
                for a in range(2):
                    t = TURN[f"h{s}.{n}"] + a
                    act_e.wait_ge(turn_done, t + 1)
                    for c in range(2):
                        k = 4 * n + 2 * a + c
                        if n == 0 and a == 0 and c == 0:
                            act_e.wait_ge(side_dve, SIDE["gain" if s else "gain0"][2])
                        A(hT_hi[:, k, :], turn[:, t % 2, c * T:(c + 1) * T], ACT.Copy,
                          scale=gains[:, s * KC + k:s * KC + k + 1]).then_inc(turn_hi, 1)

            def root(s):
                act_e.wait_ge(ms_ready, s + 1)
                A(rtmp[:, s, :], rtmp[:, s, :], ACT.Sqrt).then_inc(root_ready, 1)

            def act_turn(f, b, par):
                t = b + TURN[f"act{f}"]
                act_e.wait_ge(turn_done, t + 1)
                dst = a_hiT[:, bass.ds(b * 2, 2), :]
                src = turn[:, (TURN[f"act{f}"] + par) % 2, :].rearrange("p (c t) -> p c t", c=2)
                A(dst, src, ACT.Copy).then_inc(turn_hi, 1)

            def gated(f, b, par):
                B = b + B_GU[f]
                for m in range(M):
                    if m == 0:
                        act_e.wait_ge(unit_done, b * 2 + (U_GU[f] + 2))
                        if isinstance(b, int) and b == 0:
                            act_e.wait_ge(rstd_ready, 2 * f + 1)
                        if not (isinstance(b, int) and B == 0):
                            act_e.wait_ge(acc_read, B * 2)
                    A(silu_g[:, m, :], acc[:, 2 * ((B_GU[f] + par) % 2) + m, 0:FB], ACT.Silu,
                      scale=rstd[:, 2 * f, m:m + 1]).then_inc(silu_ready, 1)

            def ffn(f):
                U = U_GU[f]

                def blk(b, j, i=None):
                    def sp_(k):
                        v = U + 2 * j + k + RING
                        if i is None:
                            split(v)
                        else:
                            split(i * 4 + v, v % RING, i + v // RING)
                    if j == 0:
                        if f == 1:
                            squares(2, 1)
                            h_turns(2, 1)
                            root(2)
                            sp_(0)
                    else:
                        act_turn(f, b - 1, (j - 1) % 2)
                        sp_(0)
                    gated(f, b, j % 2)
                    if f == 0 and j == 0:
                        sp_(0)
                    sp_(1)

                blk(0, 0)
                with act_e.Fori(0, (NB - 1) // 2) as i:
                    for j in range(2):
                        blk(i * 2 + (1 + j), 1 + j, i)
                for n in range(2):
                    for k in range(6):
                        u = U_DOWN[f] + 6 * n + k
                        if n == 0 and k == 0:
                            act_turn(f, NB - 1, (NB - 1) % 2)
                        if f == 1 and n == 0 and k == 2:
                            t = TURN["p"]
                            act_e.wait_ge(turn_done, t + 1)
                            A(pT_hi[:], turn[:, t % 2, :].rearrange("p (c t) -> p c t", c=2), ACT.Copy
                              ).then_inc(turn_hi, 1)
                        if f == 0 and n == 0 and k == 2:
                            act_e.wait_ge(lrw_in, 16)
                            act_e.wait_ge(zeroed, 2)
                            A(lrw_pad[:, :, 0:LR], lrw[:], ACT.Copy).then_inc(consts_hi, 1)
                            act_e.wait_ge(seg_in, 16)
                            A(seg[:], seg_f[:], ACT.Copy).then_inc(consts_hi, 1)
                        if n == 1 and k == 0:
                            squares(2 * f + 1, 0)
                        if n == 1 and k == 1:
                            h_turns(2 * f + 1, 0)
                        split(u + RING)

            def evacuate(s):
                t, a = TURN[s], int(s[3])
                act_e.wait_ge(turn_done, t + 1)
                dst, scale = {"T_q": (q_mT[:, 2 * a:2 * a + 2, :].rearrange("p c t -> p (c t)"), MD ** -0.5),
                              "T_k": (k_mT[:, 2 * a:2 * a + 2, :].rearrange("p c t -> p (c t)"), 1.0),
                              "T_g": ([q_gT, k_gT][a][:], [GDK ** -0.5, 1.0][a])}[s[:3]]
                A(dst, turn[:, t % 2, :], ACT.Copy, scale=scale).then_inc(turn_act, 1)

            def nat(b):
                dst = [nat0, nat1, nat0, nat1, vg, gg][b]
                act_e.wait_ge(unit_done, U_WIN + 2 * b + 2)
                if b == 0:
                    act_e.wait_ge(rstd_ready, 2)
                for m in range(M):
                    A(dst[:, m, :], acc[:, 2 * ((B_WIN + b) % 2) + m, :], ACT.Silu if b == 5 else ACT.Copy,
                      scale=rstd[:, 1, m:m + 1]).then_inc(acc_read, 1)

            def step(s):
                if s[:2] == "hi":
                    split(int(s[2:]))
                elif s[:3] == "nat":
                    nat(int(s[3]))
                elif s[:3] in ("T_q", "T_k", "T_g"):
                    evacuate(s)
                elif s == "z":
                    act_e.wait_ge(side_dve, SIDE[s][2])
                    A(lg[:], log_a[:], ACT.Abs).then_inc(z_abs, 1)
                    evacuate("T_q0")
                    act_e.wait_ge(z_abs, 1)
                    A(lg[:], lg[:], ACT.Exp, scale=-1.0).then_inc(act_step, 1)
                    evacuate("T_q1")
                    act_e.wait_ge(act_step, 1)
                    A(lg[:], lg[:], ACT.Ln, bias=1.0).then_inc(lg_ready, 1)
                    act_e.wait_ge(la_ready, 1)
                    A(la_hi[:], log_a[:], ACT.Copy).then_inc(la_hi_ready, 1)
                elif s[0] == "D":
                    d = int(s[1])
                    m, hp, half = d // 4, d // 2 % 2, d % 2
                    act_e.wait_ge(side_done, SIDE[s][0] + 1)
                    k = m + 4 * half
                    src = side[:, SIDE[s][0] % 2, :].rearrange("p (l t) -> p l t", l=4)
                    A(E[:, k:k + 4, hp * T + m * P:hp * T + (m + 1) * P], src, ACT.Exp).then_inc(side_act, 1)
                elif s[:2] == "sc":
                    for i in range(2):
                        head = 2 * int(s[2]) + i
                        act_e.wait_ge(neg_max, head + 1)
                        A(pr[:, i, 0:P], pr[:, i, 0:P], ACT.Exp, bias=mx[:, head, 0:1],
                          accum_out=sums[:, head, 0:1])
                        A(pr[:, i, P:3 * P], pr[:, i, P:3 * P], ACT.Exp, bias=mx[:, head, 1:2],
                          accum_out=sums[:, head, 1:2]).then_inc(exp_ready, 1)
                elif s == "pvg":
                    for m in range(M):
                        i = SIDE[f"pvg{m}"][0]
                        act_e.wait_ge(side_done, i + 1)
                        if m:
                            act_e.wait_ge(gms_ready, m)
                        A(sq[:], side[:, i % 2, :], ACT.Square).then_inc(gss_sq, 1)
                elif s == "groot":
                    act_e.wait_ge(gms_ready, M + 1)
                    A(grs[:], gss[:], ACT.Sqrt).then_inc(groot, 1)
                elif s[:2] == "pv":
                    t, pair = TURN[s], int(s[2])
                    act_e.wait_ge(turn_done, t + 1)
                    A(oT_hi[:, pair, :], turn[:, t % 2, 0:T], ACT.Copy).then_inc(turn_hi, 1)
                elif s[:3] == "T_o":
                    t, a = TURN[s], int(s[3])
                    act_e.wait_ge(turn_done, t + 1)
                    A(hT_hi[:, 4 + 2 * a:6 + 2 * a, :], turn[:, t % 2, :].rearrange("p (c t) -> p c t", c=2), ACT.Copy
                      ).then_inc(turn_hi, 1)

            act_e.dma_start(ident[:], identity).then_inc(ident_in, 16)
            act_e.dma_start(gain_rows0[:], ffn1_norm.rearrange("a (c p) -> (a c) p", p=P)).then_inc(gain0_in, 16)
            act_e.wait_ge(spare_set, 1)
            A(spare[:, 0:1], spare[:, 1:2], ACT.Silu)
            half = CH * N // 2
            act_e.wait_ge(half_in, 32)
            A(w_hi[:, 0, :half], raw[:, 0, :half], ACT.Copy).then_inc(half_hi, 1)
            h_turns(0, 0)
            act_e.wait_ge(raw_in[0], 32)
            A(w_hi[:, 0, half:], raw[:, 0, half:], ACT.Copy).then_inc(hi_ready, 1)
            h_turns(0, 1)
            split(1)
            split(2)
            squares(0, 0)
            squares(0, 1)
            root(0)
            split(3)
            ffn(0)
            squares(1, 1)
            h_turns(1, 1)
            root(1)
            for s in ACT_STEPS:
                step(s)
            split(U_WOUT + RING)
            for a in range(2):
                step(f"T_o{a}")
            split(U_WOUT + 1 + RING)
            split(U_WOUT + 2 + RING)
            squares(2, 0)
            h_turns(2, 0)
            split(U_WOUT + 3 + RING)
            ffn(1)
            squares(3, 1)
            h_turns(3, 1)
            for v in range(U_PROJ, U_PROJ + 2):
                split(v + RING)
            root(3)

            def sigmoid(n, m):
                if n:
                    act_e.wait_ge(h_final, m + 1)
                A(gate[:, m, :], acc[:, 2 * ((B_GATE + n) % 2) + m, :], ACT.Sigmoid,
                  scale=rstd[:, 3, m:m + 1]).then_inc(gate_ready, 1)

            def last_squares(n, m):
                k = 2 * n + m
                act_e.wait_ge(h_final, k + 1)
                act_e.wait_ge(ssq_ready, 16 + k)
                A(junk[:], h[:, m, n * N:(n + 1) * N], ACT.Square, accum_out=ssq[:, 4, n, m:m + 1]).then_inc(ssq_ready, 1)

            A(spare[:, 3:4], spare[:, 1:2], ACT.Sigmoid)
            act_e.wait_ge(rstd_ready, 4)
            act_e.wait_ge(unit_done, U_GATE + 2)
            for m in range(M):
                sigmoid(0, m)
            for m in range(M):
                last_squares(0, m)
            for m in range(M):
                act_e.wait_ge(last_tile, m + 1)
                sigmoid(1, m)
                A(spare[:, 0:1], spare[:, 1:2], ACT.Sqrt)
                last_squares(1, m)
                act_e.wait_ge(ssq_ready, 19 + m)
                act_e.wait_ge(ms_ready, 5)
                A(rtmp[:, 4, m:m + 1], ssq[:, 4, 1, m:m + 1], ACT.Sqrt, bias=rtmp[:, 4, m:m + 1],
                  scale=1.0 / D).then_inc(root_ready, 1)
                if m == 0:
                    A(spare[:, 2:3], spare[:, 1:2], ACT.Sigmoid)

        @block.vector
        def _(dve):
            V = nc.vector
            steps = [0]

            def link(ins):
                steps[0] += 1
                ins.then_inc(dve_step, 1)
                dve.wait_ge(dve_step, steps[0])

            def split(v, slot=None):
                if isinstance(v, int):
                    if v >= UNITS:
                        return
                    slot, nk = v % RING, chunks_of(v)
                else:
                    nk = CH
                dve.wait_ge(hi_ready, v + 1)
                V.tensor_tensor(w_lo[:, slot, :nk * N], raw[:, slot, :nk * N],
                                w_hi[:, slot, :nk * N].bitcast(F32), ALU.subtract).then_inc(lo_ready, 1)

            def resid(s, n, coef):
                B = B_H[s] + n
                last = {1: U_DOWN[0] + 6 * n + 6, 2: U_WOUT + 3 + n, 3: U_DOWN[1] + 6 * n + 6}[s]
                dve.wait_ge(unit_done, last)
                for m in range(M):
                    c = slice(n * N, (n + 1) * N)
                    V.scalar_tensor_tensor(out=h[:, m, c], in0=acc[:, 2 * (B % 2) + m, :], scalar=coef,
                                           in1=h[:, m, c], op0=ALU.mult, op1=ALU.add).then_inc(acc_read, 1)

            def h_turns(s, n):
                for a in range(2):
                    t = TURN[f"h{s}.{n}"] + a
                    for c in range(2):
                        k = 4 * n + 2 * a + c
                        dve.wait_ge(turn_hi, hi_count[f"h{s}.{n}"] + 2 * a + 2)
                        ins = V.scalar_tensor_tensor(
                            out=hT_lo[:, k, :], in0=turn[:, t % 2, c * T:(c + 1) * T],
                            scalar=gains[:, s * KC + k:s * KC + k + 1], in1=hT_hi[:, k, :].bitcast(F32),
                            op0=ALU.mult, op1=ALU.subtract)
                    ins.then_inc(turn_read, 1)

            def rms(s):
                dve.wait_ge(ssq_ready, 4 * s + 4)
                link(V.tensor_tensor(rtmp[:, s, :], ssq[:, s, 0, :], ssq[:, s, 1, :], ALU.add))
                V.tensor_scalar(rtmp[:, s, :], rtmp[:, s, :], 1.0 / D, EPS, ALU.mult, ALU.add).then_inc(ms_ready, 1)
                dve.wait_ge(root_ready, s + 1)
                V.reciprocal(rstd[:, s, :], rtmp[:, s, :]).then_inc(rstd_ready, 1)
                dve.wait_ge(rstd_ready, s + 1)

            def act_turn(f, b, par):
                dve.wait_ge(turn_hi, b + (hi_count[f"act{f}"] + 1))
                r = bass.ds(b * 2, 2)
                V.tensor_tensor(a_loT[:, r, :], turn[:, (TURN[f"act{f}"] + par) % 2, :].rearrange("p (c t) -> p c t", c=2),
                                a_hiT[:, r, :].bitcast(F32), ALU.subtract).then_inc(turn_read, 1)

            def gated(f, b, par):
                for m in range(M):
                    dve.wait_ge(silu_ready, b * 2 + (2 * NB * f + m + 1))
                    V.scalar_tensor_tensor(out=act[:, m, :], in0=acc[:, 2 * ((B_GU[f] + par) % 2) + m, FB:N],
                                           scalar=rstd[:, 2 * f, m:m + 1], in1=silu_g[:, m, :],
                                           op0=ALU.mult, op1=ALU.mult).then_inc(acc_read, 1)

            def ffn(f):
                U = U_GU[f]

                def blk(b, j, i=None):
                    def sp_(k):
                        v = U + 2 * j + k + RING
                        split(v if i is None else i * 4 + v, v % RING)
                    if j == 0:
                        if f == 1:
                            resid(2, 1, 1.0)
                            split(U + 3)
                            h_turns(2, 1)
                            rms(2)
                            sp_(0)
                    else:
                        act_turn(f, b - 1, (j - 1) % 2)
                        sp_(0)
                    gated(f, b, j % 2)
                    if f == 0 and j == 0:
                        sp_(0)
                    sp_(1)

                blk(0, 0)
                with dve.Fori(0, (NB - 1) // 2) as i:
                    for j in range(2):
                        blk(i * 2 + (1 + j), 1 + j, i)
                for n in range(2):
                    for k in range(6):
                        u = U_DOWN[f] + 6 * n + k
                        if n == 0 and k == 0:
                            act_turn(f, NB - 1, (NB - 1) % 2)
                        if f == 0 and n == 0 and k == 2:
                            o = side_of("gain")
                            V.tensor_copy(gains[:, KC:], o[:, 0:3 * KC]).then_inc(side_dve, 1)
                            dve.wait_ge(side_dve, SIDE["gain"][2])
                            o = side_of("bias_row")
                            V.tensor_tensor(bias_row[:], o[0:MH, 0:BIAS_W], causal[:], ALU.add).then_inc(side_dve, 1)
                            dve.wait_ge(consts_hi, 1)
                            V.tensor_tensor(lrw_pad[:, :, 2 * LR:3 * LR], lrw[:], lrw_pad[:, :, 0:LR].bitcast(F32),
                                            ALU.subtract).then_inc(consts_lo, 1)
                        if f == 1 and n == 0 and k == 2:
                            dve.wait_ge(turn_hi, hi_count["p"] + 1)
                            V.tensor_tensor(pT_lo[:].rearrange("p c t -> p (c t)"), turn[:, TURN["p"] % 2, :],
                                            pT_hi[:].rearrange("p c t -> p (c t)").bitcast(F32),
                                            ALU.subtract).then_inc(turn_read, 1)
                        if n == 1 and k == 0:
                            resid(2 * f + 1, 0, 0.5)
                        if n == 1 and k == 1:
                            h_turns(2 * f + 1, 0)
                        if n == 0 or k < 4:
                            split(u + RING)
                resid(2 * f + 1, 1, 0.5)
                split(U_DOWN[f] + 10 + RING)
                if f == 0:
                    h_turns(1, 1)
                    split(U_DOWN[0] + 11 + RING)

            def side_of(name):
                dve.wait_ge(side_done, SIDE[name][0] + 1)
                return side[:, SIDE[name][0] % 2, :]

            def make_z(lv):
                w = 1 << lv
                dve.wait_ge(side_act, SIDE["D7"][2])
                dve.wait_ge(turn_act, turned("T_g1"))
                if lv == 7:
                    lower, upper = E[:, 0, :], E[:, 8, :]
                else:
                    lower = upper = E[:, lv + 1, :]
                dims = [[2 * w, T // w], [1, w]]
                V.tensor_tensor(view(lower, dims), view(lower, dims), view(k_gT[:], dims), ALU.mult)
                V.tensor_tensor(view(upper, dims, w), view(upper, dims, w), view(q_gT[:], dims, w), ALU.mult
                                ).then_inc(Z_ready, 1)

            def step(s):
                if s == "lr":
                    o = side_of(s)
                    V.tensor_copy(lrT[:], o[0:3 * LR, 0:T]).then_inc(side_dve, 1)
                elif s == "z":
                    o = side_of(s)
                    for m in range(M):
                        c = slice(m * T, (m + 1) * T)
                        ins = V.scalar_tensor_tensor(out=log_a[:, c], in0=o[:, c], scalar=rstd[:, 1, m:m + 1],
                                                     in1=b_row[:], op0=ALU.mult, op1=ALU.add)
                        if m == 0:
                            link(ins)
                    ins.then_inc(side_dve, 1)
                    dve.wait_ge(side_dve, SIDE[s][2])
                    dve.wait_ge(z_abs, 1)
                    link(V.tensor_scalar(log_a[:], log_a[:], 0.0, 1.0 / TAU, ALU.min, ALU.mult))
                elif s == "la":
                    dve.wait_ge(lg_ready, 1)
                    V.scalar_tensor_tensor(out=log_a[:], in0=lg[:], scalar=-1.0 / TAU, in1=log_a[:],
                                           op0=ALU.mult, op1=ALU.add).then_inc(la_ready, 1)
                    dve.wait_ge(la_ready, 1)
                    dve.wait_ge(la_hi_ready, 1)
                    V.tensor_tensor(la_lo[:], log_a[:], la_hi[:].bitcast(F32), ALU.subtract).then_inc(la_lo_ready, 1)
                elif s[:2] == "lo":
                    split(int(s[2:]))
                elif s[0] == "Z":
                    for lv in range(2 * int(s[1]), 2 * int(s[1]) + 2):
                        make_z(lv)
                elif s == "clear":
                    dve.wait_ge(turn_done, TURN["T_g1"] + 1)
                    link(V.memset(AT[:], 0.0))
                elif s[:2] == "sc":
                    pair = int(s[2])
                    for i in range(2):
                        head = 2 * pair + i
                        o = side_of(f"{s}.{i}")
                        if head == 0:
                            dve.wait_ge(biasT_in, 16)
                        if pair:
                            dve.wait_ge(turn_done, TURN[f"pt{pair - 1}.{i}"] + 1)
                        V.tensor_tensor_reduce(pr[:, i, 0:P], o[:, 0:P], bias[:, head, P:T], 1.0, -3.0e38,
                                               ALU.add, ALU.max, mx[:, head, 0:1])
                        V.tensor_tensor_reduce(pr[:, i, P:3 * P], o[:, P:3 * P], bias[:, head, :], 1.0, -3.0e38,
                                               ALU.add, ALU.max, mx[:, head, 1:2]).then_inc(side_dve, 1)
                        dve.wait_ge(side_dve, SIDE[f"{s}.{i}"][2])
                        V.tensor_scalar(mx[:, head, :], mx[:, head, :], -1.0, None, ALU.mult).then_inc(neg_max, 1)
                elif s[:2] == "pr":
                    for i in range(2):
                        head = 2 * int(s[2]) + i
                        dve.wait_ge(exp_ready, head + 1)
                        link(V.reciprocal(sums[:, head, :], sums[:, head, :]))
                        V.tensor_scalar(pr[:, i, 0:P], pr[:, i, 0:P], sums[:, head, 0:1], None, ALU.mult)
                        V.tensor_scalar(pr[:, i, P:3 * P], pr[:, i, P:3 * P], sums[:, head, 1:2], None,
                                        ALU.mult).then_inc(probs_ready, 1)
                elif s[:2] == "pt":
                    pair, i, t = int(s[2]), int(s[4]), TURN[s]
                    dve.wait_ge(turn_done, t + 1)
                    if pair:
                        dve.wait_ge(turn_done, TURN[f"pv{pair - 1}"] + 1)
                    V.tensor_copy(prT[:, i, :], turn[:, t % 2, 0:3 * P]).then_inc(turn_read, 1)
                elif s == "pvg":
                    for m in range(M):
                        dve.wait_ge(gss_sq, m + 1)
                        V.tensor_reduce(gss[:, m, :], sq[:].rearrange("p (g e) -> p g e", g=GH), AX, ALU.add
                                        ).then_inc(gms_ready, 1)
                    dve.wait_ge(gms_ready, M)
                    V.tensor_scalar(gss[:], gss[:], 1.0 / GDV, EPS, ALU.mult, ALU.add).then_inc(gms_ready, 1)
                elif s == "gg":
                    dve.wait_ge(acc_read, 2 * B_WOUT)
                    link(V.tensor_tensor(gg[:].rearrange("p m (g e) -> p (m g) e", g=GH),
                                         gg[:].rearrange("p m (g e) -> p (m g) e", g=GH),
                                         view(gout[:], [[0, M * GH], [1, GDV]]), ALU.mult))
                elif s == "o_g":
                    dve.wait_ge(groot, 1)
                    link(V.reciprocal(grs[:], grs[:]))
                    for m in range(M):
                        i = SIDE[f"pvg{m}"][0]
                        for hd in range(GH):
                            c = slice(hd * GDV, (hd + 1) * GDV)
                            ins = V.scalar_tensor_tensor(out=gg[:, m, c], in0=side[:, i % 2, c], scalar=grs[:, m, hd:hd + 1],
                                                         in1=gg[:, m, c], op0=ALU.mult, op1=ALU.mult)
                        ins.then_inc(side_dve, 1)
                elif s[:2] == "pv":
                    pair = int(s[2])
                    dve.wait_ge(turn_hi, hi_count[s] + 1)
                    V.tensor_tensor(oT_lo[:, pair, :], turn[:, TURN[s] % 2, 0:T], oT_hi[:, pair, :].bitcast(F32),
                                    ALU.subtract).then_inc(turn_read, 1)
                elif s == "diag":
                    dve.wait_ge(masks_in, 16)
                    for hh in range(2):
                        o = side_of(f"diag.{hh}")
                        V.copy_predicated(AT[:, 4 * hh:4 * hh + 4, :], view(masks[:, 7 * 64:], [[0, 4], [1, P]]),
                                          o.rearrange("p (b i) -> p b i", b=4)).then_inc(side_dve, 1)
                    dve.wait_ge(side_dve, SIDE["diag.1"][2])
                elif s[:2] == "lv":
                    for hh in [int(s[4])] if s[3:] else range(2):
                        name = f"{s[:3]}.{hh}"
                        o = side_of(name)
                        for a in range(2):
                            lv = 2 * int(s[2]) + a
                            w = 1 << lv
                            n = 64 // w if lv < 7 else 0
                            if lv == 7:
                                ins = V.tensor_copy(AT2[:, 2 * hh:2 * hh + 2, :].rearrange("p g i -> p (g i)"), o[:, T:])
                            else:
                                ins = V.copy_predicated(view(AT[:, 4 * hh, :], [[P, 4], [2 * w, n], [1, w]], w),
                                                        view(masks[:, lv * 64:], [[0, 4], [w, n], [1, w]]),
                                                        view(o[:, a * T:], [[64, 4], [w, n], [1, w]]))
                            if a == 0:
                                link(ins)
                        ins.then_inc(side_dve, 1)
                        dve.wait_ge(side_dve, SIDE[name][2])
                elif s[:3] == "T_o":
                    t, a = TURN[s], int(s[3])
                    dve.wait_ge(turn_hi, hi_count[s] + 1)
                    V.tensor_tensor(hT_lo[:, 4 + 2 * a:6 + 2 * a, :], turn[:, t % 2, :].rearrange("p (c t) -> p c t", c=2),
                                    hT_hi[:, 4 + 2 * a:6 + 2 * a, :].bitcast(F32), ALU.subtract).then_inc(turn_read, 1)

            hi_count, n = {}, 0
            for name in sorted(TURN, key=lambda k: TURN[k]):
                hi_count[name] = n
                if name[0] == "h":
                    n += 4
                elif name[:3] == "act":
                    n += NB
                elif name == "p" or name[:2] == "pv" or name[:3] == "T_o":
                    n += 1

            V.memset(spare[:], 1.0).then_inc(spare_set, 1)
            V.memset(junk[:], 0.0).then_inc(junk_set, 1)
            o = side_of("gain0")
            V.tensor_copy(gains[:, 0:KC], o[:, 0:KC]).then_inc(side_dve, 1)
            dve.wait_ge(side_dve, SIDE["gain0"][2])
            half = CH * N // 2
            for ready, done, c in ((half_hi, half_lo, slice(0, half)), (hi_ready, lo_ready, slice(half, None))):
                dve.wait_ge(ready, 1)
                V.tensor_tensor(w_lo[:, 0, c], raw[:, 0, c], w_hi[:, 0, c].bitcast(F32), ALU.subtract).then_inc(done, 1)
                if done is half_lo:
                    h_turns(0, 0)
            h_turns(0, 1)
            split(1)
            split(2)
            rms(0)
            split(3)
            ffn(0)
            rms(1)
            for s in DVE_STEPS:
                step(s)
            for a in range(2):
                step(f"T_o{a}")
            split(U_WOUT + RING)
            split(U_WOUT + 1 + RING)
            resid(2, 0, 1.0)
            split(U_WOUT + 2 + RING)
            h_turns(2, 0)
            ffn(1)
            for n in range(2):
                B = B_PROJ + n
                dve.wait_ge(unit_done, U_PROJ + n + 1)
                for m in range(M):
                    V.tensor_copy(pp[:, m, n * N:(n + 1) * N], acc[:, 2 * (B % 2) + m, :]).then_inc(acc_read, 1)
                if n == 0:
                    h_turns(3, 1)
                split(U_GATE + n + 1)
            rms(3)
            split(U_GATE + 3)
            dve.wait_ge(acc_read, 2 * B_GATE)
            for n in range(2):
                c = slice(n * N, (n + 1) * N)
                for m in range(M):
                    dve.wait_ge(gate_ready, 2 * n + m + 1)
                    V.tensor_tensor(gate[:, m, :], gate[:, m, :], pp[:, m, c], ALU.mult).then_inc(acc_read, 1)
                    dve.wait_ge(acc_read, 2 * (B_GATE + n) + m + 1)
                    V.tensor_tensor(h[:, m, c], h[:, m, c], gate[:, m, :], ALU.add).then_inc(h_final, 1)
                    dve.wait_ge(h_final, 2 * n + m + 1)
                    link(V.tensor_tensor(res[:, m, c], h[:, m, c], fgain[:, c], ALU.mult))
                    if n == 1:
                        if m == 0:
                            dve.wait_ge(ssq_ready, 18)
                            V.tensor_scalar(rtmp[:, 4, :], ssq[:, 4, 0, :], 1.0 / D, EPS, ALU.mult, ALU.add
                                            ).then_inc(ms_ready, 1)
                        dve.wait_ge(root_ready, 5 + m)
                        link(V.reciprocal(rstd[:, 4, m:m + 1], rtmp[:, 4, m:m + 1]))
                        for c in (slice(0, N), slice(N, D)):
                            V.tensor_scalar(res[:, m, c], res[:, m, c], rstd[:, 4, m:m + 1], None, ALU.mult
                                            ).then_inc(res_ready, 1)


_INS = ["x", "p", "ffn1_norm", "ffn1_w_gu", "ffn1_w_down", "mix_norm", "w_in", "w_gk_up", "b_gk", "gla_out_norm",
        "w_out", "ffn2_norm", "ffn2_w_gu", "ffn2_w_down", "ple_norm", "w_ple_gate", "w_ple_proj", "rel_bias",
        "final_norm"]


def constants():
    import math
    import numpy as np

    t = np.arange(P)
    seg = np.zeros((P, 9, P), np.float32)
    for lv in range(7):
        w = 1 << lv
        mid = t // (2 * w) * 2 * w + w
        upper = (t[:, None] >= mid) & (t[:, None] <= t)
        lower = (t[:, None] > t) & (t[:, None] < mid)
        seg[:, lv + 1] = np.where(t >= mid, upper, lower)
    seg[:, 0] = t[:, None] > t
    seg[:, 8] = t[:, None] <= t
    masks = np.zeros((P, 7 * 64 + P), np.int32)
    q = np.arange(64)
    for lv in range(7):
        w = 1 << lv
        i = q // w * 2 * w + w + q % w
        masks[:, lv * 64:(lv + 1) * 64] = (t[:, None] // (2 * w) == i // (2 * w)) & (t[:, None] % (2 * w) < w)
    masks[:, 7 * 64:] = np.eye(P, dtype=np.int32)
    dist = np.arange(T)
    nf = np.maximum(dist, 1).astype(np.float32)
    exact = BUCKETS // 2
    large = exact + (np.log(nf / np.float32(exact)) / np.float32(math.log(4096 / exact))
                     * np.float32(BUCKETS - exact)).astype(np.int32)
    bucket = np.where(dist < exact, dist, np.minimum(large, BUCKETS - 1))
    rows = np.zeros((BUCKETS, BIAS_W), np.float32)
    rows[bucket, T - 1 - dist] = 1.0
    causal = np.zeros((MH, BIAS_W), np.float32)
    causal[:, T:] = -1e30
    return {"identity": np.eye(P, dtype=np.float32), "seg_sums": seg.reshape(P, 9 * P), "pair_masks": masks,
            "bucket_rows": rows, "causal_row": causal}


def kernel(**inputs):
    import numpy as _np
    import concourse.bacc as _bacc
    from concourse import mybir as _mybir
    from concourse.bass_utils import run_bass_kernel_spmd as _run

    nc = _bacc.Bacc("TRN2", target_bir_lowering=False, num_devices=1)
    arrays, args = {}, []
    given = {name: _np.ascontiguousarray(inputs[name]) for name in _INS} | constants()
    for name, a in given.items():
        arrays[f"in_{name}"] = a
        args.append(nc.dram_tensor(f"in_{name}", a.shape, _mybir.dt.from_np(a.dtype), kind="ExternalInput").ap())
    args.append(nc.dram_tensor("out_0", (1, T, D), _mybir.dt.float32, kind="ExternalOutput").ap())
    build(nc, *args)
    r = _run(nc, [arrays], core_ids=[0])
    return r.results[0]["out_0"]
```
